# Optimizing a Trainium2 kernel written in Bass

```python
import math
import jax, jax.numpy as jnp
from jax import lax
import numpy as np
import jax
import jax.numpy as jnp

D_MODEL = 1024
BATCH = 1
SEQ = 256
DEPTH = 1

CHUNK = 64
CONV_WIDTH = 512
CONV_GROUPS = 8
CONV_TAPS = 3
N_HEADS = 8
HEAD_DIM = 64
ATTN_WIDTH = N_HEADS * HEAD_DIM
D_FF = 4 * D_MODEL
Q_BLOCK = 128
N_MOD = 6
EPS = 1e-6
IN_COLS = 3 * CONV_WIDTH + 3 * ATTN_WIDTH + 2 * D_MODEL


def rms_norm(x, g):
    xf = x.astype(jnp.float32)
    y = xf * lax.rsqrt(jnp.mean(xf * xf, axis=-1, keepdims=True) + EPS)
    return (y * g.astype(jnp.float32)).astype(x.dtype)

def modulate(h, shift, scale):
    return h * (1.0 + scale[:, None, :]) + shift[:, None, :]

def short_conv_branch(b_gate, c_gate, u, conv_w):
    s = u.shape[1]
    v = c_gate * u
    vp = jnp.pad(v, ((0, 0), (CONV_TAPS - 1, 0), (0, 0)))
    y = sum(conv_w[k] * vp[:, k:k + s, :] for k in range(CONV_TAPS))
    return b_gate * y

def stick_breaking_attention(q, k, v):
    b, s, h, dh = q.shape
    qh = jnp.transpose(q, (0, 2, 1, 3))
    kh = jnp.transpose(k, (0, 2, 1, 3))
    vh = jnp.transpose(v, (0, 2, 1, 3))
    inv_sqrt = 1.0 / math.sqrt(dh)
    key_pos = jnp.arange(s)
    n_blocks = s // Q_BLOCK

    def block(i):
        start = i * Q_BLOCK
        q_blk = lax.dynamic_slice_in_dim(qh, start, Q_BLOCK, axis=2)
        z = jnp.einsum('bhqd,bhkd->bhqk', q_blk, kh).astype(jnp.float32) * inv_sqrt
        q_pos = start + jnp.arange(Q_BLOCK)
        mask = key_pos[None, :] < q_pos[:, None]
        log_1m_beta = jnp.where(mask, jax.nn.log_sigmoid(-z), 0.0)
        suffix = lax.cumsum(log_1m_beta, axis=3, reverse=True) - log_1m_beta
        a = jnp.where(mask, jnp.exp(jax.nn.log_sigmoid(z) + suffix), 0.0)
        return jnp.einsum('bhqk,bhkd->bhqd', a, vh.astype(jnp.float32)).astype(q.dtype)

    o = lax.map(block, jnp.arange(n_blocks))
    o = jnp.transpose(o, (1, 0, 3, 2, 4))
    return o.reshape(b, s, h * dh)

def first_inputs(seed: int = 0) -> dict:
    key = jax.random.key(seed)
    ks = jax.random.split(key, 16)
    f32 = jnp.float32
    L, D = DEPTH, D_MODEL

    def nrm(k, shape, fan_in):
        return jax.random.normal(k, shape, f32) * (fan_in ** -0.5)

    def gain(k):
        return 1.0 + 0.05 * jax.random.normal(k, (L, D), f32)

    return {
        "x": jax.random.normal(ks[0], (BATCH, SEQ, D), f32),
        "c": jax.random.normal(ks[1], (BATCH, D), f32),
        "w_ada": nrm(ks[2], (L, D, N_MOD * D), D) * 0.5,
        "b_ada": 0.01 * jax.random.normal(ks[3], (L, N_MOD * D), f32),
        "g_pre_mix": gain(ks[4]),
        "g_post_mix": gain(ks[5]),
        "g_pre_mlp": gain(ks[6]),
        "g_post_mlp": gain(ks[7]),
        "w_in": nrm(ks[8], (L, D, IN_COLS), D),
        "conv_w": nrm(ks[9], (L, CONV_TAPS, CONV_WIDTH), CONV_TAPS),
        "w_proj_conv": nrm(ks[10], (L, CONV_WIDTH, D), CONV_WIDTH),
        "w_proj_attn": nrm(ks[11], (L, ATTN_WIDTH, D), ATTN_WIDTH),
        "w_out": nrm(ks[12], (L, D, D), D),
        "w_mlp_in": nrm(ks[13], (L, D, D_FF), D),
        "w_mlp_out": nrm(ks[14], (L, D_FF, D), D_FF),
    }

def first_block(x, c, w_ada, b_ada, g_pre_mix, g_post_mix, g_pre_mlp, g_post_mlp,
              w_in, conv_w, w_proj_conv, w_proj_attn, w_out, w_mlp_in, w_mlp_out):
    b, s, d = x.shape
    split_pts = np.cumsum([CONV_WIDTH, CONV_WIDTH, CONV_WIDTH,
                           ATTN_WIDTH, ATTN_WIDTH, ATTN_WIDTH, D_MODEL])
    for l in range(DEPTH):
        mod = c @ w_ada[l] + b_ada[l]
        sh1, sc1, gt1, sh2, sc2, gt2 = jnp.split(mod, N_MOD, axis=-1)

        h = modulate(rms_norm(x, g_pre_mix[l]), sh1, sc1)
        proj = h @ w_in[l]
        bg, cg, u, q, k, v, ga, gb = jnp.split(proj, split_pts, axis=-1)
        y_conv = short_conv_branch(bg, cg, u, conv_w[l]) @ w_proj_conv[l]
        o = stick_breaking_attention(q.reshape(b, s, N_HEADS, HEAD_DIM),
                                     k.reshape(b, s, N_HEADS, HEAD_DIM),
                                     v.reshape(b, s, N_HEADS, HEAD_DIM))
        y_attn = o @ w_proj_attn[l]
        merged = jax.nn.sigmoid(ga) * y_conv + jax.nn.sigmoid(gb) * y_attn
        mix_out = merged @ w_out[l]
        x = x + gt1[:, None, :] * rms_norm(mix_out, g_post_mix[l])

        h2 = modulate(rms_norm(x, g_pre_mlp[l]), sh2, sc2)
        ff = jnp.square(jax.nn.relu(h2 @ w_mlp_in[l])) @ w_mlp_out[l]
        x = x + gt2[:, None, :] * rms_norm(ff, g_post_mlp[l])
    return x


CONV_CH = 256
CONV_WIDTH_2 = 31
N_Q_HEADS = 12
N_KV_HEADS = 4
Q_PER_KV = N_Q_HEADS // N_KV_HEADS
NSA_WIDTH = N_Q_HEADS * HEAD_DIM
MIX_WIDTH = CONV_CH + NSA_WIDTH
KV_WIDTH = N_KV_HEADS * HEAD_DIM
CMP_LEN = 32
CMP_STRIDE = 16
CMP_HIDDEN = 256
SEL_BLOCK = 64
SEL_TOPK = 8
WINDOW = 512
Q_BLOCK_2 = 64
N_BRANCH = 3
FORCED_BONUS = 1000.0
D_FF_2 = -(-8 * D_MODEL // (3 * 256)) * 256
IN_COLS_2 = 2 * CONV_CH + NSA_WIDTH + 6 * KV_WIDTH + N_BRANCH * N_Q_HEADS


def rms_norm_2(x, g):
    xf = x.astype(jnp.float32)
    y = xf * lax.rsqrt(jnp.mean(xf * xf, axis=-1, keepdims=True) + EPS)
    return (y * g.astype(jnp.float32)).astype(x.dtype)

def layer_norm(x, g, b):
    xf = x.astype(jnp.float32)
    mu = jnp.mean(xf, axis=-1, keepdims=True)
    var = jnp.mean(jnp.square(xf - mu), axis=-1, keepdims=True)
    y = (xf - mu) * lax.rsqrt(var + EPS)
    return (y * g.astype(jnp.float32) + b.astype(jnp.float32)).astype(x.dtype)

def alibi_slopes(n):
    def pow2_slopes(m):
        start = 2.0 ** (-8.0 / m)
        return [start ** (i + 1) for i in range(m)]
    if math.log2(n).is_integer():
        s = pow2_slopes(n)
    else:
        c = 2 ** math.floor(math.log2(n))
        s = pow2_slopes(c) + pow2_slopes(2 * c)[0::2][: n - c]
    return np.asarray(s, dtype=np.float32)

def masked_softmax(s, mask):
    s = jnp.where(mask, s.astype(jnp.float32), -jnp.inf)
    m = jnp.max(s, axis=-1, keepdims=True)
    m = jnp.where(jnp.isfinite(m), m, 0.0)
    p = jnp.exp(s - m)
    return p / jnp.maximum(jnp.sum(p, axis=-1, keepdims=True), 1e-30)

def conv_mixer(a, w_dw, b_dw, ln_g, ln_b):
    u, v = jnp.split(a, 2, axis=-1)
    y = u * jax.nn.sigmoid(v)
    y = lax.conv_general_dilated(
        y, w_dw[:, None, :], window_strides=(1,),
        padding=[(CONV_WIDTH_2 - 1, 0)],
        dimension_numbers=("NWC", "WIO", "NWC"),
        feature_group_count=CONV_CH) + b_dw
    y = layer_norm(y, ln_g, ln_b)
    return jax.nn.silu(y)

def compress(kr, pe, w1, w2):
    b, t = kr.shape[:2]
    chunks = kr.reshape(b, t // CMP_STRIDE, CMP_STRIDE, N_KV_HEADS, HEAD_DIM)
    lo = jnp.einsum("bclgd,ldh->bcgh", chunks, w1[:CMP_STRIDE])
    hi = jnp.einsum("bclgd,ldh->bcgh", chunks, w1[CMP_STRIDE:])
    h = lo[:, :-1] + hi[:, 1:] + jnp.einsum("ld,ldh->h", pe, w1)
    return jnp.einsum("bngh,hd->bngd", jax.nn.silu(h), w2)

def nsa_attention(q, kc, vc, ks, vs, kw, vw, gates):
    b, t = q.shape[:2]
    n_cmp = kc.shape[1]
    n_sel = t // SEL_BLOCK
    k_top = min(SEL_TOPK, n_sel)
    scale = HEAD_DIM ** -0.5
    slopes = jnp.asarray(alibi_slopes(N_Q_HEADS)).reshape(N_KV_HEADS, Q_PER_KV)[None, :, :, None, None]
    cmp_idx = jnp.arange(n_cmp)
    cmp_start = cmp_idx * CMP_STRIDE
    cmp_center = cmp_start.astype(jnp.float32) + 0.5 * (CMP_LEN - 1)
    cmp_end = cmp_start + CMP_LEN - 1
    sel_start = jnp.arange(n_sel) * SEL_BLOCK
    overlap = ((cmp_start[:, None] < sel_start[None, :] + SEL_BLOCK)
               & (cmp_start[:, None] + CMP_LEN > sel_start[None, :])).astype(jnp.float32)
    ks_blk = ks.reshape(b, n_sel, SEL_BLOCK, N_KV_HEADS, HEAD_DIM).transpose(0, 3, 1, 2, 4)
    vs_blk = vs.reshape(b, n_sel, SEL_BLOCK, N_KV_HEADS, HEAD_DIM).transpose(0, 3, 1, 2, 4)
    pad = ((0, 0), (WINDOW, 0), (0, 0), (0, 0))
    kw_pad = jnp.pad(kw, pad)
    vw_pad = jnp.pad(vw, pad)
    b_idx = jnp.arange(b)[:, None, None, None]
    g_idx = jnp.arange(N_KV_HEADS)[None, :, None, None]
    offs = jnp.arange(SEL_BLOCK)
    win_offs = jnp.arange(WINDOW + Q_BLOCK_2) - WINDOW
    sel_j = jnp.arange(n_sel)

    def block(i):
        t0 = i * Q_BLOCK_2
        tq = t0 + jnp.arange(Q_BLOCK_2)
        tqf = tq.astype(jnp.float32)
        qb = lax.dynamic_slice_in_dim(q, t0, Q_BLOCK_2, axis=1) * scale
        gb = lax.dynamic_slice_in_dim(gates, t0, Q_BLOCK_2, axis=1)

        s_c = jnp.einsum("bqgrd,bngd->bgrqn", qb, kc) - slopes * (tqf[:, None] - cmp_center[None, :])
        p_c = masked_softmax(s_c, cmp_end[None, :] <= tq[:, None])
        o_c = jnp.einsum("bgrqn,bngd->bqgrd", p_c, vc)

        imp = jnp.einsum("bgrqn,nj->bgqj", p_c, overlap)
        cur = tq // SEL_BLOCK
        forced = ((sel_j[None, :] == 0) | (sel_j[None, :] == cur[:, None])
                  | (sel_j[None, :] == cur[:, None] - 1))
        imp = jnp.where(sel_j[None, :] <= cur[:, None],
                        imp + FORCED_BONUS * forced.astype(jnp.float32), -jnp.inf)
        top_s, top_i = lax.top_k(imp, k_top)

        kg = ks_blk[b_idx, g_idx, top_i]
        vg = vs_blk[b_idx, g_idx, top_i]
        pos = top_i[..., None] * SEL_BLOCK + offs
        mask_s = jnp.isfinite(top_s)[..., None] & (pos <= tq[None, None, :, None, None])
        dist_s = (tqf[None, None, :, None, None] - pos.astype(jnp.float32))[:, :, None]
        s_s = jnp.einsum("bqgrd,bgqksd->bgrqks", qb, kg) - slopes[..., None] * dist_s
        s_s = s_s.reshape(b, N_KV_HEADS, Q_PER_KV, Q_BLOCK_2, k_top * SEL_BLOCK)
        p_s = masked_softmax(s_s, mask_s.reshape(b, N_KV_HEADS, 1, Q_BLOCK_2, k_top * SEL_BLOCK))
        o_s = jnp.einsum("bgrqs,bgqsd->bqgrd", p_s,
                         vg.reshape(b, N_KV_HEADS, Q_BLOCK_2, k_top * SEL_BLOCK, HEAD_DIM))

        kwb = lax.dynamic_slice_in_dim(kw_pad, t0, WINDOW + Q_BLOCK_2, axis=1)
        vwb = lax.dynamic_slice_in_dim(vw_pad, t0, WINDOW + Q_BLOCK_2, axis=1)
        pos_w = t0 + win_offs
        dist_w = tq[:, None] - pos_w[None, :]
        mask_w = (dist_w >= 0) & (dist_w < WINDOW) & (pos_w[None, :] >= 0)
        s_w = jnp.einsum("bqgrd,bkgd->bgrqk", qb, kwb) - slopes * dist_w.astype(jnp.float32)
        p_w = masked_softmax(s_w, mask_w)
        o_w = jnp.einsum("bgrqk,bkgd->bqgrd", p_w, vwb)

        out = gb[..., 0:1] * o_c + gb[..., 1:2] * o_s + gb[..., 2:3] * o_w
        return out.astype(q.dtype)

    outs = lax.map(block, jnp.arange(t // Q_BLOCK_2))
    return jnp.moveaxis(outs, 0, 1).reshape(b, t, NSA_WIDTH)

def hybrid_layer(x, attn_norm, w_in, conv_w, conv_b, conv_ln_g, conv_ln_b,
                 cmp_k_pe, cmp_k_w1, cmp_k_w2, cmp_v_pe, cmp_v_w1, cmp_v_w2,
                 w_out, ffn_norm, w_gate_up, w_down):
    b, t, _ = x.shape
    h = rms_norm_2(x, attn_norm)
    z = h @ w_in
    splits = np.cumsum([2 * CONV_CH, NSA_WIDTH] + [KV_WIDTH] * 6).tolist()
    a_conv, q, kc_r, vc_r, ks, vs, kw, vw, g = jnp.split(z, splits, axis=-1)
    kv_shape = (b, t, N_KV_HEADS, HEAD_DIM)
    conv_out = conv_mixer(a_conv, conv_w, conv_b, conv_ln_g, conv_ln_b)
    kc = compress(kc_r.reshape(kv_shape), cmp_k_pe, cmp_k_w1, cmp_k_w2)
    vc = compress(vc_r.reshape(kv_shape), cmp_v_pe, cmp_v_w1, cmp_v_w2)
    gates = jax.nn.sigmoid(g).reshape(b, t, N_KV_HEADS, Q_PER_KV, N_BRANCH)
    nsa_out = nsa_attention(q.reshape(b, t, N_KV_HEADS, Q_PER_KV, HEAD_DIM), kc, vc,
                            ks.reshape(kv_shape), vs.reshape(kv_shape),
                            kw.reshape(kv_shape), vw.reshape(kv_shape), gates)
    mix = jnp.concatenate([conv_out, nsa_out.astype(conv_out.dtype)], axis=-1)
    x = x + mix @ w_out
    h = rms_norm_2(x, ffn_norm)
    gu = h @ w_gate_up
    gate, up = jnp.split(gu, 2, axis=-1)
    return x + (jax.nn.silu(gate) * up) @ w_down

def second_inputs(seed: int = 0) -> dict:
    key = jax.random.key(seed)
    ks = jax.random.split(key, 20)
    f32 = jnp.float32

    def nrm(k, shape, scale):
        return jax.random.normal(k, shape, f32) * scale

    return {
        "x": nrm(ks[0], (BATCH, SEQ, D_MODEL), 1.0),
        "attn_norm": 1.0 + nrm(ks[1], (DEPTH, D_MODEL), 0.05),
        "w_in": nrm(ks[2], (DEPTH, D_MODEL, IN_COLS_2), D_MODEL ** -0.5),
        "conv_w": nrm(ks[3], (DEPTH, CONV_WIDTH_2, CONV_CH), CONV_WIDTH_2 ** -0.5),
        "conv_b": nrm(ks[4], (DEPTH, CONV_CH), 0.01),
        "conv_ln_g": 1.0 + nrm(ks[5], (DEPTH, CONV_CH), 0.05),
        "conv_ln_b": nrm(ks[6], (DEPTH, CONV_CH), 0.01),
        "cmp_k_pe": nrm(ks[7], (DEPTH, CMP_LEN, HEAD_DIM), 0.1),
        "cmp_k_w1": nrm(ks[8], (DEPTH, CMP_LEN, HEAD_DIM, CMP_HIDDEN), (CMP_LEN * HEAD_DIM) ** -0.5),
        "cmp_k_w2": nrm(ks[9], (DEPTH, CMP_HIDDEN, HEAD_DIM), CMP_HIDDEN ** -0.5),
        "cmp_v_pe": nrm(ks[10], (DEPTH, CMP_LEN, HEAD_DIM), 0.1),
        "cmp_v_w1": nrm(ks[11], (DEPTH, CMP_LEN, HEAD_DIM, CMP_HIDDEN), (CMP_LEN * HEAD_DIM) ** -0.5),
        "cmp_v_w2": nrm(ks[12], (DEPTH, CMP_HIDDEN, HEAD_DIM), CMP_HIDDEN ** -0.5),
        "w_out": nrm(ks[13], (DEPTH, MIX_WIDTH, D_MODEL), MIX_WIDTH ** -0.5),
        "ffn_norm": 1.0 + nrm(ks[14], (DEPTH, D_MODEL), 0.05),
        "w_gate_up": nrm(ks[15], (DEPTH, D_MODEL, 2 * D_FF_2), D_MODEL ** -0.5),
        "w_down": nrm(ks[16], (DEPTH, D_FF_2, D_MODEL), D_FF_2 ** -0.5),
        "final_norm": 1.0 + nrm(ks[17], (D_MODEL,), 0.05),
    }

def second_block(x, attn_norm, w_in, conv_w, conv_b, conv_ln_g, conv_ln_b,
              cmp_k_pe, cmp_k_w1, cmp_k_w2, cmp_v_pe, cmp_v_w1, cmp_v_w2,
              w_out, ffn_norm, w_gate_up, w_down, final_norm):
    for l in range(DEPTH):
        x = hybrid_layer(x, attn_norm[l], w_in[l], conv_w[l], conv_b[l], conv_ln_g[l], conv_ln_b[l],
                         cmp_k_pe[l], cmp_k_w1[l], cmp_k_w2[l], cmp_v_pe[l], cmp_v_w1[l], cmp_v_w2[l],
                         w_out[l], ffn_norm[l], w_gate_up[l], w_down[l])
    return rms_norm_2(x, final_norm)


def setup_inputs(seed=0):
    out = dict(first_inputs(seed))
    for name, value in second_inputs(seed + 1).items():
        if name != "x":
            out[name + "_2"] = value
    return out


def reference(
    x, c, w_ada, b_ada, g_pre_mix, g_post_mix, g_pre_mlp, g_post_mlp, w_in, conv_w, w_proj_conv,
    w_proj_attn, w_out, w_mlp_in, w_mlp_out, attn_norm_2, w_in_2, conv_w_2, conv_b_2,
    conv_ln_g_2, conv_ln_b_2, cmp_k_pe_2, cmp_k_w1_2, cmp_k_w2_2, cmp_v_pe_2, cmp_v_w1_2,
    cmp_v_w2_2, w_out_2, ffn_norm_2, w_gate_up_2, w_down_2, final_norm_2,
):
    x = first_block(
        x, c, w_ada, b_ada, g_pre_mix, g_post_mix, g_pre_mlp, g_post_mlp, w_in, conv_w,
        w_proj_conv, w_proj_attn, w_out, w_mlp_in, w_mlp_out,
    )
    return second_block(
        x, attn_norm_2, w_in_2, conv_w_2, conv_b_2, conv_ln_g_2, conv_ln_b_2, cmp_k_pe_2,
        cmp_k_w1_2, cmp_k_w2_2, cmp_v_pe_2, cmp_v_w1_2, cmp_v_w2_2, w_out_2, ffn_norm_2,
        w_gate_up_2, w_down_2, final_norm_2,
    )


_drawn_inputs = setup_inputs


def setup_inputs(seed=0):
    import zlib

    import numpy as np

    out = dict(_drawn_inputs(seed))
    spreads = {}
    factors = {'b_ada': 3.136,
     'conv_b_2': 8.0,
     'conv_ln_g_2': 3.736,
     'conv_ln_b_2': 26.869,
     'cmp_k_pe_2': 48.864,
     'cmp_v_pe_2': 3.433}
    for name, (base, spread) in spreads.items():
        noise = np.random.default_rng([zlib.crc32(name.encode()), seed]).standard_normal(out[name].shape)
        drawn = base * np.exp(spread * noise) if base else spread * noise
        out[name] = jnp.asarray(drawn.astype(out[name].dtype))
    for name, factor in factors.items():
        out[name] = (out[name] * factor).astype(out[name].dtype)
    return out
```

```python
import math

import numpy as np

import concourse.bass as bass
from concourse import mybir

ALU = mybir.AluOpType
ACT = mybir.ActivationFunctionType
AX = mybir.AxisListType
F32 = mybir.dt.float32
F32R = mybir.dt.float32r
I32 = mybir.dt.int32

P = 128
CHUNK_COLS = 256
CHUNK_TILES = 8
N_RAW = 4
N_SPLIT = 3
EPS = 1e-6
MASKED = -1e38
MASK_LIMIT = -1e37


def alibi_slopes(n):
    def pow2(m):
        start = 2.0 ** (-8.0 / m)
        return [start ** (i + 1) for i in range(m)]
    if math.log2(n).is_integer():
        s = pow2(n)
    else:
        c = 2 ** math.floor(math.log2(n))
        s = pow2(c) + pow2(2 * c)[0::2][: n - c]
    return [float(x) for x in np.asarray(s, dtype=np.float32)]


class Queues:

    def __init__(self, semaphores):
        self.sem = semaphores
        self.count = {name: 0 for name in semaphores}
        self.items = {name: [] for name in semaphores}
        self.passed = {name: {} for name in semaphores}

    def put(self, engine, issue, waits=(), signal=True):
        for sem, value in flat(waits):
            if self.passed[engine].get(id(sem), 0) < value:
                self.passed[engine][id(sem)] = value
                self.items[engine].append(lambda e, s=sem, v=value: e.wait_ge(s, v))
        if not signal:
            self.items[engine].append(issue)
            return None
        self.count[engine] += 1
        sem = self.sem[engine]
        self.items[engine].append(lambda e: issue(e).then_inc(sem, 1))
        return (sem, self.count[engine])

    def load(self, engine, out, in_, sem, total, waits=()):
        self.put(engine, lambda e: e.dma_start(out, in_).then_inc(sem, 16), waits, signal=False)
        return (sem, total)

    def matmul(self, out, stationary, moving, start, stop, waits=(), signal=False):
        return self.put("pe", lambda e: e.matmul(out, stationary, moving, start=start, stop=stop,
                                                 skip_group_check=True), waits, signal)

    def transpose(self, out, in_, identity, waits=(), signal=False):
        return self.put("pe", lambda e: e.transpose(out, in_, identity), waits, signal)

    def act(self, out, in_, func, waits=(), scale=1.0, bias=None, accum=None):
        if bias is None:
            if accum is None:
                return self.put("act", lambda e: e.activation(out, in_, func, scale=scale), waits)
            return self.put("act", lambda e: e.activation(out, in_, func, scale=scale,
                                                          accum_out=accum), waits)
        if accum is None:
            return self.put("act", lambda e: e.activation(out, in_, func, scale=scale, bias=bias), waits)
        return self.put("act", lambda e: e.activation(out, in_, func, scale=scale, bias=bias,
                                                      accum_out=accum), waits)

    def tt(self, out, a, b, op, waits=(), engine="dve"):
        return self.put(engine, lambda e: e.tensor_tensor(out, a, b, op), waits)

    def ts(self, out, a, s1, op1, s2=None, op2=None, waits=(), engine="dve"):
        if op2 is None:
            return self.put(engine, lambda e: e.tensor_scalar(out, a, s1, None, op1), waits)
        return self.put(engine, lambda e: e.tensor_scalar(out, a, s1, s2, op1, op2), waits)

    def stt(self, out, a, s, b, op1, op2, waits=()):
        return self.put("dve", lambda e: e.scalar_tensor_tensor(out=out, in0=a, scalar=s, in1=b,
                                                                op0=op1, op1=op2), waits)

    def copy(self, out, in_, waits=(), engine="dve"):
        return self.put(engine, lambda e: e.tensor_copy(out, in_), waits)

    def recip(self, out, in_, waits=()):
        return self.put("dve", lambda e: e.reciprocal(out, in_), waits)

    def reduce(self, out, in_, op, waits=(), negate=False):
        return self.put("dve", lambda e: e.tensor_reduce(out, in_, AX.X, op, negate=negate), waits)

    def scan(self, out, a, b, initial, op1, op2, waits=()):
        return self.put("dve", lambda e: e.tensor_tensor_scan(out, a, b, initial, op1, op2), waits)

    def memset(self, out, value, waits=(), engine="dve"):
        return self.put(engine, lambda e: e.memset(out, value), waits)


def flat(waits):
    if waits is None:
        return []
    if isinstance(waits, tuple) and len(waits) == 2 and isinstance(waits[1], int):
        return [waits]
    return [t for w in waits for t in flat(w)]


class Split:

    def __init__(self, hi, lo, tiles):
        self.hi, self.lo = hi, lo
        self.ready = [None] * tiles


class WeightStream:

    def __init__(self, q, raw, raw_sem, hi, lo):
        self.q, self.raw, self.raw_sem, self.hi, self.lo = q, raw, raw_sem, hi, lo
        self.plan = []
        self.loaded = self.split = self.used = 0
        self.n_split = 0
        self.landed, self.raw_free, self.parts, self.split_free = [], [], [], []

    def add(self, source, split=True):
        rows, cols = source.shape
        assert rows % P == 0 and rows // P * cols <= CHUNK_TILES * CHUNK_COLS
        self.plan.append((source, split))

    def raw_view(self, n):
        source, _ = self.plan[n]
        kt, cols = source.shape[0] // P, source.shape[1]
        return self.raw[n % N_RAW][:, 0:kt * cols].rearrange("p (k c) -> p k c", k=kt)

    def ahead(self):
        while True:
            n = self.loaded
            if n < len(self.plan) and (n < N_RAW or self.raw_free[n - N_RAW] is not None):
                waits = self.raw_free[n - N_RAW] if n >= N_RAW else None
                source = self.plan[n][0].rearrange("(k p) c -> p k c", p=P)
                self.landed.append(self.q.load("sp", self.raw_view(n), source, self.raw_sem[n % N_RAW],
                                               16 * (n // N_RAW + 1), waits))
                self.raw_free.append(None)
                self.loaded += 1
                continue
            n = self.split
            if n < min(self.loaded, self.used + N_SPLIT) and n < len(self.plan):
                source, split = self.plan[n]
                if split:
                    slot = self.n_split % N_SPLIT
                    free = self.split_free[self.n_split - N_SPLIT] if self.n_split >= N_SPLIT else None
                    if self.n_split >= N_SPLIT and free is None:
                        return
                    kt, cols = source.shape[0] // P, source.shape[1]
                    hi = self.hi[slot][:, 0:kt * cols]
                    lo = self.lo[slot][:, 0:kt * cols]
                    raw = self.raw[n % N_RAW][:, 0:kt * cols]
                    t_hi = self.q.act(hi, raw, ACT.Copy, [self.landed[n], free])
                    t_lo = self.q.tt(lo, raw, hi.bitcast(F32), ALU.subtract, [t_hi, self.landed[n], free])
                    self.raw_free[n] = t_lo
                    shape = "p (k c) -> p k c"
                    self.parts.append((hi.rearrange(shape, k=kt), lo.rearrange(shape, k=kt),
                                       t_hi, t_lo, self.n_split))
                    self.n_split += 1
                    self.split_free.append(None)
                else:
                    self.parts.append(None)
                self.split += 1
                continue
            return

    def next(self):
        self.ahead()
        self.used += 1
        return self.used - 1

    def done(self, n, ticket):
        if self.parts[n] is None:
            self.raw_free[n] = ticket
        else:
            self.split_free[self.parts[n][4]] = ticket


def build(nc, a, out):
    T, D = a["x"].shape[1], a["x"].shape[2]
    TT = T // P
    DT = D // P
    assert TT == 2
    CONV = a["conv_w"].shape[2]
    CT = CONV // P
    HD = 64
    ATTN = a["w_proj_attn"].shape[1]
    HEADS = ATTN // HD
    FF = a["w_mlp_in"].shape[2]
    CH2 = a["conv_b_2"].shape[1]
    TAPS2 = a["conv_w_2"].shape[1]
    KV = 4
    KVW = KV * HD
    QH = (a["w_out_2"].shape[1] - CH2) // HD
    PER_KV = QH // KV
    FF2 = a["w_down_2"].shape[1]
    CMP_LEN, CMP_HID = a["cmp_k_w1_2"].shape[1], a["cmp_k_w1_2"].shape[3]
    STRIDE = CMP_LEN // 2
    N_CHUNKS = T // STRIDE
    N_CMP = N_CHUNKS - 1
    assert T // 64 <= 8 and T <= 512
    INV_SQRT = HD ** -0.5
    slopes = alibi_slopes(QH)

    from contextlib import ExitStack
    fixed = ExitStack()
    with fixed:
        def sem(name):
            return fixed.enter_context(nc.semaphore(name))

        def alloc(stack, name, shape, dt=F32):
            return stack.enter_context(nc.sbuf_tensor(name, shape, dt))

        q = Queues({name: sem("done_" + name) for name in ("sp", "pe", "act", "dve", "pool")})
        bank = [fixed.enter_context(nc.psum_tensor(f"bank{i}", [P, 512], F32)) for i in range(8)]
        bank_readers = [None] * 8
        SUMS = 3

        raw = [alloc(fixed, f"raw{i}", [P, CHUNK_TILES * CHUNK_COLS]) for i in range(N_RAW)]
        w_hi = [alloc(fixed, f"w_hi{i}", [P, CHUNK_TILES * CHUNK_COLS], F32R) for i in range(N_SPLIT)]
        w_lo = [alloc(fixed, f"w_lo{i}", [P, CHUNK_TILES * CHUNK_COLS], F32R) for i in range(N_SPLIT)]
        stream = WeightStream(q, raw, [sem(f"raw_landed{i}") for i in range(N_RAW)], w_hi, w_lo)
        x_T = alloc(fixed, "x_T", [P, DT, T])
        act_hi = alloc(fixed, "act_hi", [P, DT, T], F32R)
        act_lo = alloc(fixed, "act_lo", [P, DT, T], F32R)
        wide = [alloc(fixed, f"wide{i}", [P, DT, T]) for i in range(3)]
        rms = alloc(fixed, "rms", [P, T])
        rstd = alloc(fixed, "rstd", [P, T])
        ident = alloc(fixed, "ident", [P, P])
        ones = alloc(fixed, "ones", [P, P])
        eps = alloc(fixed, "eps", [P, 1])
        scan_mask = alloc(fixed, "scan_mask", [P, 3 * P])
        mask_T = alloc(fixed, "mask_T", [P, 3 * P])

        rows = {0: [], 1: []}
        row_at = {}

        def place(part, name, source):
            at = sum(s.shape[0] for _, s in rows[part])
            rows[part].append((at, source))
            row_at[name] = (part, at)

        place(0, "b_ada", a["b_ada"].rearrange("o (r p) -> (o r) p", p=P))
        for name in ("g_pre_mix", "g_post_mix", "g_pre_mlp", "g_post_mlp", "attn_norm_2", "ffn_norm_2"):
            place(0, name, a[name].rearrange("o (r p) -> (o r) p", p=P))
        place(0, "final_norm", a["final_norm_2"].rearrange("(r p) -> r p", p=P))
        place(0, "c", a["c"].rearrange("o (r p) -> (o r) p", p=P))
        place(0, "conv_w", a["conv_w"].rearrange("o k (r p) -> (o k r) p", p=P))
        place(1, "conv_w_2", a["conv_w_2"].rearrange("o k (r p) -> (o k r) p", p=P))
        for name in ("conv_b_2", "conv_ln_g_2", "conv_ln_b_2"):
            place(1, name, a[name].rearrange("o (r p) -> (o r) p", p=P))
        for name in ("cmp_k_pe_2", "cmp_v_pe_2"):
            place(1, name, a[name].rearrange("o (l two) d -> (o l) (two d)", two=2))
        row_tile = [alloc(fixed, f"row_tile{i}", [P, P]) for i in range(2)]
        col_tile = [alloc(fixed, f"col_tile{i}", [P, P]) for i in range(2)]

        def cols(name, first, n):
            part, at = row_at[name]
            return col_tile[part][:, at + first:at + first + n]

        mod = alloc(fixed, "mod", [P, 6 * DT])
        scale1 = alloc(fixed, "scale1", [P, DT])
        scale2 = alloc(fixed, "scale2", [P, DT])
        gain1 = alloc(fixed, "gain1", [P, DT])
        gain2 = alloc(fixed, "gain2", [P, DT])
        w2k = alloc(fixed, "w2k", [P, 2, HD])
        w2v = alloc(fixed, "w2v", [P, 2, HD])

        def w(name):
            return a[name][0]

        def columns(name, first, n_cols):
            m = w(name)
            for c in range(first, first + n_cols, CHUNK_COLS):
                for r in range(0, m.shape[0], CHUNK_TILES * P):
                    yield m[r:min(r + CHUNK_TILES * P, m.shape[0]), c:min(c + CHUNK_COLS, first + n_cols)]

        in1 = {}
        at = 0
        for name, width in (("b", CONV), ("c", CONV), ("u", CONV), ("q", ATTN), ("k", ATTN), ("v", ATTN),
                            ("ga", D), ("gb", D)):
            in1[name] = (at, width)
            at += width
        in1_order = ("q", "k", "v", "c", "u", "b", "ga", "gb")
        ada = list(columns("w_ada", 0, 6 * D))
        n_ada_first = 2 * D // CHUNK_COLS
        for s in ada[:n_ada_first]:
            stream.add(s, split=False)
        ada_later = ada[n_ada_first:]
        in1_chunks = [(name, i, s) for name in in1_order for i, s in enumerate(columns("w_in", *in1[name]))]
        assert len(ada_later) <= len(in1_chunks)
        for n, (_, _, s) in enumerate(in1_chunks):
            stream.add(s)
            if n < len(ada_later):
                stream.add(ada_later[n], split=False)
        for name in ("w_proj_conv", "w_proj_attn", "w_out", "w_mlp_in", "w_mlp_out"):
            for s in columns(name, 0, w(name).shape[1]):
                stream.add(s)
        in2 = {}
        at = 0
        for name, width in (("cu", CH2), ("cv", CH2), ("q", QH * HD), ("kc", KVW), ("vc", KVW), ("ks", KVW),
                            ("vs", KVW), ("kw", KVW), ("vw", KVW), ("g", 3 * QH)):
            in2[name] = (at, width)
            at += width
        in2_order = ("cu", "cv", "kc", "vc", "q", "g", "ks", "kw", "vs", "vw")
        in2_chunks = []
        for name in in2_order:
            for i, s in enumerate(columns("w_in_2", *in2[name])):
                in2_chunks.append((name, i))
                stream.add(s)
            if name == "vc":
                for cmp_name in ("cmp_k_w1_2", "cmp_v_w1_2"):
                    flat_w1 = w(cmp_name).rearrange("l d h -> (l d) h")
                    for half in range(2):
                        in2_chunks.append((cmp_name, half))
                        stream.add(flat_w1[half * CHUNK_TILES * P:(half + 1) * CHUNK_TILES * P, :], split=False)
        for s in columns("w_out_2", 0, D):
            stream.add(s)
        for c in range(0, FF2, CHUNK_COLS):
            for base in (0, FF2):
                for s in columns("w_gate_up_2", base + c, CHUNK_COLS):
                    stream.add(s)
        for s in columns("w_down_2", 0, D):
            stream.add(s)

        rows_sem, x_sem, w2_sem, out_sem = sem("rows_landed"), sem("x_landed"), sem("w2_landed"), sem("stored")
        x_nat = wide[0]
        x_nat_v = x_nat[:].rearrange("p k t -> p (k t)").rearrange("p (t d) -> p t d", t=TT)
        n_rows = sum(len(r) for r in rows.values())
        x_landed = q.load("act", x_nat_v, a["x"][0].rearrange("(t p) d -> p t d", p=P), x_sem, 16)
        for part in (0, 1):
            for at, source in rows[part]:
                rows_landed = q.load("act", row_tile[part][at:at + source.shape[0], :], source,
                                     rows_sem, 16 * n_rows)
        for dst, name in ((w2k, "cmp_k_w2_2"), (w2v, "cmp_v_w2_2")):
            w2_landed = q.load("act", dst[:], w(name).rearrange("(m p) d -> p m d", p=P), w2_sem, 32)

        t = q.memset(ident[:], 0.0, engine="pool")
        ident_ready = q.put("pool", lambda e: e.affine_select(
            out=ident[:], in_=ident[:], compare_op=ALU.not_equal, fill=1.0, base=0,
            pattern=[[-1, P]], channel_multiplier=1), t)
        ones_ready = q.memset(ones[:], 1.0)
        eps_ready = q.memset(eps[:], EPS)

        t = q.memset(scan_mask[:], 0.0, engine="pool")
        q.put("pool", lambda e: e.affine_select(
            out=scan_mask[:, 0:P], in_=scan_mask[:, 0:P], compare_op=ALU.is_gt, fill=1.0, base=0,
            pattern=[[-1, P]], channel_multiplier=1), t)
        scan_mask_ready = q.put("pool", lambda e: e.affine_select(
            out=scan_mask[:, P:], in_=scan_mask[:, P:], compare_op=ALU.is_gt, fill=1.0, base=P,
            pattern=[[-1, 2 * P]], channel_multiplier=1), t)
        t = q.memset(mask_T[:], 1.0, engine="pool")
        for b in (0, 2):
            mask_T_ready = q.put("pool", lambda e, m=mask_T[:, b * P:(b + 1) * P]: e.affine_select(
                out=m, in_=m, compare_op=ALU.is_gt, fill=0.0, base=0,
                pattern=[[1, P]], channel_multiplier=-1), t)

        main_ring = [0, 1, 2]
        ring_pos = [0]

        def next_bank():
            ring_pos[0] += 1
            return main_ring[ring_pos[0] % len(main_ring)]

        def product(b, act, k0=0, start=True, stop=True, tokens_first=False):
            n = stream.next()
            hi, lo, t_hi, t_lo, _ = stream.parts[n]
            kt, n_cols = hi.shape[1], hi.shape[2]
            first = start
            for m in range(TT if tokens_first else n_cols // P):
                for k in range(kt):
                    for wp, ap, t_w in ((hi, act.hi, t_hi), (hi, act.lo, t_hi), (lo, act.hi, t_lo)):
                        if tokens_first:
                            dst = bank[b][:, m * n_cols:(m + 1) * n_cols]
                            lhs, rhs = ap[:, k0 + k, m * P:(m + 1) * P], wp[:, k, :]
                        else:
                            dst = bank[b][:, m * T:(m + 1) * T]
                            lhs, rhs = wp[:, k, m * P:(m + 1) * P], ap[:, k0 + k, :]
                        ticket = q.matmul(dst, lhs, rhs, first, stop and k == kt - 1 and wp is lo,
                                          [t_w, act.ready[k0 + k], bank_readers[b] if first else None],
                                          signal=(k == kt - 1 and wp is lo))
                        first = False
            stream.done(n, ticket)
            return ticket

        def modulation(n):
            c = stream.next()
            src = stream.raw_view(c)
            b = next_bank()
            for m in range(2):
                for k in range(DT):
                    t = q.matmul(bank[b][:, m:m + 1], src[:, k, m * P:(m + 1) * P], cols("c", k, 1),
                                 k == 0, k == DT - 1,
                                 [stream.landed[c], cols_ready, bank_readers[b]], signal=(k == DT - 1))
            stream.done(c, t)
            bank_readers[b] = q.tt(mod[:, 2 * n:2 * n + 2], bank[b][:, 0:2], cols("b_ada", 2 * n, 2),
                                   ALU.add, [t, cols_ready])
            return bank_readers[b]

        def split_tiles(act, k, n, source, ready, free=None):
            t_hi = q.act(act.hi[:, k:k + n, :], source, ACT.Copy, [ready, free])
            t_lo = q.tt(act.lo[:, k:k + n, :], source, act.hi[:, k:k + n, :].bitcast(F32),
                        ALU.subtract, [t_hi, ready, free])
            for i in range(k, k + n):
                act.ready[i] = [t_hi, t_lo]
            return [t_hi, t_lo]

        squares = wide[2]

        def norm_begin(k, source, ready, free=None, last=DT - 1):
            t = q.act(squares[:, k, :], source, ACT.Square, [ready, free])
            t = q.matmul(bank[SUMS][:, 0:T], ones[:], squares[:, k, :], k == 0, k == last,
                         [t, ones_ready, bank_readers[SUMS] if k == 0 else None], signal=True)
            return t

        def norm_end(sums, width, free=None):
            t = q.act(rms[:], bank[SUMS][:, 0:T], ACT.Sqrt, [sums, eps_ready, free],
                      scale=1.0 / width, bias=eps[:, 0:1])
            bank_readers[SUMS] = t
            return q.recip(rstd[:], rms[:], [t, free])

        def preload(func):
            return q.act(scratch1[:], eps[:], func, eps_ready)

        scratch1 = alloc(fixed, "scratch1", [P, 1])
        act = Split(act_hi, act_lo, DT)
        act_free = [None]

        def modulated(scale, shift, rstd_ready, x_ready, more):
            y = wide[1]
            for k in range(0, DT, 2):
                ts_ = []
                for i in (k, k + 1):
                    t = q.stt(y[:, i, :], x_T[:, i, :], scale[:, i:i + 1], rstd[:], ALU.mult, ALU.mult,
                              [rstd_ready, x_ready[i], more])
                    if shift is not None:
                        t = q.act(y[:, i, :], y[:, i, :], ACT.Identity, [t, more], bias=shift[:, i:i + 1])
                    ts_.append(t)
                split_tiles(act, k, 2, y[:, k:k + 2, :], ts_, act_free[0])

        stream.ahead()
        t = None
        for part in (0, 1):
            n = sum(s.shape[0] for _, s in rows[part])
            t = q.transpose(bank[part][:, 0:n], row_tile[part][0:n, :], ident[0:n, 0:n],
                            [rows_landed, ident_ready], signal=True)
            cols_ready = q.copy(col_tile[part][:, 0:n], bank[part][:, 0:n], t)
            bank_readers[part] = cols_ready

        x_ready = [None] * DT
        sums = None
        for k in range(0, DT, 2):
            b = next_bank()
            for j in range(2):
                for tt_ in range(TT):
                    t = q.transpose(bank[b][:, j * T + tt_ * P:j * T + (tt_ + 1) * P],
                                    x_nat_v[:, tt_, (k + j) * P:(k + j + 1) * P], ident[:],
                                    [x_landed, ident_ready, bank_readers[b]], signal=(j + tt_ == 2))
            t = q.copy(x_T[:, k:k + 2, :], bank[b][:].rearrange("p (k t) -> p k t", k=2), t)
            bank_readers[b] = t
            for i in (k, k + 1):
                x_ready[i] = t
                sums = norm_begin(i, x_T[:, i, :], t)
        rstd_ready = norm_end(sums, D)

        for n in range(n_ada_first):
            mod_ready = modulation(n)
        t = q.ts(scale1[:], mod[:, DT:2 * DT], 1.0, ALU.add, waits=mod_ready)
        t = q.tt(scale1[:], scale1[:], cols("g_pre_mix", 0, DT), ALU.mult, t)
        modulated(scale1, mod[:, 0:DT], rstd_ready, x_ready, t)
        preload(ACT.Sigmoid)

        with ExitStack() as phase:
            qk_T = [alloc(phase, f"{n}_T", [P, HEADS // 2, T]) for n in "qk"]
            v_nat = alloc(phase, "v_nat", [P, TT, ATTN])
            c_gate = alloc(phase, "c_gate", [P, CT, T])
            b_gate = alloc(phase, "b_gate", [P, CT, T])
            padded = alloc(phase, "padded", [P, CT, T + 2])
            conv_y = alloc(phase, "conv_y", [P, CT, T])
            mixed = Split(alloc(phase, "mixed_hi", [P, CT, T], F32R), alloc(phase, "mixed_lo", [P, CT, T], F32R), CT)
            heads_o = Split(alloc(phase, "heads_hi", [P, HEADS // 2, T], F32R),
                            alloc(phase, "heads_lo", [P, HEADS // 2, T], F32R), HEADS // 2)
            beta = [alloc(phase, f"beta{i}", [P, 3 * P]) for i in range(2)]
            nbeta = [alloc(phase, f"nbeta{i}", [P, 3 * P]) for i in range(2)]
            remain = [alloc(phase, f"remain{i}", [P, 3 * P + 2]) for i in range(2)]
            weight = [alloc(phase, f"weight{i}", [P, 3 * P]) for i in range(2)]
            weight_T = [alloc(phase, f"weight_T{i}", [P, 3 * P]) for i in range(2)]
            gates = [wide[0], wide[1]]

            ends_ready = []
            for r in remain:
                ends_ready.append(q.memset(r[:, P:P + 1], 1.0))
                ends_ready.append(q.memset(r[:, 3 * P + 1:3 * P + 2], 1.0))
            pad_ready = q.memset(padded[:, :, 0:2], 0.0)

            S_BANKS, T_BANK, O_BANK = (4, 5), 6, 7
            head = {}

            def stick_scores(h):
                b, base, tile = S_BANKS[h % 2], h % 2 * HD, h // 2
                qh, kh = (m[base:base + HD, tile, :] for m in qk_T)
                q.matmul(bank[b][:, 0:P], qh[:, 0:P], kh[:, 0:P], True, True, [qk_ready, bank_readers[b]])
                t = q.matmul(bank[b][:, P:3 * P], qh[:, P:T], kh, True, True, signal=True)
                free = head.get(h - 2)
                t1 = q.act(beta[h % 2][:], bank[b][:, 0:3 * P], ACT.Sigmoid, [t, free], scale=INV_SQRT)
                t2 = q.act(nbeta[h % 2][:], bank[b][:, 0:3 * P], ACT.Sigmoid, [t, free], scale=-INV_SQRT)
                bank_readers[b] = t2
                r, nb = remain[h % 2], nbeta[h % 2]
                ts_ = []
                for lo_, hi_, off in ((0, P, 0), (P, 3 * P, 1)):
                    ts_.append(q.scan(r[:, lo_ + off:hi_ + off][:, ::-1], nb[:, lo_:hi_][:, ::-1],
                                      scan_mask[:, lo_:hi_][:, ::-1], 1.0, ALU.mult, ALU.max,
                                      [t2, scan_mask_ready, ends_ready, free]))
                for lo_, hi_, off in ((0, P, 1), (P, 3 * P, 2)):
                    t = q.tt(weight[h % 2][:, lo_:hi_], beta[h % 2][:, lo_:hi_],
                             r[:, lo_ + off:hi_ + off], ALU.mult, [ts_, t1, free], engine="pool")
                return t

            def stick_transpose(h, weight_ready):
                blocks = [weight[h % 2][:, i * P:(i + 1) * P] for i in range(3)]
                for i in range(3):
                    t = q.transpose(bank[T_BANK][:, i * P:(i + 1) * P], blocks[i], ident[:],
                                    [weight_ready, bank_readers[T_BANK]], signal=(i == 2))
                head[h] = t
                t = q.tt(weight_T[h % 2][:], bank[T_BANK][:, 0:3 * P], mask_T[:], ALU.mult,
                         [t, mask_T_ready, head.get(("o", h - 2))])
                bank_readers[T_BANK] = t
                return t

            def stick_output(h, ready):
                base = h % 2 * HD
                o = bank[O_BANK][base:base + HD, :]
                q.matmul(o[:, 0:T], v_nat[:, 0, h * HD:(h + 1) * HD], weight_T[h % 2][:, 0:T], True, False,
                         [ready, v_ready, bank_readers[O_BANK]])
                t = q.matmul(o[:, P:T], v_nat[:, 1, h * HD:(h + 1) * HD], weight_T[h % 2][:, 2 * P:3 * P],
                             False, True, signal=True)
                head[("o", h)] = t
                if h % 2:
                    bank_readers[O_BANK] = split_tiles(heads_o, h // 2, 1, bank[O_BANK][:, 0:T].rearrange(
                        "p (k t) -> p k t", k=1), t)

            def short_conv():
                for j in range(CT):
                    t = q.ts(conv_y[:, j, :], padded[:, j, 0:T], cols("conv_w", j, 1), ALU.mult,
                             waits=[u_ready, pad_ready])
                    for k in (1, 2):
                        t = q.stt(conv_y[:, j, :], padded[:, j, k:k + T], cols("conv_w", k * CT + j, 1),
                                  conv_y[:, j, :], ALU.mult, ALU.add, t)
                    t = q.tt(conv_y[:, j, :], conv_y[:, j, :], b_gate[:, j, :], ALU.mult, [t, b_ready])
                    if j % 2:
                        split_tiles(mixed, j - 1, 2, conv_y[:, j - 1:j + 1, :], t)

            weights_of, attending, step = {}, False, 0
            b_ready = c_ready = u_ready = qk_ready = v_ready = None
            stick_T = {}
            for n, (name, i, _) in enumerate(in1_chunks):
                if attending and step < HEADS + 2:
                    if step < HEADS:
                        weights_of[step] = stick_scores(step)
                    if 1 <= step <= HEADS:
                        stick_T[step - 1] = stick_transpose(step - 1, weights_of[step - 1])
                    if step >= 2:
                        stick_output(step - 2, stick_T[step - 2])
                    step += 1
                b = next_bank()
                t = product(b, act, tokens_first=(name == "v"))
                act_free[0] = t
                src = bank[b][:].rearrange("p (k t) -> p k t", k=2)
                s2 = slice(2 * i, 2 * i + 2)
                if name in "qk":
                    t = q.copy(qk_T["qk".index(name)][:, s2, :], src, t)
                    qk_ready = t
                elif name == "v":
                    t = q.copy(v_nat[:, :, i * CHUNK_COLS:(i + 1) * CHUNK_COLS], src, t)
                    v_ready = t
                    attending = i == 1
                elif name == "c":
                    t = c_ready = q.act(c_gate[:, s2, :], src, ACT.Copy, t)
                elif name == "u":
                    t = u_ready = q.tt(padded[:, s2, 2:], src, c_gate[:, s2, :], ALU.mult, [t, c_ready])
                elif name == "b":
                    t = b_ready = q.act(b_gate[:, s2, :], src, ACT.Copy, t)
                else:
                    t = gates_ready = q.act(gates["ga gb".split().index(name)][:, s2, :], src, ACT.Sigmoid,
                                            [t, act.ready[DT - 1]])
                bank_readers[b] = t
                if n < len(ada_later):
                    mod_ready = modulation(n_ada_first + n)
                if name == "ga" and i == 0:
                    short_conv()
            assert step == HEADS + 2
            preload(ACT.Sqrt)
            t = q.ts(scale2[:], mod[:, 4 * DT:5 * DT], 1.0, ALU.add, waits=mod_ready)
            q.tt(scale2[:], scale2[:], cols("g_pre_mlp", 0, DT), ALU.mult, t)
            q.tt(gain1[:], mod[:, 2 * DT:3 * DT], cols("g_post_mix", 0, DT), ALU.mult, mod_ready)
            mod_ready = q.tt(gain2[:], mod[:, 5 * DT:6 * DT], cols("g_post_mlp", 0, DT), ALU.mult, mod_ready)

            conv_part = wide[2]
            for i in range(DT // 2):
                b = next_bank()
                t = product(b, mixed)
                s2 = slice(2 * i, 2 * i + 2)
                conv_part_ready = bank_readers[b] = q.tt(
                    conv_part[:, s2, :], bank[b][:].rearrange("p (k t) -> p k t", k=2), gates[0][:, s2, :],
                    ALU.mult, [t, gates_ready])
            for i in range(DT // 2):
                b = next_bank()
                t = product(b, heads_o)
                s2 = slice(2 * i, 2 * i + 2)
                t = bank_readers[b] = q.tt(gates[1][:, s2, :], bank[b][:].rearrange("p (k t) -> p k t", k=2),
                                           gates[1][:, s2, :], ALU.mult, [t, gates_ready])
                t = q.tt(gates[1][:, s2, :], gates[1][:, s2, :], conv_part[:, s2, :], ALU.add,
                         [t, conv_part_ready])
                merged_ready = split_tiles(act, 2 * i, 2, gates[1][:, s2, :], t, act_free[0])

        def residual_norm(source, gain, rstd_ready):
            ready, sums = [], None
            for k in range(DT):
                t = q.stt(source[:, k, :], source[:, k, :], gain[:, k:k + 1], rstd[:], ALU.mult, ALU.mult,
                          [rstd_ready, mod_ready])
                t = q.tt(x_T[:, k, :], x_T[:, k, :], source[:, k, :], ALU.add, t)
                ready.append(t)
                sums = norm_begin(k, x_T[:, k, :], t, rstd_ready)
            return ready, sums, t

        branch = wide[0]
        for i in range(DT // 2):
            b = next_bank()
            t = act_free[0] = product(b, act)
            s2 = slice(2 * i, 2 * i + 2)
            t = bank_readers[b] = q.copy(branch[:, s2, :], bank[b][:].rearrange("p (k t) -> p k t", k=2), t)
            for k in (2 * i, 2 * i + 1):
                sums = norm_begin(k, branch[:, k, :], t, merged_ready)
        rstd_ready = norm_end(sums, D)
        x_ready, sums, t = residual_norm(branch, gain1, rstd_ready)
        rstd_ready = norm_end(sums, D, t)
        modulated(scale2, mod[:, 3 * DT:4 * DT], rstd_ready, x_ready, mod_ready)

        def accumulate_tiles(source, n_tiles, evacuate):
            for i in range(DT // 2):
                b = next_bank()
                for r in range(0, n_tiles, CHUNK_TILES):
                    t = product(b, source, k0=r, start=(r == 0), stop=(r + CHUNK_TILES >= n_tiles))
                bank_readers[b] = evacuate(i, bank[b][:].rearrange("p (k t) -> p k t", k=2), t)
            return t

        with ExitStack() as phase:
            FT = FF // P
            hidden = Split(alloc(phase, "hidden_hi", [P, FT, T], F32R), alloc(phase, "hidden_lo", [P, FT, T], F32R), FT)
            relu = [wide[0][:, 2 * i:2 * i + 2, :] for i in range(4)]
            relu_free = [x_ready[DT - 1]] * 4
            for i in range(FT // 2):
                b = next_bank()
                t = act_free[0] = product(b, act)
                r = relu[i % 4]
                t = bank_readers[b] = q.act(r, bank[b][:].rearrange("p (k t) -> p k t", k=2), ACT.Relu,
                                            [t, relu_free[i % 4]])
                t = q.tt(r, r, r, ALU.mult, t)
                relu_free[i % 4] = split_tiles(hidden, 2 * i, 2, r, t)
            branch = wide[1]
            state = {}

            def evacuate(i, src, t):
                t = q.copy(branch[:, 2 * i:2 * i + 2, :], src, [t, act_free[0]])
                for k in (2 * i, 2 * i + 1):
                    state["sums"] = norm_begin(k, branch[:, k, :], t)
                return t

            mlp_done = accumulate_tiles(hidden, FT, evacuate)
        rstd_ready = norm_end(state["sums"], D)
        x_ready, sums, t = residual_norm(branch, gain2, rstd_ready)

        rstd_ready = norm_end(sums, D, t)
        modulated(cols("attn_norm_2", 0, DT), None, rstd_ready, x_ready, cols_ready)
        preload(ACT.Sigmoid)
        with ExitStack() as phase:
            CT2 = CH2 // P
            PAD = TAPS2 - 1
            q2 = alloc(phase, "q2", [HD, QH, T])
            keys = {n: alloc(phase, n + "_T", [HD, KV, T]) for n in ("ks", "kw")}
            vals = {n: alloc(phase, n + "_nat", [P, TT, KVW]) for n in ("vs", "vw")}
            gate = alloc(phase, "gate", [P, TT, 3 * QH])
            bias = alloc(phase, "bias", [P, QH, 3 * P])
            dist_i = alloc(phase, "dist_i", [P, 3 * P], I32)
            dist = alloc(phase, "dist", [P, 3 * P])
            far = alloc(phase, "far", [P, 3 * P])
            bias_c = alloc(phase, "bias_c", [P, QH, TT, N_CMP])
            dist_ci = alloc(phase, "dist_ci", [P, TT, N_CMP], I32)
            dist_c = alloc(phase, "dist_c", [P, TT, N_CMP])
            far_c = alloc(phase, "far_c", [P, TT, N_CMP])
            cmp_in = {n: alloc(phase, n + "_pairs", [P, CMP_LEN // 4, KV * N_CHUNKS + 2]) for n in ("kc", "vc")}
            cmp_hid = alloc(phase, "cmp_hid", [P, 2, KV, N_CMP])
            cmp_pe = alloc(phase, "cmp_pe", [P, 2])
            kc_T = alloc(phase, "kc_T", [HD, KV * N_CMP])
            vc_nat = alloc(phase, "vc_nat", [N_CMP, KV * HD])
            score_c = alloc(phase, "score_c", [P, QH * TT, N_CMP])
            stat_c = alloc(phase, "stat_c", [P, QH * TT])
            free = mlp_done

            conv_u = wide[0][:, 0:CT2, :]
            conv_s = wide[0][:, CT2:2 * CT2, :]
            conv_acc = wide[0][:, 4:4 + CT2, :]
            conv_tmp = wide[0][:, 6:6 + CT2, :]
            conv_pad = wide[1][:].rearrange("p k t -> p (k t)")[:, 0:CT2 * (T + PAD)].rearrange(
                "p (k t) -> p k t", k=CT2)
            cmp_raw = {"kc": wide[2][:, 0:2, :], "vc": wide[2][:, 2:4, :]}
            cmp_sum = wide[2][:, 4:6, :].rearrange("p k t -> p (k t)")[:, 0:4 * (KV * N_CHUNKS + 2)].rearrange(
                "p (m s c) -> p m s c", m=2, s=2)

            t = q.put("pool", lambda e: e.iota(dist_i[:, 0:P], pattern=[[-1, P]], base=0,
                                               channel_multiplier=1), free)
            t = q.put("pool", lambda e: e.iota(dist_i[:, P:], pattern=[[-1, 2 * P]], base=P,
                                               channel_multiplier=1), free)
            dist_ready = q.copy(dist[:], dist_i[:], [t, free])
            t = q.memset(far[:], 0.0, free, engine="pool")
            q.put("pool", lambda e: e.affine_select(
                out=far[:, 0:P], in_=far[:, 0:P], compare_op=ALU.is_ge, fill=MASKED, base=0,
                pattern=[[-1, P]], channel_multiplier=1), t)
            far_ready = q.put("pool", lambda e: e.affine_select(
                out=far[:, P:], in_=far[:, P:], compare_op=ALU.is_ge, fill=MASKED, base=P,
                pattern=[[-1, 2 * P]], channel_multiplier=1), t)
            t = q.put("pool", lambda e: e.iota(dist_ci[:], pattern=[[P, TT], [-STRIDE, N_CMP]], base=0,
                                               channel_multiplier=1), free)
            dist_c_ready = q.ts(dist_c[:], dist_ci[:], -0.5 * (CMP_LEN - 1), ALU.add, waits=[t, free])
            t = q.memset(far_c[:], 0.0, free, engine="pool")
            far_c_ready = q.put("pool", lambda e: e.affine_select(
                out=far_c[:], in_=far_c[:], compare_op=ALU.is_ge, fill=MASKED, base=-(CMP_LEN - 1),
                pattern=[[P, TT], [-STRIDE, N_CMP]], channel_multiplier=1), t)
            pad2_ready = q.memset(conv_pad[:, :, 0:PAD], 0.0, act.ready[DT - 1], engine="pool")

            ready = {}
            conv_done = [None] * CT2

            def mixer_conv():
                y = [ready["pad"], pad2_ready]
                for j in range(CT2):
                    eng = "pool" if j == 0 else "dve"
                    t = q.ts(conv_acc[:, j, :], conv_pad[:, j, 0:T], cols("conv_w_2", j, 1), ALU.mult,
                             cols("conv_b_2", j, 1), ALU.add, waits=[y, cols_ready], engine=eng)
                    for k in range(1, TAPS2):
                        if eng == "dve":
                            t = q.stt(conv_acc[:, j, :], conv_pad[:, j, k:k + T], cols("conv_w_2", k * CT2 + j, 1),
                                      conv_acc[:, j, :], ALU.mult, ALU.add, t)
                        else:
                            tmp = conv_tmp[:, k % 2, :]
                            tm = q.ts(tmp, conv_pad[:, j, k:k + T], cols("conv_w_2", k * CT2 + j, 1), ALU.mult,
                                      waits=t if k > 2 else None, engine=eng)
                            t = q.tt(conv_acc[:, j, :], conv_acc[:, j, :], tmp, ALU.add, [t, tm], engine=eng)
                    conv_done[j] = t

            def pair_tokens(name):
                dst, engine = cmp_in[name], ("act" if name == "kc" else "dve")
                out_ = []
                for g in range(KV):
                    src = cmp_raw[name][g % 2 * HD:(g % 2 + 1) * HD, g // 2, :].rearrange(
                        "p (c l two) -> p two l c", two=2, l=STRIDE // 2)
                    for par in range(2):
                        o = dst[par * HD:(par + 1) * HD, :, g * N_CHUNKS:(g + 1) * N_CHUNKS]
                        if engine == "act":
                            out_.append(q.act(o, src[:, par], ACT.Copy, [ready[name], free]))
                        else:
                            out_.append(q.copy(o, src[:, par], [ready[name], free]))
                pe_name = "cmp_k_pe_2" if name == "kc" else "cmp_v_pe_2"
                out_.append(q.copy(dst[:, :, KV * N_CHUNKS:], cols(pe_name, 0, CMP_LEN // 2).rearrange(
                    "p (s l) -> p l s", s=2), [cols_ready, free]))
                ready[name + "_pairs"] = out_

            def compress(name, half):
                c = stream.next()
                src = stream.raw_view(c)
                width = KV * N_CHUNKS + 2
                b = T_BANK
                for m in range(2):
                    dst = bank[b][:, (m * 2 + half) * width:(m * 2 + half + 1) * width]
                    for j in range(CHUNK_TILES):
                        t = q.matmul(dst, src[:, j, m * P:(m + 1) * P], cmp_in[name][:, j, :], j == 0,
                                     j == CHUNK_TILES - 1, [stream.landed[c], ready[name + "_pairs"],
                                                            bank_readers[b]], signal=(j == CHUNK_TILES - 1))
                stream.done(c, t)
                if half == 0:
                    return
                t = q.act(cmp_sum, bank[b][:, 0:4 * width].rearrange("p (m s c) -> p m s c", m=2, s=2), ACT.Copy,
                          [t, ready.get("cmp_sum_free")])
                bank_readers[b] = t
                n0 = KV * N_CHUNKS
                tp = q.tt(cmp_pe[:], cmp_sum[:, :, 0, n0], cmp_sum[:, :, 1, n0 + 1], ALU.add,
                          [t, ready.get("cmp_hid_free"), free])
                ts_ = []
                for m in range(2):
                    lo_, hi_ = (cmp_sum[:, m, s, 0:n0].rearrange("p (g c) -> p g c", g=KV) for s in range(2))
                    ts_.append(q.tt(cmp_hid[:, m], lo_[:, :, 0:N_CMP], hi_[:, :, 1:], ALU.add,
                                    [t, ready.get("cmp_hid_free"), free]))
                ready["cmp_sum_free"] = ts_
                for m in range(2):
                    v = cmp_hid[:, m].rearrange("p g n -> p (g n)")
                    t = q.act(v, v, ACT.Silu, [ts_, tp], bias=cmp_pe[:, m:m + 1])
                b = T_BANK
                if name == "kc":
                    for m in range(2):
                        t2 = q.matmul(bank[b][0:HD, 0:KV * N_CMP], w2k[:, m, :],
                                      cmp_hid[:, m].rearrange("p g n -> p (g n)"), m == 0, m == 1,
                                      [t, w2_landed, bank_readers[b]], signal=True)
                    ready["kc_T"] = bank_readers[b] = q.copy(kc_T[:], bank[b][0:HD, 0:KV * N_CMP], [t2, free])
                else:
                    for g in range(KV):
                        for m in range(2):
                            t2 = q.matmul(bank[b][0:N_CMP, g * HD:(g + 1) * HD], cmp_hid[:, m, g, :], w2v[:, m, :],
                                          m == 0, m == 1, [t, w2_landed, bank_readers[b]], signal=True)
                    ready["vc_nat"] = bank_readers[b] = q.copy(vc_nat[:], bank[b][0:N_CMP, 0:KV * HD], [t2, free])
                ready["cmp_hid_free"] = t2

            for n, (name, i) in enumerate(in2_chunks):
                if name.startswith("cmp"):
                    compress("kc" if "_k_" in name else "vc", i)
                    continue
                b = next_bank()
                t = product(b, act, tokens_first=(name in ("vs", "vw", "g")))
                act_free[0] = t
                src = bank[b][:].rearrange("p (k t) -> p k t", k=2)
                if name == "cu":
                    t = ready["cu"] = q.copy(conv_u, src, [t, x_ready, rstd_ready])
                elif name == "cv":
                    t = q.act(conv_s, src, ACT.Sigmoid, t)
                    bank_readers[b] = t
                    ready["pad"] = q.tt(conv_pad[:, :, PAD:], conv_u, conv_s, ALU.mult,
                                        [t, ready["cu"], act.ready[DT - 1]])
                elif name in ("kc", "vc"):
                    t = ready[name] = q.act(cmp_raw[name], src, ACT.Copy, [t, rstd_ready])
                    pair_tokens(name)
                    if name == "vc":
                        mixer_conv()
                elif name == "q":
                    ts_ = []
                    for j in range(4):
                        s_ = bank[b][j % 2 * HD:(j % 2 + 1) * HD, j // 2 * T:(j // 2 + 1) * T]
                        ts_.append(q.act(q2[:, 4 * i + j, :], s_, ACT.Copy, [t, free]))
                    t = ready["q"] = ts_[-1]
                elif name in ("ks", "kw"):
                    for g in range(KV):
                        s_ = bank[b][g % 2 * HD:(g % 2 + 1) * HD, g // 2 * T:(g // 2 + 1) * T]
                        t2 = q.copy(keys[name][:, g, :], s_, [t, free])
                    t = ready[name] = t2
                elif name in ("vs", "vw"):
                    t = ready[name] = q.copy(vals[name][:], src, [t, free])
                else:
                    t = ready["g"] = q.act(gate[:], bank[b][:, 0:TT * 3 * QH].rearrange(
                        "p (t c) -> p t c", t=TT), ACT.Sigmoid, [t, free])
                bank_readers[b] = t
                if name == "g":
                    for h in range(QH):
                        bias_ready = q.stt(bias[:, h, :], dist[:], -slopes[h], far[:], ALU.mult, ALU.add,
                                           [dist_ready, far_ready])
                        bias_c_ready = q.stt(bias_c[:, h], dist_c[:], -slopes[h], far_c[:], ALU.mult, ALU.add,
                                             [dist_c_ready, far_c_ready])
            preload(ACT.Exp)

            b = T_BANK
            for h in range(QH):
                for tt_ in range(TT):
                    c0 = (h * TT + tt_) * N_CMP
                    g = h // PER_KV
                    t = q.matmul(bank[b][:, c0:c0 + N_CMP], q2[:, h, tt_ * P:(tt_ + 1) * P],
                                 kc_T[:, g * N_CMP:(g + 1) * N_CMP], True, True,
                                 [ready["q"], ready["kc_T"], bank_readers[b]], signal=True)
            n_c = QH * TT * N_CMP
            shape_c = "p (h n) -> p h n"
            t = q.stt(score_c[:], bank[b][:, 0:n_c].rearrange(shape_c, n=N_CMP), INV_SQRT,
                      bias_c[:].rearrange("p h t n -> p (h t) n"), ALU.mult, ALU.add, [t, bias_c_ready, free])
            bank_readers[b] = t

            def spread(v):
                return v.rearrange("p (h o) -> p h o", o=1).to_broadcast([P, QH * TT, N_CMP])

            t = q.reduce(stat_c[:], score_c[:], ALU.max, t)
            t = q.ts(stat_c[:], stat_c[:], MASK_LIMIT, ALU.max, waits=t)
            t = q.tt(score_c[:], score_c[:], spread(stat_c[:]), ALU.subtract, t)
            t = q.act(score_c[:], score_c[:], ACT.Exp, t)
            t = q.reduce(stat_c[:], score_c[:], ALU.add, t)
            t = q.ts(stat_c[:], stat_c[:], 1e-30, ALU.max, waits=t)
            t = q.recip(stat_c[:], stat_c[:], t)
            t = q.tt(stat_c[:].rearrange("p (h t) -> p h t", t=TT), stat_c[:].rearrange("p (h t) -> p h t", t=TT),
                     gate[:].rearrange("p t (h b) -> p h t b", b=3)[:, :, :, 0], ALU.mult, [t, ready["g"]])
            ready["p_c"] = q.tt(score_c[:], score_c[:], spread(stat_c[:]), ALU.mult, t)

            score = [alloc(phase, f"score{i}", [P, 3 * P]) for i in range(4)]
            prob_T = [alloc(phase, f"prob_T{i}", [P, 3 * P]) for i in range(4)]
            pc_T = [alloc(phase, f"pc_T{i}", [N_CMP, T]) for i in range(2)]
            neg_max = [alloc(phase, f"neg_max{i}", [P, 4]) for i in range(2)]
            total = [alloc(phase, f"total{i}", [P, 4]) for i in range(2)]
            S2_BANKS, T2_BANKS, O2_BANK, C_BANK = (0, 1, 4, 5), (6, 7), 2, 3
            BR = (("ks", "vs"), ("kw", "vw"))
            free_score, free_probs = {}, {}

            def softmax(h):
                g, par = h // PER_KV, h % 2
                ts_ = []
                for br, (kn, _) in enumerate(BR):
                    b, sc = S2_BANKS[2 * par + br], score[2 * par + br]
                    q.matmul(bank[b][:, 0:P], q2[:, h, 0:P], keys[kn][:, g, 0:P], True, True,
                             [ready["q"], ready[kn], bank_readers[b]])
                    t = q.matmul(bank[b][:, P:3 * P], q2[:, h, P:T], keys[kn][:, g, :], True, True, signal=True)
                    t = bank_readers[b] = q.stt(sc[:], bank[b][:, 0:3 * P], INV_SQRT, bias[:, h, :], ALU.mult,
                                                ALU.add, [t, bias_ready, free_score.get(h - 2)])
                    for i, (lo_, hi_) in enumerate(((0, P), (P, 3 * P))):
                        c = 2 * br + i
                        t2 = q.reduce(neg_max[par][:, c:c + 1], sc[:, lo_:hi_], ALU.max,
                                      [t, free_score.get(h - 2)], negate=True)
                        ts_.append(q.act(sc[:, lo_:hi_], sc[:, lo_:hi_], ACT.Exp, [t2, free_score.get(h - 2)],
                                         bias=neg_max[par][:, c:c + 1], accum=total[par][:, c:c + 1]))
                tot = total[par]
                t = q.ts(tot[:], tot[:], 1e-30, ALU.max, waits=ts_)
                t = q.recip(tot[:], tot[:], t)
                t = q.tt(tot[:].rearrange("p (b t) -> p b t", t=TT), tot[:].rearrange("p (b t) -> p b t", t=TT),
                         gate[:, :, 3 * h + 1:3 * h + 3].rearrange("p t b -> p b t"), ALU.mult, [t, ready["g"]])
                out_ = []
                for br in range(2):
                    for i, (lo_, hi_) in enumerate(((0, P), (P, 3 * P))):
                        c = 2 * br + i
                        sc = score[2 * par + br]
                        out_.append(q.ts(sc[:, lo_:hi_], sc[:, lo_:hi_], tot[:, c:c + 1], ALU.mult, waits=t,
                                         engine="pool"))
                return out_

            def turn(h, probs_ready):
                par = h % 2
                out_ = []
                for br in range(2):
                    b = T2_BANKS[br]
                    for i in range(3):
                        t = q.transpose(bank[b][:, i * P:(i + 1) * P], score[2 * par + br][:, i * P:(i + 1) * P],
                                        ident[:], [probs_ready, bank_readers[b]], signal=(i == 2))
                    bank_readers[b] = q.act(prob_T[2 * par + br][:], bank[b][:, 0:3 * P], ACT.Copy,
                                            [t, free_probs.get(h - 2)])
                    out_.append(bank_readers[b])
                free_score[h] = t
                for tt_ in range(TT):
                    t = q.transpose(bank[C_BANK][0:N_CMP, tt_ * P:(tt_ + 1) * P], score_c[:, h * TT + tt_, :],
                                    ident[:], [ready["p_c"], bank_readers[C_BANK]], signal=(tt_ == 1))
                bank_readers[C_BANK] = q.copy(pc_T[par][:], bank[C_BANK][0:N_CMP, 0:T], [t, free_probs.get(h - 2)])
                return out_ + [bank_readers[C_BANK]]

            def attend(h, probs_T_ready):
                g, par, base = h // PER_KV, h % 2, h % 2 * HD
                o = bank[O2_BANK][base:base + HD, :]
                q.matmul(o[:, 0:T], vc_nat[:, g * HD:(g + 1) * HD], pc_T[par][:], True, False,
                         [probs_T_ready, ready["vc_nat"], bank_readers[O2_BANK]])
                for br, (_, vn) in enumerate(BR):
                    p_T, v = prob_T[2 * par + br], vals[vn]
                    q.matmul(o[:, 0:T], v[:, 0, g * HD:(g + 1) * HD], p_T[:, 0:T], False, False,
                             [ready[vn], probs_T_ready])
                    t = q.matmul(o[:, P:T], v[:, 1, g * HD:(g + 1) * HD], p_T[:, 2 * P:3 * P], False, br == 1,
                                 signal=True)
                free_probs[h] = t
                if par:
                    bank_readers[O2_BANK] = split_tiles(act, CT2 + h // 2, 1, bank[O2_BANK][:, 0:T].rearrange(
                        "p (k t) -> p k t", k=1), t, act_free[0])

            probs, probs_T = {}, {}
            for h in range(QH + 2):
                if h < QH:
                    probs[h] = softmax(h)
                if 1 <= h <= QH:
                    probs_T[h - 1] = turn(h - 1, probs[h - 1])
                if h >= 2:
                    attend(h - 2, probs_T[h - 2])

            preload(ACT.Sqrt)
            mean = conv_u[:, 0, :]
            for j in range(CT2):
                t = q.matmul(bank[C_BANK][:, 0:T], ones[:], conv_acc[:, j, :], j == 0, j == CT2 - 1,
                             [conv_done[j], bank_readers[C_BANK]], signal=True)
            t = bank_readers[C_BANK] = q.ts(mean, bank[C_BANK][:, 0:T], 1.0 / CH2, ALU.mult, waits=t)
            sums = None
            ts_ = []
            for j in range(CT2):
                ts_.append(q.tt(conv_acc[:, j, :], conv_acc[:, j, :], mean, ALU.subtract, [t, conv_done[j]]))
                sums = norm_begin(j, conv_acc[:, j, :], ts_[-1], ready["cmp_sum_free"], last=CT2 - 1)
            rstd_ready = norm_end(sums, CH2)
            preload(ACT.Silu)
            for j in range(CT2):
                z = conv_acc[:, j, :]
                t = q.tt(z, z, rstd[:], ALU.mult, [rstd_ready, ts_[j]])
                t = q.ts(z, z, cols("conv_ln_g_2", j, 1), ALU.mult, cols("conv_ln_b_2", j, 1), ALU.add, waits=t)
                t = q.act(z, z, ACT.Silu, t)
                split_tiles(act, j, 1, conv_acc[:, j:j + 1, :], t, act_free[0])
            preload(ACT.Sqrt)
            mixer2_done = list(act.ready)

        for i in range(DT // 2):
            b = next_bank()
            t = act_free[0] = product(b, act)
            s2 = slice(2 * i, 2 * i + 2)
            t = bank_readers[b] = q.tt(x_T[:, s2, :], x_T[:, s2, :], bank[b][:].rearrange("p (k t) -> p k t", k=2),
                                       ALU.add, t)
            for k in (2 * i, 2 * i + 1):
                x_ready[k] = t
                sums = norm_begin(k, x_T[:, k, :], t)
        rstd_ready = norm_end(sums, D)
        modulated(cols("ffn_norm_2", 0, DT), None, rstd_ready, x_ready, cols_ready)
        preload(ACT.Silu)

        with ExitStack() as phase:
            FT = FF2 // P
            hidden = Split(alloc(phase, "hidden2_hi", [P, FT, T], F32R), alloc(phase, "hidden2_lo", [P, FT, T], F32R), FT)
            silu = [wide[0][:, 2 * i:2 * i + 2, :] for i in range(4)]
            silu_free = [mixer2_done] * 4
            for i in range(FT // 2):
                b = next_bank()
                t = product(b, act)
                s_ = silu[i % 4]
                t_silu = bank_readers[b] = q.act(s_, bank[b][:].rearrange("p (k t) -> p k t", k=2), ACT.Silu,
                                                 [t, silu_free[i % 4]])
                b = next_bank()
                t = act_free[0] = product(b, act)
                t = bank_readers[b] = q.tt(s_, bank[b][:].rearrange("p (k t) -> p k t", k=2), s_, ALU.mult,
                                           [t, t_silu])
                silu_free[i % 4] = split_tiles(hidden, 2 * i, 2, s_, t)
            preload(ACT.Sqrt)

            def evacuate2(i, src, t):
                t = q.tt(x_T[:, 2 * i:2 * i + 2, :], x_T[:, 2 * i:2 * i + 2, :], src, ALU.add, t)
                for k in (2 * i, 2 * i + 1):
                    x_ready[k] = t
                    state["sums"] = norm_begin(k, x_T[:, k, :], t)
                return t

            accumulate_tiles(hidden, FT, evacuate2)

        rstd_ready = norm_end(state["sums"], D)
        normed, out_nat = wide[1], wide[0]
        out_v = out_nat[:].rearrange("p k t -> p (k t)").rearrange("p (t d) -> p t d", t=TT)
        fin = []
        for k in range(DT):
            fin.append(q.stt(normed[:, k, :], x_T[:, k, :], cols("final_norm", k, 1), rstd[:], ALU.mult, ALU.mult,
                             [rstd_ready, x_ready[k]]))
        n_stores = 0
        for tt_ in range(TT):
            for k in range(0, DT, 4):
                b = next_bank()
                for j in range(4):
                    t = q.transpose(bank[b][:, j * P:(j + 1) * P], normed[:, k + j, tt_ * P:(tt_ + 1) * P], ident[:],
                                    [fin[k + j], bank_readers[b]], signal=(j == 3))
                if k == 0:
                    t = q.act(out_v[:, tt_, k * P:(k + 4) * P], bank[b][:], ACT.Copy, [t, silu_free])
                else:
                    t = q.copy(out_v[:, tt_, k * P:(k + 4) * P], bank[b][:], [t, silu_free])
                bank_readers[b] = t
                n_stores += 1
                q.load("sp", out[0, tt_ * P:(tt_ + 1) * P, k * P:(k + 4) * P], out_v[:, tt_, k * P:(k + 4) * P],
                       out_sem, 16 * n_stores, t)
        q.put("sp", lambda e: e.wait_ge(out_sem, 16 * n_stores), signal=False)
        assert stream.used == len(stream.plan)

        block = fixed.enter_context(nc.Block())

        @block.sync
        def _(e):
            for issue in q.items["sp"]:
                issue(e)

        @block.tensor
        def _(e):
            for issue in q.items["pe"]:
                issue(e)

        @block.scalar
        def _(e):
            for issue in q.items["act"]:
                issue(e)

        @block.vector
        def _(e):
            for issue in q.items["dve"]:
                issue(e)

        @block.gpsimd
        def _(e):
            for issue in q.items["pool"]:
                issue(e)


INPUTS = ["x", "c", "w_ada", "b_ada", "g_pre_mix", "g_post_mix", "g_pre_mlp", "g_post_mlp", "w_in", "conv_w",
          "w_proj_conv", "w_proj_attn", "w_out", "w_mlp_in", "w_mlp_out", "attn_norm_2", "w_in_2", "conv_w_2",
          "conv_b_2", "conv_ln_g_2", "conv_ln_b_2", "cmp_k_pe_2", "cmp_k_w1_2", "cmp_k_w2_2", "cmp_v_pe_2",
          "cmp_v_w1_2", "cmp_v_w2_2", "w_out_2", "ffn_norm_2", "w_gate_up_2", "w_down_2", "final_norm_2"]


def kernel(**inputs):
    import numpy as _np
    import concourse.bacc as _bacc
    from concourse import mybir as _mybir
    from concourse.bass_utils import run_bass_kernel_spmd as _run

    nc = _bacc.Bacc("TRN2", target_bir_lowering=False, num_devices=1)
    arrays, aps = {}, {}
    for name in INPUTS:
        v = _np.ascontiguousarray(inputs[name])
        arrays[f"in_{name}"] = v
        aps[name] = nc.dram_tensor(f"in_{name}", v.shape, _mybir.dt.from_np(v.dtype), kind="ExternalInput").ap()
    y = nc.dram_tensor("out_y", arrays["in_x"].shape, _mybir.dt.float32, kind="ExternalOutput").ap()
    build(nc, aps, y)
    r = _run(nc, [arrays], core_ids=[0])
    return r.results[0]["out_y"]
```

```python
import math

import numpy as np

import concourse.bass as bass
from concourse import mybir

ALU = mybir.AluOpType
ACT = mybir.ActivationFunctionType
AX = mybir.AxisListType
F32 = mybir.dt.float32
F32R = mybir.dt.float32r
I32 = mybir.dt.int32

P = 128
CHUNK_COLS = 256
CHUNK_TILES = 8
N_RAW = 4
N_SPLIT = 3
EPS = 1e-6
MASKED = -1e38
MASK_LIMIT = -1e37


def alibi_slopes(n):
    def pow2(m):
        start = 2.0 ** (-8.0 / m)
        return [start ** (i + 1) for i in range(m)]
    if math.log2(n).is_integer():
        s = pow2(n)
    else:
        c = 2 ** math.floor(math.log2(n))
        s = pow2(c) + pow2(2 * c)[0::2][: n - c]
    return [float(x) for x in np.asarray(s, dtype=np.float32)]


class Queues:

    def __init__(self, semaphores):
        self.sem = semaphores
        self.count = {name: 0 for name in semaphores}
        self.items = {name: [] for name in semaphores}
        self.passed = {name: {} for name in semaphores}

    def put(self, engine, issue, waits=(), signal=True):
        for sem, value in flat(waits):
            if self.passed[engine].get(id(sem), 0) < value:
                self.passed[engine][id(sem)] = value
                self.items[engine].append(lambda e, s=sem, v=value: e.wait_ge(s, v))
        if not signal:
            self.items[engine].append(issue)
            return None
        self.count[engine] += 1
        sem = self.sem[engine]
        self.items[engine].append(lambda e: issue(e).then_inc(sem, 1))
        return (sem, self.count[engine])

    def load(self, engine, out, in_, sem, total, waits=()):
        self.put(engine, lambda e: e.dma_start(out, in_).then_inc(sem, 16), waits, signal=False)
        return (sem, total)

    def matmul(self, out, stationary, moving, start, stop, waits=(), signal=False):
        return self.put("pe", lambda e: e.matmul(out, stationary, moving, start=start, stop=stop,
                                                 skip_group_check=True), waits, signal)

    def transpose(self, out, in_, identity, waits=(), signal=False):
        return self.put("pe", lambda e: e.transpose(out, in_, identity), waits, signal)

    def act(self, out, in_, func, waits=(), scale=1.0, bias=None, accum=None):
        if bias is None:
            if accum is None:
                return self.put("act", lambda e: e.activation(out, in_, func, scale=scale), waits)
            return self.put("act", lambda e: e.activation(out, in_, func, scale=scale,
                                                          accum_out=accum), waits)
        if accum is None:
            return self.put("act", lambda e: e.activation(out, in_, func, scale=scale, bias=bias), waits)
        return self.put("act", lambda e: e.activation(out, in_, func, scale=scale, bias=bias,
                                                      accum_out=accum), waits)

    def tt(self, out, a, b, op, waits=(), engine="dve"):
        return self.put(engine, lambda e: e.tensor_tensor(out, a, b, op), waits)

    def ts(self, out, a, s1, op1, s2=None, op2=None, waits=(), engine="dve"):
        if op2 is None:
            return self.put(engine, lambda e: e.tensor_scalar(out, a, s1, None, op1), waits)
        return self.put(engine, lambda e: e.tensor_scalar(out, a, s1, s2, op1, op2), waits)

    def stt(self, out, a, s, b, op1, op2, waits=()):
        return self.put("dve", lambda e: e.scalar_tensor_tensor(out=out, in0=a, scalar=s, in1=b,
                                                                op0=op1, op1=op2), waits)

    def copy(self, out, in_, waits=(), engine="dve"):
        return self.put(engine, lambda e: e.tensor_copy(out, in_), waits)

    def recip(self, out, in_, waits=()):
        return self.put("dve", lambda e: e.reciprocal(out, in_), waits)

    def reduce(self, out, in_, op, waits=(), negate=False):
        return self.put("dve", lambda e: e.tensor_reduce(out, in_, AX.X, op, negate=negate), waits)

    def scan(self, out, a, b, initial, op1, op2, waits=()):
        return self.put("dve", lambda e: e.tensor_tensor_scan(out, a, b, initial, op1, op2), waits)

    def memset(self, out, value, waits=(), engine="dve"):
        return self.put(engine, lambda e: e.memset(out, value), waits)


def flat(waits):
    if waits is None:
        return []
    if isinstance(waits, tuple) and len(waits) == 2 and isinstance(waits[1], int):
        return [waits]
    return [t for w in waits for t in flat(w)]


class Split:

    def __init__(self, hi, lo, tiles):
        self.hi, self.lo = hi, lo
        self.ready = [None] * tiles


class WeightStream:

    def __init__(self, q, raw, raw_sem, hi, lo):
        self.q, self.raw, self.raw_sem, self.hi, self.lo = q, raw, raw_sem, hi, lo
        self.plan = []
        self.loaded = self.split = self.used = 0
        self.n_split = 0
        self.landed, self.raw_free, self.parts, self.split_free = [], [], [], []

    def add(self, source, split=True, use=None):
        rows, cols = source.shape
        assert rows % P == 0 and rows // P * cols <= CHUNK_TILES * CHUNK_COLS
        self.plan.append((source, use or split))

    def raw_view(self, n):
        source, _ = self.plan[n]
        kt, cols = source.shape[0] // P, source.shape[1]
        return self.raw[n % N_RAW][:, 0:kt * cols].rearrange("p (k c) -> p k c", k=kt)

    def ahead(self, limit=None):
        while True:
            n = self.loaded
            if n < len(self.plan) and (n < N_RAW or self.raw_free[n - N_RAW] is not None):
                waits = self.raw_free[n - N_RAW] if n >= N_RAW else None
                source = self.plan[n][0].rearrange("(k p) c -> p k c", p=P)
                self.landed.append(self.q.load("sp", self.raw_view(n), source, self.raw_sem[n % N_RAW],
                                               16 * (n // N_RAW + 1), waits))
                self.raw_free.append(None)
                self.loaded += 1
                continue
            n = self.split
            if limit is not None and n >= limit:
                return
            if n < self.loaded and self.products(n) < N_SPLIT:
                source, split = self.plan[n]
                if callable(split):
                    self.raw_free[n] = split(self.raw_view(n), self.landed[n])
                    if self.raw_free[n] is None:
                        return
                    self.parts.append(None)
                elif split:
                    slot = self.n_split % N_SPLIT
                    free = self.split_free[self.n_split - N_SPLIT] if self.n_split >= N_SPLIT else None
                    if self.n_split >= N_SPLIT and free is None:
                        return
                    kt, cols = source.shape[0] // P, source.shape[1]
                    hi = self.hi[slot][:, 0:kt * cols]
                    lo = self.lo[slot][:, 0:kt * cols]
                    raw = self.raw[n % N_RAW][:, 0:kt * cols]
                    t_hi = self.q.act(hi, raw, ACT.Copy, [self.landed[n], free])
                    t_lo = self.q.tt(lo, raw, hi.bitcast(F32), ALU.subtract, [t_hi, self.landed[n], free])
                    self.raw_free[n] = t_lo
                    shape = "p (k c) -> p k c"
                    self.parts.append((hi.rearrange(shape, k=kt), lo.rearrange(shape, k=kt),
                                       t_hi, t_lo, self.n_split))
                    self.n_split += 1
                    self.split_free.append(None)
                else:
                    self.parts.append(None)
                self.split += 1
                continue
            return

    def products(self, n):
        return sum(not callable(use) for _, use in self.plan[self.used:n])

    def next(self):
        self.ahead()
        while callable(self.plan[self.used][1]):
            self.used += 1
        self.used += 1
        return self.used - 1

    def done(self, n, ticket):
        if self.parts[n] is None:
            self.raw_free[n] = ticket
        else:
            self.split_free[self.parts[n][4]] = ticket


def build(nc, a, out):
    T, D = a["x"].shape[1], a["x"].shape[2]
    TT = T // P
    DT = D // P
    assert TT == 2
    CONV = a["conv_w"].shape[2]
    CT = CONV // P
    HD = 64
    ATTN = a["w_proj_attn"].shape[1]
    HEADS = ATTN // HD
    FF = a["w_mlp_in"].shape[2]
    CH2 = a["conv_b_2"].shape[1]
    TAPS2 = a["conv_w_2"].shape[1]
    KV = 4
    KVW = KV * HD
    QH = (a["w_out_2"].shape[1] - CH2) // HD
    PER_KV = QH // KV
    FF2 = a["w_down_2"].shape[1]
    CMP_LEN, CMP_HID = a["cmp_k_w1_2"].shape[1], a["cmp_k_w1_2"].shape[3]
    STRIDE = CMP_LEN // 2
    N_CHUNKS = T // STRIDE
    N_CMP = N_CHUNKS - 1
    assert T // 64 <= 8 and T <= 512
    INV_SQRT = HD ** -0.5
    slopes = alibi_slopes(QH)

    from contextlib import ExitStack
    fixed = ExitStack()
    with fixed:
        def sem(name):
            return fixed.enter_context(nc.semaphore(name))

        def alloc(stack, name, shape, dt=F32):
            return stack.enter_context(nc.sbuf_tensor(name, shape, dt))

        q = Queues({name: sem("done_" + name) for name in ("sp", "pe", "act", "dve", "pool")})
        bank = [fixed.enter_context(nc.psum_tensor(f"bank{i}", [P, 512], F32)) for i in range(8)]
        bank_readers = [None] * 8
        SUMS = 3

        raw = [alloc(fixed, f"raw{i}", [P, CHUNK_TILES * CHUNK_COLS]) for i in range(N_RAW)]
        w_hi = [alloc(fixed, f"w_hi{i}", [P, CHUNK_TILES * CHUNK_COLS], F32R) for i in range(N_SPLIT)]
        w_lo = [alloc(fixed, f"w_lo{i}", [P, CHUNK_TILES * CHUNK_COLS], F32R) for i in range(N_SPLIT)]
        stream = WeightStream(q, raw, [sem(f"raw_landed{i}") for i in range(N_RAW)], w_hi, w_lo)
        x_T = alloc(fixed, "x_T", [P, DT, T])
        act_hi = alloc(fixed, "act_hi", [P, DT, T], F32R)
        act_lo = alloc(fixed, "act_lo", [P, DT, T], F32R)
        wide = [alloc(fixed, f"wide{i}", [P, DT, T]) for i in range(3)]
        rms = alloc(fixed, "rms", [P, T])
        rstd = alloc(fixed, "rstd", [P, T])
        ident = alloc(fixed, "ident", [P, P])
        ones = alloc(fixed, "ones", [P, P])
        eps = alloc(fixed, "eps", [P, 1])
        scratch1 = alloc(fixed, "scratch1", [P, 1])

        rows = [[], [], []]
        row_at = {}
        FIRST_ROWS = 64

        def place(group, name, source):
            at = sum(s.shape[0] for _, s in rows[group]) + (FIRST_ROWS if group == 1 else 0)
            rows[group].append((at, source))
            row_at[name] = (group // 2, at)

        place(0, "c", a["c"].rearrange("o (r p) -> (o r) p", p=P))
        place(0, "b_ada", a["b_ada"].rearrange("o (r p) -> (o r) p", p=P))
        place(0, "g_pre_mix", a["g_pre_mix"].rearrange("o (r p) -> (o r) p", p=P))
        for name in ("g_post_mix", "g_pre_mlp", "g_post_mlp", "attn_norm_2", "ffn_norm_2"):
            place(1, name, a[name].rearrange("o (r p) -> (o r) p", p=P))
        place(1, "final_norm", a["final_norm_2"].rearrange("(r p) -> r p", p=P))
        place(1, "conv_w", a["conv_w"].rearrange("o k (r p) -> (o k r) p", p=P))
        place(2, "conv_w_2", a["conv_w_2"].rearrange("o k (r p) -> (o k r) p", p=P))
        for name in ("conv_b_2", "conv_ln_g_2", "conv_ln_b_2"):
            place(2, name, a[name].rearrange("o (r p) -> (o r) p", p=P))
        for name in ("cmp_k_pe_2", "cmp_v_pe_2"):
            place(2, name, a[name].rearrange("o (l two) d -> (o l) (two d)", two=2))
        assert sum(s.shape[0] for _, s in rows[0]) == FIRST_ROWS
        row_tile = [alloc(fixed, f"row_tile{i}", [P, P]) for i in range(2)]
        col_tile = [alloc(fixed, f"col_tile{i}", [P, P]) for i in range(2)]

        def cols(name, first, n):
            part, at = row_at[name]
            return col_tile[part][:, at + first:at + first + n]

        mod_acc = [alloc(fixed, f"mod_acc{i}", [P, D]) for i in range(2)]
        mod = alloc(fixed, "mod", [P, 6 * DT])
        scale1 = alloc(fixed, "scale1", [P, DT])
        scale2 = alloc(fixed, "scale2", [P, DT])
        gain1 = alloc(fixed, "gain1", [P, DT])
        gain2 = alloc(fixed, "gain2", [P, DT])
        w2k = alloc(fixed, "w2k", [P, 2, HD])
        w2v = alloc(fixed, "w2v", [P, 2, HD])
        mixer1 = ExitStack()
        scan_mask = alloc(mixer1, "scan_mask", [P, 3 * P])
        mask_T = alloc(mixer1, "mask_T", [P, 3 * P])

        def w(name):
            return a[name][0]

        def columns(name, first, n_cols):
            m = w(name)
            for c in range(first, first + n_cols, CHUNK_COLS):
                for r in range(0, m.shape[0], CHUNK_TILES * P):
                    yield m[r:min(r + CHUNK_TILES * P, m.shape[0]), c:min(c + CHUNK_COLS, first + n_cols)]

        in1 = {}
        at = 0
        for name, width in (("b", CONV), ("c", CONV), ("u", CONV), ("q", ATTN), ("k", ATTN), ("v", ATTN),
                            ("ga", D), ("gb", D)):
            in1[name] = (at, width)
            at += width
        in1_order = ("q", "k", "v", "c", "u", "b", "ga", "gb")
        ADA_TILES = CHUNK_TILES * CHUNK_COLS // D
        ADA_CHUNKS = DT // ADA_TILES

        mod_acc_readers = [None, None]
        mod_acc_busy = [False, False]
        mod_chunk = {}

        def modulation(v, r):
            def use(src, landed):
                acc, waits = mod_acc[v % 2], [landed, cols_ready]
                if r == 0 and mod_acc_busy[v % 2]:
                    return None
                mod_acc_busy[v % 2] = True
                for k in range(ADA_TILES):
                    if r == 0 and k == 0:
                        t = q.ts(acc[:], src[:, k, :], cols("c", 0, 1), ALU.mult,
                                 waits=[waits, mod_acc_readers[v % 2]])
                    else:
                        t = q.stt(acc[:], src[:, k, :], cols("c", r * ADA_TILES + k, 1), acc[:], ALU.mult, ALU.add,
                                  [waits, mod_chunk[v]])
                    mod_chunk[v] = t
                return t
            return use

        def ada_chunk(v, r):
            return w("w_ada")[r * ADA_TILES * P:(r + 1) * ADA_TILES * P, v * D:(v + 1) * D]

        SHIFT1, SCALE1, GATE1, SHIFT2, SCALE2, GATE2 = range(6)
        for v in (SCALE1, SHIFT1):
            for r in range(ADA_CHUNKS):
                stream.add(ada_chunk(v, r), use=modulation(v, r))
        ada_later = [(v, r) for v in (GATE1, SHIFT2, SCALE2, GATE2) for r in range(ADA_CHUNKS)]
        ada_plan = iter(ada_later)
        in1_chunks = [(name, i, s) for name in in1_order for i, s in enumerate(columns("w_in", *in1[name]))]
        proj_chunks = 2 * (DT // 2)
        later = [s for name in ("w_proj_conv", "w_proj_attn", "w_out", "w_mlp_in") for s in columns(name, 0, w(name).shape[1])]
        n_before_mlp = len(in1_chunks) + proj_chunks + DT // 2

        def ada_after(n):
            return n % 2 == 1 and (n < 6 * ADA_CHUNKS or n_before_mlp <= n < n_before_mlp + 2 * ADA_CHUNKS)

        ada_at, sum_after = {}, {}
        for n in range(len(in1_chunks) + len(later)):
            if ada_after(n):
                v, r = ada_at[n] = ada_later[len(ada_at)]
                if r == ADA_CHUNKS - 1:
                    sum_after[v] = n
        for n, s in enumerate([c[2] for c in in1_chunks] + later):
            stream.add(s)
            if ada_after(n):
                stream.add(ada_chunk(*next(ada_plan)), use=modulation(*ada_at[n]))
        assert next(ada_plan, None) is None
        for s in columns("w_mlp_out", 0, D):
            stream.add(s)
        in2 = {}
        at = 0
        for name, width in (("cu", CH2), ("cv", CH2), ("q", QH * HD), ("kc", KVW), ("vc", KVW), ("ks", KVW),
                            ("vs", KVW), ("kw", KVW), ("vw", KVW), ("g", 3 * QH)):
            in2[name] = (at, width)
            at += width
        in2_order = ("cu", "cv", "q0", "ks", "kw", "g", "vs", "vw", "q1", "kc", "w1k0", "w1k1",
                     "vc", "q2", "w1v0", "w1v1")
        FIRST_HEAD_AFTER = in2_order.index("g")
        assert QH * HD == 3 * CHUNK_COLS
        for name in in2_order:
            if name.startswith("w1"):
                flat_w1 = w(f"cmp_{name[2]}_w1_2").rearrange("l d h -> (l d) h")
                half = int(name[3])
                stream.add(flat_w1[half * CHUNK_TILES * P:(half + 1) * CHUNK_TILES * P, :], split=False)
            elif name in in2:
                for s in columns("w_in_2", *in2[name]):
                    stream.add(s)
            else:
                for s in columns("w_in_2", in2["q"][0] + int(name[1]) * CHUNK_COLS, CHUNK_COLS):
                    stream.add(s)
        for s in columns("w_out_2", 0, D):
            stream.add(s)
        for c in range(0, FF2, CHUNK_COLS):
            for base in (0, FF2):
                for s in columns("w_gate_up_2", base + c, CHUNK_COLS):
                    stream.add(s)
        for s in columns("w_down_2", 0, D):
            stream.add(s)

        rows_sem = [sem(f"rows{i}_landed") for i in range(3)]
        x_sem, w2_sem, out_sem = sem("x_landed"), sem("w2_landed"), sem("stored")
        x_nat = wide[0]
        x_nat_v = x_nat[:].rearrange("p k t -> p (k t)").rearrange("p (t d) -> p t d", t=TT)
        def load_rows(group):
            n = len(rows[group])
            for at, source in rows[group]:
                ticket = q.load("act" if group else "sp", row_tile[group // 2][at:at + source.shape[0], :], source,
                                rows_sem[group], 16 * n)
            return ticket

        rows_landed = [load_rows(0)]
        x_landed = q.load("act", x_nat_v, a["x"][0].rearrange("(t p) d -> p t d", p=P), x_sem, 16)
        rows_landed += [load_rows(1), load_rows(2)]
        for dst, name in ((w2k, "cmp_k_w2_2"), (w2v, "cmp_v_w2_2")):
            w2_landed = q.load("act", dst[:], w(name).rearrange("(m p) d -> p m d", p=P), w2_sem, 32)

        t = q.memset(ident[:], 0.0, engine="pool")
        ident_ready = q.put("pool", lambda e: e.affine_select(
            out=ident[:], in_=ident[:], compare_op=ALU.not_equal, fill=1.0, base=0,
            pattern=[[-1, P]], channel_multiplier=1), t)
        ones_ready = q.memset(ones[:], 1.0)
        eps_ready = q.memset(eps[:], EPS)

        t = q.memset(scan_mask[:], 0.0, engine="pool")
        q.put("pool", lambda e: e.affine_select(
            out=scan_mask[:, 0:P], in_=scan_mask[:, 0:P], compare_op=ALU.is_gt, fill=1.0, base=0,
            pattern=[[-1, P]], channel_multiplier=1), t)
        scan_mask_ready = q.put("pool", lambda e: e.affine_select(
            out=scan_mask[:, P:], in_=scan_mask[:, P:], compare_op=ALU.is_gt, fill=1.0, base=P,
            pattern=[[-1, 2 * P]], channel_multiplier=1), t)
        t = q.memset(mask_T[:], 1.0, engine="pool")
        for b in (0, 2):
            mask_T_ready = q.put("pool", lambda e, m=mask_T[:, b * P:(b + 1) * P]: e.affine_select(
                out=m, in_=m, compare_op=ALU.is_gt, fill=0.0, base=0,
                pattern=[[1, P]], channel_multiplier=-1), t)

        main_ring = [0, 1, 2]
        ring_pos = [0]

        def next_bank():
            ring_pos[0] += 1
            return main_ring[ring_pos[0] % len(main_ring)]

        def passes(n, b, act, k, start, stop, tokens_first=False, k0=0):
            hi, lo, t_hi, t_lo, _ = stream.parts[n]
            kt, n_cols = hi.shape[1], hi.shape[2]
            first, ticket = start and k == 0, None
            last_m = (TT if tokens_first else n_cols // P) - 1
            for m in range(last_m + 1):
                for wp, ap, t_w in ((hi, act.hi, t_hi), (hi, act.lo, t_hi), (lo, act.hi, t_lo)):
                    if tokens_first:
                        dst = bank[b][:, m * n_cols:(m + 1) * n_cols]
                        lhs, rhs = ap[:, k0 + k, m * P:(m + 1) * P], wp[:, k, :]
                    else:
                        dst = bank[b][:, m * T:(m + 1) * T]
                        lhs, rhs = wp[:, k, m * P:(m + 1) * P], ap[:, k0 + k, :]
                    ticket = q.matmul(dst, lhs, rhs, first, stop and k == kt - 1 and wp is lo,
                                      [t_w, act.ready[k0 + k], bank_readers[b] if first else None],
                                      signal=(k == kt - 1 and m == last_m and wp is lo))
                    first = False
            return ticket

        def product(b, act, k0=0, start=True, stop=True, tokens_first=False):
            n = stream.next()
            for k in range(stream.parts[n][0].shape[1]):
                ticket = passes(n, b, act, k, start, stop, tokens_first, k0)
            stream.done(n, ticket)
            flush_sums()
            return ticket

        def two_products(b0, b1, act):
            n0, n1 = stream.next(), stream.next()
            for k in range(DT):
                t0 = passes(n0, b0, act, k, True, True)
                t1 = passes(n1, b1, act, k, True, True)
            stream.done(n0, t0)
            stream.done(n1, t1)
            flush_sums()
            return [t0, t1]

        def each_product(n, act):
            b0, b1 = next_bank(), next_bank()
            t0, t1 = act_free[0] = two_products(b0, b1, act)
            stream.ahead()
            yield 0, b0, t0
            yield 1, b1, t1
            for i in range(2, n):
                b = next_bank()
                t = act_free[0] = product(b, act)
                yield i, b, t

        def modulation_sum(v, later=False):
            b, acc = next_bank(), mod_acc[v % 2]
            for k in range(DT):
                t = q.matmul(bank[b][:, k:k + 1], acc[:, k * P:(k + 1) * P], ones[:, 0:1], True, True,
                             [mod_chunk[v], ones_ready, bank_readers[b]], signal=(k == DT - 1))
            mod_acc_readers[v % 2], mod_acc_busy[v % 2] = t, False

            def evacuate():
                mod_vector[v] = bank_readers[b] = q.tt(mod[:, v * DT:(v + 1) * DT], bank[b][:, 0:DT],
                                                       cols("b_ada", v * DT, DT), ALU.add, [t, cols_ready])
                return mod_vector[v]

            return evacuate if later else evacuate()

        chunk_no = [0]
        mod_vector = {}

        def between():
            for v, n in sum_after.items():
                if n == chunk_no[0] and v not in (SHIFT2, SCALE2):
                    modulation_sum(v)
            chunk_no[0] += 1

        def split_tiles(act, k, n, source, ready, free=None):
            t_hi = q.act(act.hi[:, k:k + n, :], source, ACT.Copy, [ready, free])
            t_lo = q.tt(act.lo[:, k:k + n, :], source, act.hi[:, k:k + n, :].bitcast(F32),
                        ALU.subtract, [t_hi, ready, free])
            for i in range(k, k + n):
                act.ready[i] = [t_hi, t_lo]
            return [t_hi, t_lo]

        squares = wide[2]

        pending_sums = []
        sums_done = [None]

        def flush_sums():
            while pending_sums:
                pending_sums.pop(0)()

        def norm_begin(k, n, source, ready, free=None, last=DT - 1, pair_add=None):
            t_squares = t = q.act(squares[:, k:k + n, :], source, ACT.Square, [ready, free])
            if pair_add:
                t = q.tt(squares[:, k, :], squares[:, k, :], squares[:, k + 1, :], ALU.add, t, engine=pair_add)

            def sum_():
                for i in range(k, k + (1 if pair_add else n)):
                    final = i == last or (pair_add is not None and k + 1 == last)
                    sums_done[0] = q.matmul(bank[SUMS][:, 0:T], ones[:], squares[:, i, :], i == 0, final,
                                            [t, ones_ready, bank_readers[SUMS] if i == 0 else None], signal=True)

            pending_sums.append(sum_)
            return t_squares

        def norm_end(width, free=None):
            flush_sums()
            t = q.act(rms[:], bank[SUMS][:, 0:T], ACT.Sqrt, [sums_done[0], eps_ready, free],
                      scale=1.0 / width, bias=eps[:, 0:1])
            bank_readers[SUMS] = t
            return q.recip(rstd[:], rms[:], [t, free])

        preloaded = [None]

        def preload(func):
            preloaded[0] = q.act(scratch1[:], eps[:], func, [eps_ready, preloaded[0]])

        act = Split(act_hi, act_lo, DT)
        act_free = [None]

        y = wide[1]
        scaled = [None] * DT

        def scale_tile(k, scale, waits):
            scaled[k] = q.stt(y[:, k, :], x_T[:, k, :], scale[:, k:k + 1], rstd[:], ALU.mult, ALU.mult, waits)

        def shift_tile_high(k, shift, shift_ready):
            act.ready[k] = [q.act(act.hi[:, k, :], y[:, k, :], ACT.Identity, [scaled[k], shift_ready, act_free[0]],
                                  bias=shift[:, k:k + 1])]

        def shift_tile_low(k, shift, shift_ready):
            act.ready[k].append(q.stt(act.lo[:, k, :], y[:, k, :], shift[:, k:k + 1], act.hi[:, k, :].bitcast(F32),
                                      ALU.add, ALU.subtract, [act.ready[k], scaled[k], shift_ready, act_free[0]]))

        def scaled_parts(k, n, gain, ready):
            for i in range(k, k + n):
                t_hi = q.act(act.hi[:, i, :], x_T[:, i, :], ACT.Copy, [ready, cols_ready, act_free[0]],
                             scale=gain[:, i:i + 1])
                act.ready[i] = [t_hi, q.stt(act.lo[:, i, :], x_T[:, i, :], gain[:, i:i + 1],
                                            act.hi[:, i, :].bitcast(F32), ALU.mult, ALU.subtract,
                                            [t_hi, ready, cols_ready, act_free[0]])]

        rstd_2 = rstd[:].rearrange("p (o t) -> p o t", o=1).to_broadcast([P, 2, T])

        def transpose_rows(group):
            b = next_bank()
            at, n = rows[group][0][0], sum(s.shape[0] for _, s in rows[group])
            t = q.transpose(bank[b][:, 0:n], row_tile[group // 2][at:at + n, :], ident[at:at + n, at:at + n],
                            [rows_landed[group], ident_ready, bank_readers[b]], signal=True)
            bank_readers[b] = q.copy(col_tile[group // 2][:, at:at + n], bank[b][:, 0:n], t)
            return bank_readers[b]

        cols_ready = transpose_rows(0)
        stream.ahead(2)

        x_ready = [None] * DT
        for k in range(0, DT, 2):
            b = next_bank()
            for j in range(2):
                for tt_ in range(TT):
                    t = q.transpose(bank[b][:, j * T + tt_ * P:j * T + (tt_ + 1) * P],
                                    x_nat_v[:, tt_, (k + j) * P:(k + j + 1) * P], ident[:],
                                    [x_landed, ident_ready, bank_readers[b]], signal=(j + tt_ == 2))
            src = bank[b][:].rearrange("p (k t) -> p k t", k=2)
            t2 = x_ready[k] = x_ready[k + 1] = q.act(x_T[:, k:k + 2, :], src, ACT.Copy, t)
            bank_readers[b] = [t2, norm_begin(k, 2, src, t)]

        stream.ahead(ADA_CHUNKS)
        rstd_ready = norm_end(D)
        stream.ahead(ADA_CHUNKS + 2)
        t = modulation_sum(SCALE1)
        t = q.ts(scale1[:], mod[:, DT:2 * DT], 1.0, ALU.add, waits=t)
        scale1_ready = q.tt(scale1[:], scale1[:], cols("g_pre_mix", 0, DT), ALU.mult, t)
        for k in range(DT):
            t = q.act(y[:, k, :], x_T[:, k, :], ACT.Copy, [x_ready[k], scale1_ready], scale=scale1[:, k:k + 1])
            scaled[k] = q.tt(y[:, k, :], y[:, k, :], rstd[:], ALU.mult, [t, rstd_ready], engine="pool")
        stream.ahead(2 * ADA_CHUNKS)
        cols_ready = [cols_ready, transpose_rows(1)]
        cols1_ready = transpose_rows(2)
        stream.ahead(2 * ADA_CHUNKS + 1)
        t_shift = modulation_sum(SHIFT1)
        for k in range(DT):
            shift_tile_high(k, mod[:, 0:DT], t_shift)
            shift_tile_low(k, mod[:, 0:DT], t_shift)
        preload(ACT.Sigmoid)

        with mixer1 as phase:
            qk_T = [alloc(phase, f"{n}_T", [P, HEADS // 2, T]) for n in "qk"]
            v_nat = alloc(phase, "v_nat", [P, TT, ATTN])
            c_gate = alloc(phase, "c_gate", [P, CT, T])
            b_gate = alloc(phase, "b_gate", [P, CT, T])
            padded = alloc(phase, "padded", [P, CT, T + 2])
            conv_y = alloc(phase, "conv_y", [P, CT, T])
            mixed = Split(alloc(phase, "mixed_hi", [P, CT, T], F32R), alloc(phase, "mixed_lo", [P, CT, T], F32R), CT)
            heads_o = Split(alloc(phase, "heads_hi", [P, HEADS // 2, T], F32R),
                            alloc(phase, "heads_lo", [P, HEADS // 2, T], F32R), HEADS // 2)
            beta = [alloc(phase, f"beta{i}", [P, 3 * P]) for i in range(2)]
            nbeta = [alloc(phase, f"nbeta{i}", [P, 3 * P]) for i in range(2)]
            remain = [alloc(phase, f"remain{i}", [P, 3 * P + 2]) for i in range(2)]
            weight = [alloc(phase, f"weight{i}", [P, 3 * P]) for i in range(2)]
            weight_T = [alloc(phase, f"weight_T{i}", [P, 3 * P]) for i in range(2)]
            gates = [wide[0], wide[1]]

            ends_ready = []
            for r in remain:
                ends_ready.append(q.memset(r[:, P:P + 1], 1.0))
                ends_ready.append(q.memset(r[:, 3 * P + 1:3 * P + 2], 1.0))
            pad_ready = q.memset(padded[:, :, 0:2], 0.0)

            S_BANKS, T_BANK, O_BANK = (4, 5), 6, 7
            head = {}

            def stick_scores(h):
                b, base, tile = S_BANKS[h % 2], h % 2 * HD, h // 2
                qh, kh = (m[base:base + HD, tile, :] for m in qk_T)
                q.matmul(bank[b][:, 0:P], qh[:, 0:P], kh[:, 0:P], True, True, [qk_ready, bank_readers[b]])
                t = q.matmul(bank[b][:, P:3 * P], qh[:, P:T], kh, True, True, signal=True)
                free = head.get(h - 2)
                t1 = q.act(beta[h % 2][:], bank[b][:, 0:3 * P], ACT.Sigmoid, [t, free], scale=INV_SQRT)
                t2 = q.act(nbeta[h % 2][:], bank[b][:, 0:3 * P], ACT.Sigmoid, [t, free], scale=-INV_SQRT)
                bank_readers[b] = t2
                r, nb = remain[h % 2], nbeta[h % 2]
                ts_ = []
                for lo_, hi_, off in ((0, P, 0), (P, 3 * P, 1)):
                    ts_.append(q.scan(r[:, lo_ + off:hi_ + off][:, ::-1], nb[:, lo_:hi_][:, ::-1],
                                      scan_mask[:, lo_:hi_][:, ::-1], 1.0, ALU.mult, ALU.max,
                                      [t2, scan_mask_ready, ends_ready, free]))
                for lo_, hi_, off in ((0, P, 1), (P, 3 * P, 2)):
                    t = q.tt(weight[h % 2][:, lo_:hi_], beta[h % 2][:, lo_:hi_],
                             r[:, lo_ + off:hi_ + off], ALU.mult, [ts_, t1, free], engine="pool")
                return t

            def stick_transpose(h, weight_ready):
                blocks = [weight[h % 2][:, i * P:(i + 1) * P] for i in range(3)]
                for i in range(3):
                    t = q.transpose(bank[T_BANK][:, i * P:(i + 1) * P], blocks[i], ident[:],
                                    [weight_ready, bank_readers[T_BANK]], signal=(i == 2))
                head[h] = t
                t = q.tt(weight_T[h % 2][:], bank[T_BANK][:, 0:3 * P], mask_T[:], ALU.mult,
                         [t, mask_T_ready, head.get(("o", h - 2))])
                bank_readers[T_BANK] = t
                return t

            def stick_output(h, ready):
                base = h % 2 * HD
                o = bank[O_BANK][base:base + HD, :]
                q.matmul(o[:, 0:T], v_nat[:, 0, h * HD:(h + 1) * HD], weight_T[h % 2][:, 0:T], True, False,
                         [ready, v_ready, bank_readers[O_BANK]])
                t = q.matmul(o[:, P:T], v_nat[:, 1, h * HD:(h + 1) * HD], weight_T[h % 2][:, 2 * P:3 * P],
                             False, True, signal=True)
                head[("o", h)] = t
                if h % 2:
                    bank_readers[O_BANK] = split_tiles(heads_o, h // 2, 1, bank[O_BANK][:, 0:T].rearrange(
                        "p (k t) -> p k t", k=1), t)

            def short_conv():
                for j in range(CT):
                    t = q.ts(conv_y[:, j, :], padded[:, j, 0:T], cols("conv_w", j, 1), ALU.mult,
                             waits=[u_ready, pad_ready])
                    for k in (1, 2):
                        t = q.stt(conv_y[:, j, :], padded[:, j, k:k + T], cols("conv_w", k * CT + j, 1),
                                  conv_y[:, j, :], ALU.mult, ALU.add, t)
                    yield
                    t = q.tt(conv_y[:, j, :], conv_y[:, j, :], b_gate[:, j, :], ALU.mult, [t, b_ready])
                    if j % 2:
                        split_tiles(mixed, j - 1, 2, conv_y[:, j - 1:j + 1, :], t)
                        yield

            weights_of, attending, step = {}, False, 0
            conv_steps = short_conv()
            b_ready = c_ready = u_ready = qk_ready = v_ready = None
            stick_T = {}
            for n, (name, i, _) in enumerate(in1_chunks):
                if attending and step < HEADS + 2:
                    if step < HEADS:
                        weights_of[step] = stick_scores(step)
                    if 1 <= step <= HEADS:
                        stick_T[step - 1] = stick_transpose(step - 1, weights_of[step - 1])
                    if step >= 2:
                        stick_output(step - 2, stick_T[step - 2])
                    step += 1
                b = next_bank()
                t = product(b, act, tokens_first=(name == "v"))
                act_free[0] = t
                src = bank[b][:].rearrange("p (k t) -> p k t", k=2)
                s2 = slice(2 * i, 2 * i + 2)
                if name in "qk":
                    t = q.copy(qk_T["qk".index(name)][:, s2, :], src, t)
                    qk_ready = t
                elif name == "v":
                    t = q.copy(v_nat[:, :, i * CHUNK_COLS:(i + 1) * CHUNK_COLS], src, t)
                    v_ready = t
                    attending = i == 1
                elif name == "c":
                    t = c_ready = q.act(c_gate[:, s2, :], src, ACT.Copy, t)
                elif name == "u":
                    t = u_ready = q.tt(padded[:, s2, 2:], src, c_gate[:, s2, :], ALU.mult, [t, c_ready])
                elif name == "b":
                    t = b_ready = q.act(b_gate[:, s2, :], src, ACT.Copy, t)
                else:
                    t = gates_ready = q.act(gates["ga gb".split().index(name)][:, s2, :], src, ACT.Sigmoid,
                                            [t, act.ready[DT - 1]])
                bank_readers[b] = t
                between()
                if name[0] == "g":
                    next(conv_steps, None)
            assert step == HEADS + 2 and next(conv_steps, None) is None
            preload(ACT.Sqrt)
            conv_part = wide[2]
            for i in range(DT // 2):
                b = next_bank()
                t = product(b, mixed)
                s2 = slice(2 * i, 2 * i + 2)
                conv_part_ready = bank_readers[b] = q.tt(
                    conv_part[:, s2, :], bank[b][:].rearrange("p (k t) -> p k t", k=2), gates[0][:, s2, :],
                    ALU.mult, [t, gates_ready])
                between()
            for i in range(DT // 2):
                b = next_bank()
                t = product(b, heads_o)
                s2 = slice(2 * i, 2 * i + 2)
                t = bank_readers[b] = q.tt(gates[1][:, s2, :], bank[b][:].rearrange("p (k t) -> p k t", k=2),
                                           gates[1][:, s2, :], ALU.mult, [t, gates_ready])
                stream.ahead()
                t = q.tt(gates[1][:, s2, :], gates[1][:, s2, :], conv_part[:, s2, :], ALU.add,
                         [t, conv_part_ready], engine="pool" if i < DT // 2 - 1 else "dve")
                merged_ready = split_tiles(act, 2 * i, 2, gates[1][:, s2, :], t, act_free[0])
                between()
            mod_ready = q.tt(gain1[:], mod[:, GATE1 * DT:(GATE1 + 1) * DT], cols("g_post_mix", 0, DT), ALU.mult,
                             [mod_vector[GATE1], cols_ready])

        def residual_norm(source, gain, rstd_ready, then=None):
            ready = []
            for k in range(DT):
                t = q.stt(source[:, k, :], source[:, k, :], gain[:, k:k + 1], rstd[:], ALU.mult, ALU.mult,
                          [rstd_ready, mod_ready])
                t = q.tt(x_T[:, k, :], x_T[:, k, :], source[:, k, :], ALU.add, t)
                ready.append(t)
                if k % 2:
                    if then:
                        then(k - 1, ready[-2:])
                    norm_begin(k - 1, 2, x_T[:, k - 1:k + 1, :], ready[-2:], rstd_ready,
                               pair_add="pool" if k < DT - 1 else None)
            return ready

        def branch_tiles(branch, i, b, t, free=None):
            src = bank[b][:].rearrange("p (k t) -> p k t", k=2)
            t_squares = norm_begin(2 * i, 2, src, t, free, pair_add="dve" if i < DT // 2 - 1 else None)
            bank_readers[b] = q.act(branch[:, 2 * i:2 * i + 2, :], src, ACT.Copy, [t, free, t_squares])
            return bank_readers[b]

        branch = wide[0]
        main_ring[:] = [b for b in range(8) if b != SUMS]
        for i, b, t in each_product(DT // 2, act):
            branch_tiles(branch, i, b, t, merged_ready)
            between()
        rstd_ready = norm_end(D)
        finish = [modulation_sum(v, later=True) for v in (SHIFT2, SCALE2)]
        x_ready = residual_norm(branch, gain1, rstd_ready)
        mod_ready = [f() for f in finish]
        t = q.ts(scale2[:], mod[:, SCALE2 * DT:(SCALE2 + 1) * DT], 1.0, ALU.add, waits=mod_ready)
        mod_ready.append(q.tt(scale2[:], scale2[:], cols("g_pre_mlp", 0, DT), ALU.mult, [t, cols_ready]))
        rstd_ready = norm_end(D, x_ready)
        shift2 = mod[:, SHIFT2 * DT:(SHIFT2 + 1) * DT]
        for k in range(DT + 2):
            if k < DT:
                scale_tile(k, scale2, [rstd_ready, x_ready[k], mod_ready])
                shift_tile_high(k, shift2, mod_ready)
            if k >= 2:
                shift_tile_low(k - 2, shift2, mod_ready)

        def accumulate_tiles(source, n_tiles, evacuate):
            for i in range(DT // 2):
                b = next_bank()
                for r in range(0, n_tiles, CHUNK_TILES):
                    t = product(b, source, k0=r, start=(r == 0), stop=(r + CHUNK_TILES >= n_tiles))
                evacuate(i, b, t)
            return t

        with ExitStack() as phase:
            FT = FF // P
            hidden = Split(alloc(phase, "hidden_hi", [P, FT, T], F32R), alloc(phase, "hidden_lo", [P, FT, T], F32R), FT)
            relu = [wide[0][:, 2 * i:2 * i + 2, :] for i in range(4)]
            relu_free = [x_ready[DT - 1]] * 4
            for i, b, t in each_product(FT // 2, act):
                r = relu[i % 4]
                t = bank_readers[b] = q.act(r, bank[b][:].rearrange("p (k t) -> p k t", k=2), ACT.Relu,
                                            [t, relu_free[i % 4]])
                t = q.tt(r, r, r, ALU.mult, t)
                relu_free[i % 4] = split_tiles(hidden, 2 * i, 2, r, t)
                between()
            mod_ready = q.tt(gain2[:], mod[:, GATE2 * DT:], cols("g_post_mlp", 0, DT), ALU.mult, mod_vector[GATE2])
            branch = wide[1]

            def evacuate(i, b, t):
                branch_tiles(branch, i, b, t, act_free[0])

            mlp_done = accumulate_tiles(hidden, FT, evacuate)
        rstd_ready = norm_end(D)

        def attn_parts(k, ready):
            scaled_parts(k, 2, cols("attn_norm_2", 0, DT), ready)

        x_ready = residual_norm(branch, gain2, rstd_ready, then=attn_parts)

        with ExitStack() as phase:
            CT2 = CH2 // P
            PAD = TAPS2 - 1
            q2 = alloc(phase, "q2", [HD, QH, T])
            keys = {n: alloc(phase, n + "_T", [HD, KV, T]) for n in ("ks", "kw")}
            vals = {n: alloc(phase, n + "_nat", [P, TT, KVW]) for n in ("vs", "vw")}
            gate = alloc(phase, "gate", [P, TT, 3 * QH])
            bias = alloc(phase, "bias", [P, QH, 3 * P])
            dist_i = alloc(phase, "dist_i", [P, 3 * P], I32)
            dist = mod_acc[0][:, 0:3 * P]
            far = mod_acc[0][:, 3 * P:6 * P]
            bias_c = alloc(phase, "bias_c", [P, TT, QH, N_CMP])
            dist_ci = alloc(phase, "dist_ci", [P, TT, N_CMP], I32)
            dist_c = alloc(phase, "dist_c", [P, TT, N_CMP])
            far_c = alloc(phase, "far_c", [P, TT, N_CMP])
            cmp_in = alloc(phase, "cmp_in", [P, CMP_LEN // 4, KV + 1, N_CHUNKS])
            cmp_hid = alloc(phase, "cmp_hid", [P, 2, KV * N_CMP])
            cmp_pe = alloc(phase, "cmp_pe", [P, 2])
            kc_T = alloc(phase, "kc_T", [HD, KV * N_CMP])
            C_HEADS = QH // 2
            C_ROWS = C_HEADS * N_CMP
            repeat = mod_acc[0][0:N_CMP, 6 * P:6 * P + C_ROWS]
            own_rows = alloc(phase, "own_rows", [C_ROWS, C_HEADS])
            vc_own = alloc(phase, "vc_own", [C_ROWS, QH, HD])
            score_c = alloc(phase, "score_c", [P, TT * QH, N_CMP])
            stat_c = alloc(phase, "stat_c", [P, TT * QH])
            free = mlp_done

            conv_u = wide[0][:, 0:CT2, :]
            conv_s = wide[0][:, CT2:2 * CT2, :]
            conv_acc = wide[0][:, 4:4 + CT2, :]
            conv_tmp = wide[0][:, 6:6 + CT2, :]
            conv_pad = wide[1][:].rearrange("p k t -> p (k t)")[:, 0:CT2 * (T + PAD)].rearrange(
                "p (k t) -> p k t", k=CT2)
            cmp_raw = wide[2][:, 0:2, :]
            heads_o2 = [wide[0][:, i, :] for i in range(4)] + [wide[1][:, 3 + i, :] for i in range(QH // 2 - 4)]
            pc_T = wide[1][0:C_ROWS, 5:7, :]
            N_WINDOWS = (KV + 1) * N_CHUNKS - 1
            cmp_out = wide[1][0:N_WINDOWS, 7, :]
            vc_nat = wide[1][0:N_CMP, 7, :]
            mean = conv_tmp[:, 0, :]
            t = q.put("pool", lambda e: e.iota(dist_i[:, 0:P], pattern=[[-1, P]], base=0,
                                               channel_multiplier=1), free)
            t = q.put("pool", lambda e: e.iota(dist_i[:, P:], pattern=[[-1, 2 * P]], base=P,
                                               channel_multiplier=1), free)
            dist_ready = q.copy(dist[:], dist_i[:], [t, free])
            t = q.memset(far[:], 0.0, free, engine="pool")
            q.put("pool", lambda e: e.affine_select(
                out=far[:, 0:P], in_=far[:, 0:P], compare_op=ALU.is_ge, fill=MASKED, base=0,
                pattern=[[-1, P]], channel_multiplier=1), t)
            far_ready = q.put("pool", lambda e: e.affine_select(
                out=far[:, P:], in_=far[:, P:], compare_op=ALU.is_ge, fill=MASKED, base=P,
                pattern=[[-1, 2 * P]], channel_multiplier=1), t)
            t = q.put("pool", lambda e: e.iota(dist_ci[:], pattern=[[P, TT], [-STRIDE, N_CMP]], base=0,
                                               channel_multiplier=1), free)
            dist_c_ready = q.ts(dist_c[:], dist_ci[:], -0.5 * (CMP_LEN - 1), ALU.add, waits=[t, free])
            t = q.memset(far_c[:], 0.0, free, engine="pool")
            far_c_ready = q.put("pool", lambda e: e.affine_select(
                out=far_c[:], in_=far_c[:], compare_op=ALU.is_ge, fill=MASKED, base=-(CMP_LEN - 1),
                pattern=[[P, TT], [-STRIDE, N_CMP]], channel_multiplier=1), t)
            t = q.memset(own_rows[:], 1.0, free, engine="pool")
            t = q.put("pool", lambda e: e.affine_select(
                out=own_rows[:], in_=own_rows[:], compare_op=ALU.is_ge, fill=0.0, base=0,
                pattern=[[-N_CMP, C_HEADS]], channel_multiplier=1), t)
            own_ready = q.put("pool", lambda e: e.affine_select(
                out=own_rows[:], in_=own_rows[:], compare_op=ALU.is_ge, fill=0.0, base=N_CMP - 1,
                pattern=[[N_CMP, C_HEADS]], channel_multiplier=-1), t)
            t = q.memset(repeat, 0.0, free, engine="pool")
            repeat_ready = q.put("pool", lambda e: e.affine_select(
                out=repeat, in_=repeat, compare_op=ALU.not_equal, fill=1.0, base=0,
                pattern=[[0, C_HEADS], [-1, N_CMP]], channel_multiplier=1), t)
            cmp_zeros = q.memset(cmp_in[:, :, KV, :], 0.0, free, engine="pool")
            pad2_ready = q.memset(conv_pad[:, :, 0:PAD], 0.0, act.ready[DT - 1], engine="pool")

            ready = {}
            conv_done = [None] * CT2

            def mixer_conv(j):
                eng = "pool" if j == 0 else "dve"
                t = q.ts(conv_acc[:, j, :], conv_pad[:, j, 0:T], cols("conv_w_2", j, 1), ALU.mult,
                         cols("conv_b_2", j, 1), ALU.add, waits=[ready["pad"], pad2_ready, cols1_ready], engine=eng)
                for k in range(1, TAPS2):
                    yield
                    tap = cols("conv_w_2", k * CT2 + j, 1)
                    if eng == "dve":
                        t = q.stt(conv_acc[:, j, :], conv_pad[:, j, k:k + T], tap, conv_acc[:, j, :],
                                  ALU.mult, ALU.add, t)
                    else:
                        tmp = conv_tmp[:, k % 2, :]
                        tm = q.ts(tmp, conv_pad[:, j, k:k + T], tap, ALU.mult, waits=t if k > 2 else None, engine=eng)
                        t = q.tt(conv_acc[:, j, :], conv_acc[:, j, :], tmp, ALU.add, [t, tm], engine=eng)
                conv_done[j] = t

            def bias_tables():
                for h in range(QH):
                    ready["bias", h] = q.stt(bias[:, h, :], dist[:], -slopes[h], far[:], ALU.mult, ALU.add,
                                          [dist_ready, far_ready])
                    ready["bias_c"] = q.stt(bias_c[:, :, h, :], dist_c[:], -slopes[h], far_c[:], ALU.mult, ALU.add,
                                            [dist_c_ready, far_c_ready])
                    yield

            def pair_tokens(name):
                waits = [ready[name], cmp_zeros, ready.get("cmp_in_free")]
                out_ = []
                for g in range(KV):
                    src = cmp_raw[g % 2 * HD:(g % 2 + 1) * HD, g // 2, :].rearrange(
                        "p (c l two) -> p two l c", two=2, l=STRIDE // 2)
                    for par in range(2):
                        o = cmp_in[par * HD:(par + 1) * HD, :, g, :]
                        if par:
                            out_.append(q.act(o, src[:, par], ACT.Copy, waits))
                        else:
                            out_.append(q.copy(o, src[:, par], waits))
                ready["cmp_raw_free"] = list(out_)
                out_.append(q.copy(cmp_in[:, :, KV, 0:2], cols(f"cmp_{name[0]}_pe_2", 0, CMP_LEN // 2).rearrange(
                    "p (s l) -> p l s", s=2), [cols1_ready, waits]))
                ready["cmp_in"] = out_

            def compress(half):
                c = stream.next()
                src = stream.raw_view(c)
                dst = bank[SUMS][0:N_WINDOWS, 0:CMP_HID]
                for j in range(CHUNK_TILES):
                    first = half == 0 and j == 0
                    flat_in = cmp_in[:, j].rearrange("p g c -> p (g c)")
                    t = q.matmul(dst, flat_in[:, half:half + N_WINDOWS], src[:, j, :], first,
                                 half == 1 and j == CHUNK_TILES - 1,
                                 [stream.landed[c], ready["cmp_in"], bank_readers[SUMS] if first else None],
                                 signal=(j == CHUNK_TILES - 1))
                stream.done(c, t)
                if half == 1:
                    ready["cmp_in_free"] = t
                    ready["cmp_out"] = bank_readers[SUMS] = q.act(cmp_out, dst, ACT.Copy,
                                                                  [t, ready.get("cmp_out_free"), act.ready[DT - 1]])

            def cmp_hidden():
                b, rows_ = next_bank(), N_WINDOWS
                for m in range(2):
                    t = q.transpose(bank[b][:, m * P:m * P + rows_], cmp_out[:, m * P:(m + 1) * P],
                                    ident[0:rows_, 0:rows_], [ready["cmp_out"], bank_readers[b]], signal=(m == 1))
                ready["cmp_out_free"] = t
                src = bank[b][:, 0:2 * P].rearrange("p (m g c) -> p m g c", m=2, c=N_CHUNKS)
                tp = q.copy(cmp_pe[:], src[:, :, KV, 0], [t, ready.get("cmp_hid_free"), free])
                for m in range(2):
                    t = q.act(cmp_hid[:, m, :].rearrange("p (g n) -> p g n", g=KV), src[:, m, 0:KV, 0:N_CMP], ACT.Silu, tp, bias=cmp_pe[:, m:m + 1])
                ready["cmp_hid"] = bank_readers[b] = t
                preload(ACT.Exp)

            def cmp_keys():
                b = next_bank()
                for m in range(2):
                    t = q.matmul(bank[b][0:HD, 0:KV * N_CMP], w2k[:, m, :], cmp_hid[:, m, :], m == 0, m == 1,
                                 [ready["cmp_hid"], w2_landed, bank_readers[b]], signal=True)
                ready["cmp_hid_free"] = t
                ready["kc_T"] = bank_readers[b] = q.copy(kc_T[:], bank[b][0:HD, 0:KV * N_CMP], [t, free])

            def cmp_values():
                b = next_bank()
                for g in range(KV):
                    for m in range(2):
                        t = q.matmul(bank[b][0:N_CMP, g * HD:(g + 1) * HD], cmp_hid[:, m, g * N_CMP:(g + 1) * N_CMP],
                                     w2v[:, m, :], m == 0, m == 1,
                                     [ready["cmp_hid"], w2_landed, bank_readers[b]], signal=True)
                t = bank_readers[b] = q.copy(vc_nat, bank[b][0:N_CMP, 0:KVW], [t, ready["cmp_out_free"]])
                b = next_bank()
                t = q.matmul(bank[b][0:C_ROWS, 0:KVW], repeat, vc_nat, True, True,
                                                    [t, repeat_ready, bank_readers[b]], signal=True)
                for h in range(QH):
                    g, i = h // PER_KV, h % C_HEADS
                    t2 = q.ts(vc_own[:, h, :], bank[b][0:C_ROWS, g * HD:(g + 1) * HD], own_rows[:, i:i + 1],
                              ALU.mult, waits=[t, own_ready])
                ready["vc"] = bank_readers[b] = t2

            def cmp_scores():
                b = next_bank()
                for tt_ in range(TT):
                    for h in range(QH):
                        c0 = (tt_ * QH + h) * N_CMP
                        g = h // PER_KV
                        t = q.matmul(bank[b][:, c0:c0 + N_CMP], q2[:, h, tt_ * P:(tt_ + 1) * P],
                                     kc_T[:, g * N_CMP:(g + 1) * N_CMP], True, True,
                                     [ready["q2"], ready["kc_T"], bank_readers[b]], signal=True)
                n_c = QH * TT * N_CMP
                t = q.stt(score_c[:], bank[b][:, 0:n_c].rearrange("p (h n) -> p h n", n=N_CMP), INV_SQRT,
                          bias_c[:].rearrange("p t h n -> p (t h) n"), ALU.mult, ALU.add,
                          [t, ready["bias_c"], free])
                bank_readers[b] = t

                def spread(v):
                    return v.rearrange("p (h o) -> p h o", o=1).to_broadcast([P, QH * TT, N_CMP])

                t = q.reduce(stat_c[:], score_c[:], ALU.max, t)
                t = q.ts(stat_c[:], stat_c[:], MASK_LIMIT, ALU.max, waits=t)
                t = q.tt(score_c[:], score_c[:], spread(stat_c[:]), ALU.subtract, t)
                t = q.act(score_c[:], score_c[:], ACT.Exp, t)
                t = q.reduce(stat_c[:], score_c[:], ALU.add, t)
                t = q.ts(stat_c[:], stat_c[:], 1e-30, ALU.max, waits=t)
                t = q.recip(stat_c[:], stat_c[:], t)
                t = q.tt(stat_c[:].rearrange("p (t h) -> p t h", t=TT), stat_c[:].rearrange("p (t h) -> p t h", t=TT),
                         gate[:].rearrange("p t (h b) -> p t h b", b=3)[:, :, :, 0], ALU.mult, [t, ready["g"]])
                ready["p_c"] = q.tt(score_c[:], score_c[:], spread(stat_c[:]), ALU.mult, t)

            def cmp_turn():
                b = next_bank()
                for part in range(2):
                    for tt_ in range(TT):
                        h0 = tt_ * QH + part * C_HEADS
                        t = q.transpose(bank[b][0:C_ROWS, (part * TT + tt_) * P:(part * TT + tt_ + 1) * P],
                                        score_c[:, h0:h0 + C_HEADS, :].rearrange("p h n -> p (h n)"), ident[:],
                                        [ready["p_c"], bank_readers[b]], signal=(part + tt_ == 2))
                ready["pc_T"] = bank_readers[b] = q.act(
                    pc_T, bank[b][0:C_ROWS, :].rearrange("p (k t) -> p k t", k=2), ACT.Copy,
                    [t, act.ready[DT - 1]])

            def conv_norm_begin():
                for j in range(CT2):
                    t = q.matmul(bank[SUMS][:, 0:T], ones[:], conv_acc[:, j, :], j == 0, j == CT2 - 1,
                                 [conv_done[j], bank_readers[SUMS]], signal=True)
                t = bank_readers[SUMS] = q.ts(mean, bank[SUMS][:, 0:T], 1.0 / CH2, ALU.mult,
                                              waits=[t, conv_done])
                for j in range(CT2):
                    t2 = q.tt(conv_acc[:, j, :], conv_acc[:, j, :], mean, ALU.subtract, [t, conv_done[j]])
                    norm_begin(j, 1, conv_acc[:, j:j + 1, :], t2, ready["cmp_raw_free"], last=CT2 - 1)
                ready["centred"] = t2

            def conv_norm_end():
                rstd_ready = norm_end(CH2, ready["rstd_free"])
                preload(ACT.Silu)
                for j in range(CT2):
                    z = conv_acc[:, j, :]
                    t = q.tt(z, z, rstd[:], ALU.mult, [rstd_ready, ready["centred"]])
                    t = q.ts(z, z, cols("conv_ln_g_2", j, 1), ALU.mult, cols("conv_ln_b_2", j, 1), ALU.add, waits=t)
                    t = q.act(z, z, ACT.Silu, t)
                    split_tiles(act, j, 1, conv_acc[:, j:j + 1, :], t, act_free[0])

            N_HEADS_IN_FLIGHT = 3
            exps = {}
            score = [alloc(phase, f"score{i}", [P, 3 * P]) for i in range(2 * N_HEADS_IN_FLIGHT)]
            prob_T = [wide[2][:].rearrange("p k t -> p (k t)")[:, 2 * T + i * 3 * P:2 * T + (i + 1) * 3 * P]
                      for i in range(4)]
            neg_max = [alloc(phase, f"neg_max{i}", [P, 4]) for i in range(N_HEADS_IN_FLIGHT)]
            total = [alloc(phase, f"total{i}", [P, 4]) for i in range(N_HEADS_IN_FLIGHT)]
            S2_BANKS, T2_BANKS, O2_BANK = (2, 4), (5, 6), 7
            BR = (("ks", "vs"), ("kw", "vw"))
            free_score, free_probs = {}, {}

            def softmax(h):
                g, par = h // PER_KV, h % N_HEADS_IN_FLIGHT
                ts_ = []
                for br, (kn, _) in enumerate(BR):
                    b, sc = S2_BANKS[br], score[2 * par + br]
                    q.matmul(bank[b][:, 0:P], q2[:, h, 0:P], keys[kn][:, g, 0:P], True, True,
                             [ready[f"q{h // 4}"], ready[kn], bank_readers[b]])
                    t = q.matmul(bank[b][:, P:3 * P], q2[:, h, P:T], keys[kn][:, g, :], True, True, signal=True)
                    t = bank_readers[b] = q.stt(sc[:], bank[b][:, 0:3 * P], INV_SQRT, bias[:, h, :], ALU.mult,
                                                ALU.add, [t, ready["bias", h], free_score.get(h - N_HEADS_IN_FLIGHT)])
                    for i, (lo_, hi_) in enumerate(((0, P), (P, 3 * P))):
                        c = 2 * br + i
                        t2 = q.reduce(neg_max[par][:, c:c + 1], sc[:, lo_:hi_], ALU.max,
                                      [t, free_score.get(h - N_HEADS_IN_FLIGHT)], negate=True)
                        ts_.append(q.act(sc[:, lo_:hi_], sc[:, lo_:hi_], ACT.Exp, [t2, free_score.get(h - N_HEADS_IN_FLIGHT)],
                                         bias=neg_max[par][:, c:c + 1], accum=total[par][:, c:c + 1]))
                exps[h] = ts_

            def normalise(h):
                par = h % N_HEADS_IN_FLIGHT
                tot = total[par]
                t = q.ts(tot[:], tot[:], 1e-30, ALU.max, waits=exps[h])
                t = q.recip(tot[:], tot[:], t)
                t = q.tt(tot[:].rearrange("p (b t) -> p b t", t=TT), tot[:].rearrange("p (b t) -> p b t", t=TT),
                         gate[:, :, 3 * h + 1:3 * h + 3].rearrange("p t b -> p b t"), ALU.mult, [t, ready["g"]])
                out_ = []
                for br in range(2):
                    for i, (lo_, hi_) in enumerate(((0, P), (P, 3 * P))):
                        c = 2 * br + i
                        sc = score[2 * par + br]
                        out_.append(q.ts(sc[:, lo_:hi_], sc[:, lo_:hi_], tot[:, c:c + 1], ALU.mult, waits=t))
                return out_

            def turn(h, probs_ready):
                par, two = h % N_HEADS_IN_FLIGHT, h % 2
                out_ = []
                for br in range(2):
                    b = T2_BANKS[br]
                    for i in range(3):
                        t = q.transpose(bank[b][:, i * P:(i + 1) * P], score[2 * par + br][:, i * P:(i + 1) * P],
                                        ident[:], [probs_ready, bank_readers[b]], signal=(i == 2))
                    bank_readers[b] = q.act(prob_T[2 * two + br][:], bank[b][:, 0:3 * P], ACT.Copy,
                                            [t, free_probs.get(h - 2)])
                    out_.append(bank_readers[b])
                free_score[h] = t
                return out_

            def attend(h, probs_T_ready):
                g, par, base = h // PER_KV, h % 2, h % 2 * HD
                o = bank[O2_BANK][base:base + HD, :]
                for br, (_, vn) in enumerate(BR):
                    p_T, v = prob_T[2 * par + br], vals[vn]
                    q.matmul(o[:, 0:T], v[:, 0, g * HD:(g + 1) * HD], p_T[:, 0:T], br == 0, False,
                             [ready[vn], probs_T_ready, bank_readers[O2_BANK]])
                    t = q.matmul(o[:, P:T], v[:, 1, g * HD:(g + 1) * HD], p_T[:, 2 * P:3 * P], False, br == 1,
                                 signal=True)
                free_probs[h] = t
                if par:
                    ready["o", h // 2] = bank_readers[O2_BANK] = q.act(
                        heads_o2[h // 2], bank[O2_BANK][:, 0:T], ACT.Copy, [t, ready["pad"], act.ready[DT - 1]])

            probs, probs_T = {}, {}

            def head_step(h):
                if 2 <= h <= QH + 1:
                    probs_T[h - 2] = turn(h - 2, probs[h - 2])
                if h < QH:
                    softmax(h)
                if 1 <= h <= QH:
                    probs[h - 1] = normalise(h - 1)
                if 3 <= h:
                    attend(h - 3, probs_T[h - 3])

            def chunk(name, b=None, t=None):
                if name.startswith("w1"):
                    compress(int(name[3]))
                    return
                if b is None:
                    b = next_bank()
                    t = act_free[0] = product(b, act, tokens_first=(name in ("vs", "vw", "g")))
                src = bank[b][:].rearrange("p (k t) -> p k t", k=2)
                t = [t, rstd_ready]
                if name == "cu":
                    t = ready["cu"] = q.tt(conv_u, src, rstd_2, ALU.mult, [t, x_ready])
                elif name == "cv":
                    t = q.tt(conv_s, src, rstd_2, ALU.mult, [t, x_ready])
                    bank_readers[b] = t
                    t = q.act(conv_s, conv_s, ACT.Sigmoid, t)
                    ready["pad"] = q.tt(conv_pad[:, :, PAD:], conv_u, conv_s, ALU.mult, [t, ready["cu"]])
                    work["dve"].append(mixer_conv(1))
                    work["pool"].append(mixer_conv(0))
                    return
                elif name in ("kc", "vc"):
                    t = ready[name] = ready["rstd_free"] = q.tt(cmp_raw, src, rstd_2, ALU.mult,
                                                                [t, ready.get("cmp_raw_free")])
                    pair_tokens(name)
                elif name[0] == "q":
                    for j in range(4):
                        s_ = bank[b][j % 2 * HD:(j % 2 + 1) * HD, j // 2 * T:(j // 2 + 1) * T]
                        t2 = q.tt(q2[:, 4 * int(name[1]) + j, :], s_, rstd[j % 2 * HD:(j % 2 + 1) * HD, :],
                                  ALU.mult, [t, free])
                    t = ready[name] = t2
                elif name in ("ks", "kw"):
                    for g in range(KV):
                        s_ = bank[b][g % 2 * HD:(g % 2 + 1) * HD, g // 2 * T:(g // 2 + 1) * T]
                        t2 = q.tt(keys[name][:, g, :], s_, rstd[g % 2 * HD:(g % 2 + 1) * HD, :], ALU.mult, [t, free])
                    t = ready[name] = t2
                elif name in ("vs", "vw"):
                    for tt_ in range(TT):
                        t2 = q.ts(vals[name][:, tt_, :], src[:, tt_, :], rstd_col[:, tt_:tt_ + 1], ALU.mult,
                                  waits=[t, rstd_col_ready, free])
                    t = ready[name] = t2
                else:
                    for tt_ in range(TT):
                        t2 = q.ts(gate[:, tt_, :], bank[b][:, tt_ * 3 * QH:(tt_ + 1) * 3 * QH],
                                  rstd_col[:, tt_:tt_ + 1], ALU.mult, waits=[t, rstd_col_ready, free])
                    t = t2
                    ready["g"] = q.act(gate[:], gate[:], ACT.Sigmoid, t)
                    preload(ACT.Exp)
                bank_readers[b] = t

            work = {"dve": [bias_tables()], "pool": []}

            def background(engine, n):
                while n and work[engine]:
                    try:
                        next(work[engine][0])
                        n -= 1
                    except StopIteration:
                        work[engine].pop(0)

            rstd_col = alloc(phase, "rstd_col", [P, TT])
            chunks = list(in2_order[FIRST_HEAD_AFTER + 1:])
            after_k, after_v = chunks.index("w1k1") + 1, chunks.index("w1v1") + 1
            stages = {after_k: [cmp_hidden], after_k + 1: [cmp_keys],
                      after_v: [cmp_scores, conv_norm_begin], after_v + 1: [conv_norm_end, cmp_hidden],
                      after_v + 2: [cmp_turn, cmp_values]}
            b0, b1 = next_bank(), next_bank()
            t0, t1 = act_free[0] = two_products(b0, b1, act)
            rstd_ready = norm_end(D, x_ready)
            stream.ahead()
            background("dve", 2)
            preload(ACT.Sigmoid)
            chunk("cu", b0, t0)
            chunk("cv", b1, t1)
            assert in2_order[0:2] == ("cu", "cv")
            for name in in2_order[2:FIRST_HEAD_AFTER + 1]:
                background("dve", 3)
                background("pool", 2)
                chunk(name)
                if name == in2_order[2]:
                    b = next_bank()
                    for tt_ in range(TT):
                        t = q.transpose(bank[b][:, tt_ * P:(tt_ + 1) * P], rstd[:, tt_ * P:(tt_ + 1) * P], ident[:],
                                        [rstd_ready, bank_readers[b]], signal=(tt_ == TT - 1))
                    rstd_col_ready = bank_readers[b] = q.copy(
                        rstd_col[:], bank[b][:, 0:TT * P].rearrange("p (k t) -> p k t", k=TT)[:, :, 0], [t, free])
            main_ring[:] = [0, 1]
            for h in range(QH + 3):
                head_step(h)
                background("dve", 3)
                background("pool", 3)
                if h == after_v:
                    background("dve", 1000)
                    background("pool", 1000)
                for stage in stages.get(h, ()):
                    stage()
                if h < len(chunks):
                    chunk(chunks[h])

            for i in range(QH // 2):
                b = next_bank()
                for h in (2 * i, 2 * i + 1):
                    base = h % 2 * HD
                    t = q.matmul(bank[b][base:base + HD, 0:T], vc_own[:, h, :], pc_T[:, h // C_HEADS, :], True, True,
                                 [ready["vc"], ready["pc_T"], bank_readers[b]], signal=True)
                t = bank_readers[b] = q.tt(heads_o2[i], heads_o2[i], bank[b][:, 0:T], ALU.add, [t, ready["o", i]])
                split_tiles(act, CT2 + i, 1, heads_o2[i].rearrange("p (k t) -> p k t", k=1), t, act_free[0])

            main_ring[:] = [b for b in range(8) if b != SUMS]
            preload(ACT.Sqrt)
            mixer2_done = list(act.ready)

        ffn_tiles = []
        for i, b, t in each_product(DT // 2, act):
            s2 = slice(2 * i, 2 * i + 2)
            t = bank_readers[b] = q.tt(x_T[:, s2, :], x_T[:, s2, :], bank[b][:].rearrange("p (k t) -> p k t", k=2),
                                       ALU.add, t)
            x_ready[2 * i] = x_ready[2 * i + 1] = t
            ffn_tiles.append((2 * i, t))
            norm_begin(2 * i, 2, x_T[:, s2, :], t, pair_add="dve")
        for k, t in ffn_tiles:
            scaled_parts(k, 2, cols("ffn_norm_2", 0, DT), t)

        with ExitStack() as phase:
            FT = FF2 // P
            hidden = Split(alloc(phase, "hidden2_hi", [P, FT, T], F32R), alloc(phase, "hidden2_lo", [P, FT, T], F32R), FT)
            silu = [wide[0][:, 2 * i:2 * i + 2, :] for i in range(4)]
            silu_free = [mixer2_done] * 4
            for i in range(FT // 2):
                b, b_up = next_bank(), next_bank()
                if i == 0:
                    t, t_up = act_free[0] = two_products(b, b_up, act)
                    rstd_ready = norm_end(D)
                    preload(ACT.Silu)
                    stream.ahead()
                else:
                    t = product(b, act)
                s_ = silu[i % 4]
                t = bank_readers[b] = q.tt(s_, bank[b][:].rearrange("p (k t) -> p k t", k=2), rstd_2, ALU.mult,
                                           [t, rstd_ready, silu_free[i % 4]])
                t = q.act(s_, s_, ACT.Silu, t)
                t = q.tt(s_, s_, rstd_2, ALU.mult, [t, rstd_ready], engine="pool")
                if i:
                    t_up = act_free[0] = product(b_up, act)
                t = bank_readers[b_up] = q.tt(s_, bank[b_up][:].rearrange("p (k t) -> p k t", k=2), s_, ALU.mult,
                                              [t, t_up])
                silu_free[i % 4] = split_tiles(hidden, 2 * i, 2, s_, t)
            preload(ACT.Sqrt)

            def evacuate2(i, b, t):
                x_tiles = x_T[:, 2 * i:2 * i + 2, :]
                t = bank_readers[b] = q.tt(x_tiles, x_tiles, bank[b][:].rearrange("p (k t) -> p k t", k=2), ALU.add, t)
                x_ready[2 * i] = x_ready[2 * i + 1] = t
                norm_begin(2 * i, 2, x_tiles, t, pair_add="dve" if i < DT // 2 - 1 else None)

            accumulate_tiles(hidden, FT, evacuate2)

        rstd_ready = norm_end(D)
        normed, out_nat = wide[1], wide[0]
        out_v = out_nat[:].rearrange("p k t -> p (k t)").rearrange("p (t d) -> p t d", t=TT)
        fin = []
        for k in range(DT):
            fin.append(q.stt(normed[:, k, :], x_T[:, k, :], cols("final_norm", k, 1), rstd[:], ALU.mult, ALU.mult,
                             [rstd_ready, x_ready[k]]))
        n_stores = 0
        for tt_ in range(TT):
            for k in range(0, DT, 4):
                b = next_bank()
                for j in range(4):
                    t = q.transpose(bank[b][:, j * P:(j + 1) * P], normed[:, k + j, tt_ * P:(tt_ + 1) * P], ident[:],
                                    [fin[k + j], bank_readers[b]], signal=(j == 3))
                if k == 0:
                    t = q.act(out_v[:, tt_, k * P:(k + 4) * P], bank[b][:], ACT.Copy, [t, silu_free])
                else:
                    t = q.copy(out_v[:, tt_, k * P:(k + 4) * P], bank[b][:], [t, silu_free])
                bank_readers[b] = t
                n_stores += 1
                q.load("sp", out[0, tt_ * P:(tt_ + 1) * P, k * P:(k + 4) * P], out_v[:, tt_, k * P:(k + 4) * P],
                       out_sem, 16 * n_stores, t)
        q.put("sp", lambda e: e.wait_ge(out_sem, 16 * n_stores), signal=False)
        assert stream.used == len(stream.plan)

        block = fixed.enter_context(nc.Block())

        @block.sync
        def _(e):
            for issue in q.items["sp"]:
                issue(e)

        @block.tensor
        def _(e):
            for issue in q.items["pe"]:
                issue(e)

        @block.scalar
        def _(e):
            for issue in q.items["act"]:
                issue(e)

        @block.vector
        def _(e):
            for issue in q.items["dve"]:
                issue(e)

        @block.gpsimd
        def _(e):
            for issue in q.items["pool"]:
                issue(e)


INPUTS = ["x", "c", "w_ada", "b_ada", "g_pre_mix", "g_post_mix", "g_pre_mlp", "g_post_mlp", "w_in", "conv_w",
          "w_proj_conv", "w_proj_attn", "w_out", "w_mlp_in", "w_mlp_out", "attn_norm_2", "w_in_2", "conv_w_2",
          "conv_b_2", "conv_ln_g_2", "conv_ln_b_2", "cmp_k_pe_2", "cmp_k_w1_2", "cmp_k_w2_2", "cmp_v_pe_2",
          "cmp_v_w1_2", "cmp_v_w2_2", "w_out_2", "ffn_norm_2", "w_gate_up_2", "w_down_2", "final_norm_2"]


def kernel(**inputs):
    import numpy as _np
    import concourse.bacc as _bacc
    from concourse import mybir as _mybir
    from concourse.bass_utils import run_bass_kernel_spmd as _run

    nc = _bacc.Bacc("TRN2", target_bir_lowering=False, num_devices=1)
    arrays, aps = {}, {}
    for name in INPUTS:
        v = _np.ascontiguousarray(inputs[name])
        arrays[f"in_{name}"] = v
        aps[name] = nc.dram_tensor(f"in_{name}", v.shape, _mybir.dt.from_np(v.dtype), kind="ExternalInput").ap()
    y = nc.dram_tensor("out_y", arrays["in_x"].shape, _mybir.dt.float32, kind="ExternalOutput").ap()
    build(nc, aps, y)
    r = _run(nc, [arrays], core_ids=[0])
    return r.results[0]["out_y"]
```

```python
import math
from functools import partial

import numpy as np

import concourse.bass as bass
from concourse import mybir

ALU = mybir.AluOpType
ACT = mybir.ActivationFunctionType
AX = mybir.AxisListType
F32 = mybir.dt.float32
F32R = mybir.dt.float32r
I32 = mybir.dt.int32

P = 128
CHUNK_COLS = 256
CHUNK_TILES = 8
N_RAW = 4
N_SPLIT = 3
EPS = 1e-6
MASKED = -1e38
MASK_LIMIT = -1e37


def alibi_slopes(n):
    def pow2(m):
        start = 2.0 ** (-8.0 / m)
        return [start ** (i + 1) for i in range(m)]
    if math.log2(n).is_integer():
        s = pow2(n)
    else:
        c = 2 ** math.floor(math.log2(n))
        s = pow2(c) + pow2(2 * c)[0::2][: n - c]
    return [float(x) for x in np.asarray(s, dtype=np.float32)]


class Queues:

    def __init__(self, semaphores):
        self.sem = semaphores
        self.count = {name: 0 for name in semaphores}
        self.items = {name: [] for name in semaphores}
        self.passed = {name: {} for name in semaphores}

    def put(self, engine, issue, waits=(), signal=True):
        for sem, value in flat(waits):
            if self.passed[engine].get(id(sem), 0) < value:
                self.passed[engine][id(sem)] = value
                self.items[engine].append(lambda e, s=sem, v=value: e.wait_ge(s, v))
        if not signal:
            self.items[engine].append(issue)
            return None
        self.count[engine] += 1
        sem = self.sem[engine]
        self.items[engine].append(lambda e: issue(e).then_inc(sem, 1))
        return (sem, self.count[engine])

    def load(self, engine, out, in_, sem, total, waits=()):
        self.put(engine, lambda e: e.dma_start(out, in_).then_inc(sem, 16), waits, signal=False)
        return (sem, total)

    def matmul(self, out, stationary, moving, start, stop, waits=(), signal=False):
        return self.put("pe", lambda e: e.matmul(out, stationary, moving, start=start, stop=stop,
                                                 skip_group_check=True), waits, signal)

    def transpose(self, out, in_, identity, waits=(), signal=False):
        return self.put("pe", lambda e: e.transpose(out, in_, identity), waits, signal)

    def act(self, out, in_, func, waits=(), scale=1.0, bias=None, accum=None):
        if bias is None:
            if accum is None:
                return self.put("act", lambda e: e.activation(out, in_, func, scale=scale), waits)
            return self.put("act", lambda e: e.activation(out, in_, func, scale=scale,
                                                          accum_out=accum), waits)
        if accum is None:
            return self.put("act", lambda e: e.activation(out, in_, func, scale=scale, bias=bias), waits)
        return self.put("act", lambda e: e.activation(out, in_, func, scale=scale, bias=bias,
                                                      accum_out=accum), waits)

    def tt(self, out, a, b, op, waits=(), engine="dve"):
        return self.put(engine, lambda e: e.tensor_tensor(out, a, b, op), waits)

    def ts(self, out, a, s1, op1, s2=None, op2=None, waits=(), engine="dve"):
        if op2 is None:
            return self.put(engine, lambda e: e.tensor_scalar(out, a, s1, None, op1), waits)
        return self.put(engine, lambda e: e.tensor_scalar(out, a, s1, s2, op1, op2), waits)

    def stt(self, out, a, s, b, op1, op2, waits=()):
        return self.put("dve", lambda e: e.scalar_tensor_tensor(out=out, in0=a, scalar=s, in1=b,
                                                                op0=op1, op1=op2), waits)

    def copy(self, out, in_, waits=(), engine="dve"):
        return self.put(engine, lambda e: e.tensor_copy(out, in_), waits)

    def recip(self, out, in_, waits=()):
        return self.put("dve", lambda e: e.reciprocal(out, in_), waits)

    def reduce(self, out, in_, op, waits=(), negate=False):
        return self.put("dve", lambda e: e.tensor_reduce(out, in_, AX.X, op, negate=negate), waits)

    def scan(self, out, a, b, initial, op1, op2, waits=()):
        return self.put("dve", lambda e: e.tensor_tensor_scan(out, a, b, initial, op1, op2), waits)

    def memset(self, out, value, waits=(), engine="dve"):
        return self.put(engine, lambda e: e.memset(out, value), waits)


def flat(waits):
    if waits is None:
        return []
    if isinstance(waits, tuple) and len(waits) == 2 and isinstance(waits[1], int):
        return [waits]
    return [t for w in waits for t in flat(w)]


class Split:

    def __init__(self, hi, lo, tiles):
        self.hi, self.lo = hi, lo
        self.ready = [None] * tiles


class WeightStream:

    def __init__(self, q, raw, raw_sem, hi, lo):
        self.q, self.raw, self.raw_sem, self.hi, self.lo = q, raw, raw_sem, hi, lo
        self.plan = []
        self.loaded = self.split = self.used = 0
        self.lows_due = []
        self.low_engine = "dve"
        self.n_split = 0
        self.landed, self.raw_free, self.parts, self.split_free = [], [], [], []

    def add(self, source, split=True, use=None):
        rows, cols = source.shape
        assert rows % P == 0 and rows // P * cols <= CHUNK_TILES * CHUNK_COLS
        self.plan.append((source, use or split))

    def raw_view(self, n):
        source, _ = self.plan[n]
        kt, cols = source.shape[0] // P, source.shape[1]
        return self.raw[n % N_RAW][:, 0:kt * cols].rearrange("p (k c) -> p k c", k=kt)

    def low_part(self, n):
        hi, lo, t_hi, _, slot_no, free = self.parts[n]
        raw = self.raw[n % N_RAW][:, 0:hi.shape[1] * hi.shape[2]]
        shape = "p k c -> p (k c)"
        t_lo = self.q.tt(lo.rearrange(shape), raw, hi.rearrange(shape).bitcast(F32), ALU.subtract,
                         [t_hi, self.landed[n], free], engine=self.low_engine)
        self.raw_free[n] = t_lo
        self.parts[n] = (hi, lo, t_hi, t_lo, slot_no, free)

    def ahead(self, limit=None, high_only=False):
        while self.lows_due:
            self.low_part(self.lows_due.pop(0))
        while True:
            n = self.loaded
            if n < len(self.plan) and (n < N_RAW or self.raw_free[n - N_RAW] is not None):
                waits = self.raw_free[n - N_RAW] if n >= N_RAW else None
                source = self.plan[n][0].rearrange("(k p) c -> p k c", p=P)
                self.landed.append(self.q.load("sp", self.raw_view(n), source, self.raw_sem[n % N_RAW],
                                               16 * (n // N_RAW + 1), waits))
                self.raw_free.append(None)
                self.loaded += 1
                continue
            n = self.split
            if limit is not None and n >= limit:
                return
            if n < self.loaded and self.products(n) < N_SPLIT:
                source, split = self.plan[n]
                if callable(split):
                    if high_only:
                        return
                    self.raw_free[n] = split(self.raw_view(n), self.landed[n])
                    if self.raw_free[n] is None:
                        return
                    self.parts.append(None)
                elif split:
                    slot = self.n_split % N_SPLIT
                    free = self.split_free[self.n_split - N_SPLIT] if self.n_split >= N_SPLIT else None
                    if self.n_split >= N_SPLIT and free is None:
                        return
                    kt, cols = source.shape[0] // P, source.shape[1]
                    shape = "p (k c) -> p k c"
                    t_hi = self.q.act(self.hi[slot][:, 0:kt * cols], self.raw[n % N_RAW][:, 0:kt * cols], ACT.Copy,
                                      [self.landed[n], free])
                    self.parts.append((self.hi[slot][:, 0:kt * cols].rearrange(shape, k=kt),
                                       self.lo[slot][:, 0:kt * cols].rearrange(shape, k=kt),
                                       t_hi, None, self.n_split, free))
                    if high_only:
                        self.lows_due.append(n)
                    else:
                        self.low_part(n)
                    self.n_split += 1
                    self.split_free.append(None)
                else:
                    self.parts.append(None)
                self.split += 1
                continue
            return

    def products(self, n):
        return sum(not callable(use) for _, use in self.plan[self.used:n])

    def next(self):
        self.ahead()
        while callable(self.plan[self.used][1]):
            self.used += 1
        self.used += 1
        return self.used - 1

    def done(self, n, ticket):
        if self.parts[n] is None:
            self.raw_free[n] = ticket
        else:
            self.split_free[self.parts[n][4]] = ticket


def build(nc, a, out):
    T, D = a["x"].shape[1], a["x"].shape[2]
    TT = T // P
    DT = D // P
    assert TT == 2
    CONV = a["conv_w"].shape[2]
    CT = CONV // P
    HD = 64
    ATTN = a["w_proj_attn"].shape[1]
    HEADS = ATTN // HD
    FF = a["w_mlp_in"].shape[2]
    CH2 = a["conv_b_2"].shape[1]
    TAPS2 = a["conv_w_2"].shape[1]
    KV = 4
    KVW = KV * HD
    QH = (a["w_out_2"].shape[1] - CH2) // HD
    PER_KV = QH // KV
    FF2 = a["w_down_2"].shape[1]
    CMP_LEN, CMP_HID = a["cmp_k_w1_2"].shape[1], a["cmp_k_w1_2"].shape[3]
    STRIDE = CMP_LEN // 2
    N_CHUNKS = T // STRIDE
    N_CMP = N_CHUNKS - 1
    assert T // 64 <= 8 and T <= 512
    INV_SQRT = HD ** -0.5
    slopes = alibi_slopes(QH)

    from contextlib import ExitStack
    fixed = ExitStack()
    with fixed:
        def sem(name):
            return fixed.enter_context(nc.semaphore(name))

        def alloc(stack, name, shape, dt=F32):
            return stack.enter_context(nc.sbuf_tensor(name, shape, dt))

        q = Queues({name: sem("done_" + name) for name in ("sp", "pe", "act", "dve", "pool")})
        bank = [fixed.enter_context(nc.psum_tensor(f"bank{i}", [P, 512], F32)) for i in range(8)]
        bank_readers = [None] * 8
        SUMS = 3

        raw = [alloc(fixed, f"raw{i}", [P, CHUNK_TILES * CHUNK_COLS]) for i in range(N_RAW)]
        w_hi = [alloc(fixed, f"w_hi{i}", [P, CHUNK_TILES * CHUNK_COLS], F32R) for i in range(N_SPLIT)]
        w_lo = [alloc(fixed, f"w_lo{i}", [P, CHUNK_TILES * CHUNK_COLS], F32R) for i in range(N_SPLIT)]
        stream = WeightStream(q, raw, [sem(f"raw_landed{i}") for i in range(N_RAW)], w_hi, w_lo)
        x_T = alloc(fixed, "x_T", [P, DT, T])
        act_hi = alloc(fixed, "act_hi", [P, DT, T], F32R)
        act_lo = alloc(fixed, "act_lo", [P, DT, T], F32R)
        wide = [alloc(fixed, f"wide{i}", [P, DT, T]) for i in range(3)]
        rms = alloc(fixed, "rms", [P, T])
        rstd = alloc(fixed, "rstd", [P, T])
        ident = alloc(fixed, "ident", [P, P])
        ones = alloc(fixed, "ones", [P, P])
        eps = alloc(fixed, "eps", [P, 1])
        scratch1 = alloc(fixed, "scratch1", [P, 1])

        rows = [[], [], []]
        row_at = {}
        FIRST_ROWS = 64

        def place(group, name, source):
            at = sum(s.shape[0] for _, s in rows[group]) + (FIRST_ROWS if group == 1 else 0)
            rows[group].append((at, source))
            row_at[name] = (group // 2, at)

        place(0, "c", a["c"].rearrange("o (r p) -> (o r) p", p=P))
        place(0, "b_ada", a["b_ada"].rearrange("o (r p) -> (o r) p", p=P))
        place(0, "g_pre_mix", a["g_pre_mix"].rearrange("o (r p) -> (o r) p", p=P))
        for name in ("g_post_mix", "g_pre_mlp", "g_post_mlp", "attn_norm_2", "ffn_norm_2"):
            place(1, name, a[name].rearrange("o (r p) -> (o r) p", p=P))
        place(1, "final_norm", a["final_norm_2"].rearrange("(r p) -> r p", p=P))
        place(1, "conv_w", a["conv_w"].rearrange("o k (r p) -> (o k r) p", p=P))
        place(2, "conv_w_2", a["conv_w_2"].rearrange("o k (r p) -> (o k r) p", p=P))
        for name in ("conv_b_2", "conv_ln_g_2", "conv_ln_b_2"):
            place(2, name, a[name].rearrange("o (r p) -> (o r) p", p=P))
        for name in ("cmp_k_pe_2", "cmp_v_pe_2"):
            place(2, name, a[name].rearrange("o (l two) d -> (o l) (two d)", two=2))
        assert sum(s.shape[0] for _, s in rows[0]) == FIRST_ROWS
        row_tile = [alloc(fixed, f"row_tile{i}", [P, P]) for i in range(2)]
        col_tile = [alloc(fixed, f"col_tile{i}", [P, P]) for i in range(2)]

        def cols(name, first, n):
            part, at = row_at[name]
            return col_tile[part][:, at + first:at + first + n]

        mod_acc = [alloc(fixed, f"mod_acc{i}", [P, D]) for i in range(2)]
        mod = alloc(fixed, "mod", [P, 6 * DT])
        scale1 = alloc(fixed, "scale1", [P, DT])
        scale2 = alloc(fixed, "scale2", [P, DT])
        gain1 = alloc(fixed, "gain1", [P, DT])
        gain2 = alloc(fixed, "gain2", [P, DT])
        w2k = alloc(fixed, "w2k", [P, 2, HD])
        w2v = alloc(fixed, "w2v", [P, 2, HD])
        mixer1 = ExitStack()
        scan_mask = alloc(mixer1, "scan_mask", [P, 3 * P])
        mask_T = alloc(mixer1, "mask_T", [P, 3 * P])

        def w(name):
            return a[name][0]

        def columns(name, first, n_cols):
            m = w(name)
            for c in range(first, first + n_cols, CHUNK_COLS):
                for r in range(0, m.shape[0], CHUNK_TILES * P):
                    yield m[r:min(r + CHUNK_TILES * P, m.shape[0]), c:min(c + CHUNK_COLS, first + n_cols)]

        in1 = {}
        at = 0
        for name, width in (("b", CONV), ("c", CONV), ("u", CONV), ("q", ATTN), ("k", ATTN), ("v", ATTN),
                            ("ga", D), ("gb", D)):
            in1[name] = (at, width)
            at += width
        in1_order = ("q", "k", "v", "c", "u", "b", "ga", "gb")
        ADA_TILES = CHUNK_TILES * CHUNK_COLS // D
        ADA_CHUNKS = DT // ADA_TILES

        mod_acc_readers = [None, None]
        mod_acc_busy = [False, False]
        mod_chunk = {}

        def modulation(v, r):
            def use(src, landed):
                acc, waits = mod_acc[v % 2], [landed, cols_ready]
                if r == 0 and mod_acc_busy[v % 2]:
                    return None
                mod_acc_busy[v % 2] = True
                for k in range(ADA_TILES):
                    if r == 0 and k == 0:
                        t = q.ts(acc[:], src[:, k, :], cols("c", 0, 1), ALU.mult,
                                 waits=[waits, mod_acc_readers[v % 2]])
                    else:
                        t = q.stt(acc[:], src[:, k, :], cols("c", r * ADA_TILES + k, 1), acc[:], ALU.mult, ALU.add,
                                  [waits, mod_chunk[v]])
                    mod_chunk[v] = t
                return t
            return use

        def ada_chunk(v, r):
            return w("w_ada")[r * ADA_TILES * P:(r + 1) * ADA_TILES * P, v * D:(v + 1) * D]

        SHIFT1, SCALE1, GATE1, SHIFT2, SCALE2, GATE2 = range(6)
        for v in (SCALE1, SHIFT1):
            for r in range(ADA_CHUNKS):
                stream.add(ada_chunk(v, r), use=modulation(v, r))
        ada_later = [(v, r) for v in (GATE1, SHIFT2, SCALE2, GATE2) for r in range(ADA_CHUNKS)]
        ada_plan = iter(ada_later)
        in1_chunks = [(name, i, s) for name in in1_order for i, s in enumerate(columns("w_in", *in1[name]))]
        proj_chunks = 2 * (DT // 2)
        later = [s for name in ("w_proj_conv", "w_proj_attn", "w_out", "w_mlp_in") for s in columns(name, 0, w(name).shape[1])]
        n_before_mlp = len(in1_chunks) + proj_chunks + DT // 2

        def ada_after(n):
            return n % 2 == 1 and (n < 6 * ADA_CHUNKS or n_before_mlp <= n < n_before_mlp + 2 * ADA_CHUNKS)

        ada_at, sum_after = {}, {}
        for n in range(len(in1_chunks) + len(later)):
            if ada_after(n):
                v, r = ada_at[n] = ada_later[len(ada_at)]
                if r == ADA_CHUNKS - 1:
                    sum_after[v] = n
        for n, s in enumerate([c[2] for c in in1_chunks] + later):
            stream.add(s)
            if ada_after(n):
                stream.add(ada_chunk(*next(ada_plan)), use=modulation(*ada_at[n]))
        assert next(ada_plan, None) is None
        for s in columns("w_mlp_out", 0, D):
            stream.add(s)
        in2 = {}
        at = 0
        for name, width in (("cu", CH2), ("cv", CH2), ("q", QH * HD), ("kc", KVW), ("vc", KVW), ("ks", KVW),
                            ("vs", KVW), ("kw", KVW), ("vw", KVW), ("g", 3 * QH)):
            in2[name] = (at, width)
            at += width
        in2_order = ("cu", "cv", "q0", "ks", "kw", "g", "vs", "vw", "q1", "kc", "w1k0", "w1k1",
                     "q2", "vc", "w1v0", "w1v1")
        FIRST_HEAD_AFTER = in2_order.index("g")
        assert QH * HD == 3 * CHUNK_COLS
        for name in in2_order:
            if name.startswith("w1"):
                flat_w1 = w(f"cmp_{name[2]}_w1_2").rearrange("l d h -> (l d) h")
                half = int(name[3])
                stream.add(flat_w1[half * CHUNK_TILES * P:(half + 1) * CHUNK_TILES * P, :], split=False)
            elif name in in2:
                for s in columns("w_in_2", *in2[name]):
                    stream.add(s)
            else:
                for s in columns("w_in_2", in2["q"][0] + int(name[1]) * CHUNK_COLS, CHUNK_COLS):
                    stream.add(s)
        for s in columns("w_out_2", 0, D):
            stream.add(s)
        for c in range(0, FF2, CHUNK_COLS):
            for base in (0, FF2):
                for s in columns("w_gate_up_2", base + c, CHUNK_COLS):
                    stream.add(s)
        for s in columns("w_down_2", 0, D):
            stream.add(s)

        rows_sem = [sem(f"rows{i}_landed") for i in range(3)]
        x_sem, w2_sem, out_sem = sem("x_landed"), sem("w2_landed"), sem("stored")
        x_nat = wide[0]
        x_nat_v = x_nat[:].rearrange("p k t -> p (k t)").rearrange("p (t d) -> p t d", t=TT)
        def load_rows(group):
            n = len(rows[group])
            for at, source in rows[group]:
                ticket = q.load("act" if group else "sp", row_tile[group // 2][at:at + source.shape[0], :], source,
                                rows_sem[group], 16 * n)
            return ticket

        rows_landed = [load_rows(0)]
        x_landed = q.load("act", x_nat_v, a["x"][0].rearrange("(t p) d -> p t d", p=P), x_sem, 16)
        rows_landed += [load_rows(1), load_rows(2)]
        t = q.memset(ident[:], 0.0, engine="pool")
        ident_ready = q.put("pool", lambda e: e.affine_select(
            out=ident[:], in_=ident[:], compare_op=ALU.not_equal, fill=1.0, base=0,
            pattern=[[-1, P]], channel_multiplier=1), t)
        ones_ready = q.memset(ones[:], 1.0)
        eps_ready = q.memset(eps[:], EPS)

        t = q.memset(scan_mask[:], 0.0, engine="pool")
        q.put("pool", lambda e: e.affine_select(
            out=scan_mask[:, 0:P], in_=scan_mask[:, 0:P], compare_op=ALU.is_gt, fill=1.0, base=0,
            pattern=[[-1, P]], channel_multiplier=1), t)
        scan_mask_ready = q.put("pool", lambda e: e.affine_select(
            out=scan_mask[:, P:], in_=scan_mask[:, P:], compare_op=ALU.is_gt, fill=1.0, base=P,
            pattern=[[-1, 2 * P]], channel_multiplier=1), t)
        t = q.memset(mask_T[:], 1.0, engine="pool")
        for b in (0, 2):
            mask_T_ready = q.put("pool", lambda e, m=mask_T[:, b * P:(b + 1) * P]: e.affine_select(
                out=m, in_=m, compare_op=ALU.is_gt, fill=0.0, base=0,
                pattern=[[1, P]], channel_multiplier=-1), t)

        main_ring = [0, 1, 2]
        ring_pos = [0]

        def next_bank():
            ring_pos[0] += 1
            return main_ring[ring_pos[0] % len(main_ring)]

        def passes(n, b, act, k, start, stop, tokens_first=False, k0=0):
            hi, lo, t_hi, t_lo, _, _ = stream.parts[n]
            kt, n_cols = hi.shape[1], hi.shape[2]
            first, ticket = start and k == 0, None
            last_m = (TT if tokens_first else n_cols // P) - 1
            for m in range(last_m + 1):
                for wp, ap, t_w in ((hi, act.hi, t_hi), (hi, act.lo, t_hi), (lo, act.hi, t_lo)):
                    if tokens_first:
                        dst = bank[b][:, m * n_cols:(m + 1) * n_cols]
                        lhs, rhs = ap[:, k0 + k, m * P:(m + 1) * P], wp[:, k, :]
                    else:
                        dst = bank[b][:, m * T:(m + 1) * T]
                        lhs, rhs = wp[:, k, m * P:(m + 1) * P], ap[:, k0 + k, :]
                    ticket = q.matmul(dst, lhs, rhs, first, stop and k == kt - 1 and wp is lo,
                                      [t_w, act.ready[k0 + k], bank_readers[b] if first else None],
                                      signal=(k == kt - 1 and m == last_m and wp is lo))
                    first = False
            return ticket

        def product(b, act, k0=0, start=True, stop=True, tokens_first=False, last=False):
            n = stream.next()
            for k in range(stream.parts[n][0].shape[1]):
                ticket = passes(n, b, act, k, start, stop, tokens_first, k0)
            stream.done(n, ticket)
            flush_sums(keep=2)
            if not last:
                stream.ahead(high_only=True)
            return ticket

        def two_products(b0, b1, act):
            n0, n1 = stream.next(), stream.next()
            for k in range(DT):
                t0 = passes(n0, b0, act, k, True, True)
                t1 = passes(n1, b1, act, k, True, True)
            stream.done(n0, t0)
            stream.done(n1, t1)
            flush_sums()
            return [t0, t1]

        def each_product(n, act):
            b0, b1 = next_bank(), next_bank()
            t0, t1 = act_free[0] = two_products(b0, b1, act)
            stream.ahead()
            yield 0, b0, t0
            yield 1, b1, t1
            for i in range(2, n):
                b = next_bank()
                t = act_free[0] = product(b, act, last=(i == n - 1))
                yield i, b, t

        def modulation_sum(v, later=False):
            b, acc = next_bank(), mod_acc[v % 2]
            for k in range(DT):
                t = q.matmul(bank[b][:, k:k + 1], acc[:, k * P:(k + 1) * P], ones[:, 0:1], True, True,
                             [mod_chunk[v], ones_ready, bank_readers[b]], signal=(k == DT - 1))
            mod_acc_readers[v % 2], mod_acc_busy[v % 2] = t, False

            def evacuate():
                mod_vector[v] = bank_readers[b] = q.tt(mod[:, v * DT:(v + 1) * DT], bank[b][:, 0:DT],
                                                       cols("b_ada", v * DT, DT), ALU.add, [t, cols_ready])
                return mod_vector[v]

            return evacuate if later else evacuate()

        chunks_done = [0]
        mod_vector = {}

        def between():
            for v, n in sum_after.items():
                if n == chunks_done[0] and v not in (SHIFT2, SCALE2):
                    modulation_sum(v)
            chunks_done[0] += 1

        def split_tiles(act, k, n, source, ready, free=None):
            t_hi = q.act(act.hi[:, k:k + n, :], source, ACT.Copy, [ready, free])
            t_lo = q.tt(act.lo[:, k:k + n, :], source, act.hi[:, k:k + n, :].bitcast(F32),
                        ALU.subtract, [t_hi, ready, free])
            for i in range(k, k + n):
                act.ready[i] = [t_hi, t_lo]
            return [t_hi, t_lo]

        squares = wide[2]

        pending_sums = []
        sums_done = [None]

        def flush_sums(keep=0):
            while len(pending_sums) > keep:
                pending_sums.pop(0)()

        def norm_begin(k, n, source, ready, free=None, last=DT - 1, pair_add=None):
            t_squares = t = q.act(squares[:, k:k + n, :], source, ACT.Square, [ready, free])
            if pair_add:
                t = q.tt(squares[:, k, :], squares[:, k, :], squares[:, k + 1, :], ALU.add, t, engine=pair_add)

            def sum_():
                for i in range(k, k + (1 if pair_add else n)):
                    final = i == last or (pair_add is not None and k + 1 == last)
                    sums_done[0] = q.matmul(bank[SUMS][:, 0:T], ones[:], squares[:, i, :], i == 0, final,
                                            [t, ones_ready, bank_readers[SUMS] if i == 0 else None], signal=True)

            pending_sums.append(sum_)
            return t_squares

        def norm_end(width, free=None, out_=rstd[:]):
            flush_sums()
            t = q.act(rms[:], bank[SUMS][:, 0:T], ACT.Sqrt, [sums_done[0], eps_ready, free],
                      scale=1.0 / width, bias=eps[:, 0:1])
            bank_readers[SUMS] = t
            return q.recip(out_, rms[:], [t, free])

        preloaded = [None]

        def preload(func):
            preloaded[0] = q.act(scratch1[:], eps[:], func, [eps_ready, preloaded[0]])

        act = Split(act_hi, act_lo, DT)
        act_free = [None]

        y = wide[1]
        scaled = [None] * DT

        def scale_tile(k, scale, waits):
            scaled[k] = q.stt(y[:, k, :], x_T[:, k, :], scale[:, k:k + 1], rstd[:], ALU.mult, ALU.mult, waits)

        def shift_tile_high(k, shift, shift_ready):
            act.ready[k] = [q.act(act.hi[:, k, :], y[:, k, :], ACT.Identity, [scaled[k], shift_ready, act_free[0]],
                                  bias=shift[:, k:k + 1])]

        def shift_tile_low(k, shift, shift_ready):
            act.ready[k].append(q.stt(act.lo[:, k, :], y[:, k, :], shift[:, k:k + 1], act.hi[:, k, :].bitcast(F32),
                                      ALU.add, ALU.subtract, [act.ready[k], scaled[k], shift_ready, act_free[0]]))

        def scaled_parts(act, k, n, gain, ready, free):
            for i in range(k, k + n):
                t_hi = q.act(act.hi[:, i, :], x_T[:, i, :], ACT.Copy, [ready, cols_ready, free],
                             scale=gain[:, i:i + 1])
                act.ready[i] = [t_hi, q.stt(act.lo[:, i, :], x_T[:, i, :], gain[:, i:i + 1],
                                            act.hi[:, i, :].bitcast(F32), ALU.mult, ALU.subtract,
                                            [t_hi, ready, cols_ready, free])]

        rstd_2 = rstd[:].rearrange("p (o t) -> p o t", o=1).to_broadcast([P, 2, T])

        def transpose_rows(group):
            b = next_bank()
            at, n = rows[group][0][0], sum(s.shape[0] for _, s in rows[group])
            t = q.transpose(bank[b][:, 0:n], row_tile[group // 2][at:at + n, :], ident[at:at + n, at:at + n],
                            [rows_landed[group], ident_ready, bank_readers[b]], signal=True)
            bank_readers[b] = q.copy(col_tile[group // 2][:, at:at + n], bank[b][:, 0:n], t)
            return bank_readers[b]

        cols_ready = transpose_rows(0)
        stream.ahead(2)

        x_ready = [None] * DT
        for k in range(0, DT, 2):
            b = next_bank()
            for j in range(2):
                for tt_ in range(TT):
                    t = q.transpose(bank[b][:, j * T + tt_ * P:j * T + (tt_ + 1) * P],
                                    x_nat_v[:, tt_, (k + j) * P:(k + j + 1) * P], ident[:],
                                    [x_landed, ident_ready, bank_readers[b]], signal=(j + tt_ == 2))
            src = bank[b][:].rearrange("p (k t) -> p k t", k=2)
            t2 = x_ready[k] = x_ready[k + 1] = q.act(x_T[:, k:k + 2, :], src, ACT.Copy, t)
            bank_readers[b] = [t2, norm_begin(k, 2, src, t)]

        stream.ahead(ADA_CHUNKS)
        rstd_ready = norm_end(D)
        stream.ahead(ADA_CHUNKS + 2)
        t = modulation_sum(SCALE1)
        t = q.ts(scale1[:], mod[:, DT:2 * DT], 1.0, ALU.add, waits=t)
        scale1_ready = q.tt(scale1[:], scale1[:], cols("g_pre_mix", 0, DT), ALU.mult, t)
        for k in range(DT):
            t = q.act(y[:, k, :], x_T[:, k, :], ACT.Copy, [x_ready[k], scale1_ready], scale=scale1[:, k:k + 1])
            scaled[k] = q.tt(y[:, k, :], y[:, k, :], rstd[:], ALU.mult, [t, rstd_ready], engine="pool")
        stream.ahead(2 * ADA_CHUNKS)
        cols_ready = [cols_ready, transpose_rows(1)]
        cols1_ready = transpose_rows(2)
        stream.ahead(2 * ADA_CHUNKS + 1)
        t_shift = modulation_sum(SHIFT1)
        for k in range(DT):
            shift_tile_high(k, mod[:, 0:DT], t_shift)
            shift_tile_low(k, mod[:, 0:DT], t_shift)
        preload(ACT.Sigmoid)

        for dst, name in ((w2k, "cmp_k_w2_2"), (w2v, "cmp_v_w2_2")):
            w2_landed = q.load("act", dst[:], w(name).rearrange("(m p) d -> p m d", p=P), w2_sem, 32)

        with mixer1 as phase:
            qk_T = [alloc(phase, f"{n}_T", [P, HEADS // 2, T]) for n in "qk"]
            v_nat = alloc(phase, "v_nat", [P, TT, ATTN])
            c_gate = alloc(phase, "c_gate", [P, CT, T])
            b_gate = alloc(phase, "b_gate", [P, CT, T])
            padded = alloc(phase, "padded", [P, CT, T + 2])
            conv_y = alloc(phase, "conv_y", [P, CT, T])
            mixed = Split(alloc(phase, "mixed_hi", [P, CT, T], F32R), alloc(phase, "mixed_lo", [P, CT, T], F32R), CT)
            heads_o = Split(alloc(phase, "heads_hi", [P, HEADS // 2, T], F32R),
                            alloc(phase, "heads_lo", [P, HEADS // 2, T], F32R), HEADS // 2)
            beta = [alloc(phase, f"beta{i}", [P, 3 * P]) for i in range(2)]
            nbeta = [alloc(phase, f"nbeta{i}", [P, 3 * P]) for i in range(2)]
            remain = [alloc(phase, f"remain{i}", [P, 3 * P + 2]) for i in range(2)]
            weight = [alloc(phase, f"weight{i}", [P, 3 * P]) for i in range(2)]
            weight_T = [alloc(phase, f"weight_T{i}", [P, 3 * P]) for i in range(2)]
            gates = [wide[0], wide[1]]

            ends_ready = []
            for r in remain:
                ends_ready.append(q.memset(r[:, P:P + 1], 1.0))
                ends_ready.append(q.memset(r[:, 3 * P + 1:3 * P + 2], 1.0))
            pad_ready = q.memset(padded[:, :, 0:2], 0.0)

            S_BANKS, T_BANK, O_BANK = (4, 5), 6, 7
            head = {}

            def stick_scores(h):
                b, base, tile = S_BANKS[h % 2], h % 2 * HD, h // 2
                qh, kh = (m[base:base + HD, tile, :] for m in qk_T)
                q.matmul(bank[b][:, 0:P], qh[:, 0:P], kh[:, 0:P], True, True, [qk_ready, bank_readers[b]])
                t = q.matmul(bank[b][:, P:3 * P], qh[:, P:T], kh, True, True, signal=True)
                free = head.get(h - 2)
                t1 = q.act(beta[h % 2][:], bank[b][:, 0:3 * P], ACT.Sigmoid, [t, free], scale=INV_SQRT)
                t2 = q.act(nbeta[h % 2][:], bank[b][:, 0:3 * P], ACT.Sigmoid, [t, free], scale=-INV_SQRT)
                bank_readers[b] = t2
                r, nb = remain[h % 2], nbeta[h % 2]
                ts_ = []
                for lo_, hi_, off in ((0, P, 0), (P, 3 * P, 1)):
                    ts_.append(q.scan(r[:, lo_ + off:hi_ + off][:, ::-1], nb[:, lo_:hi_][:, ::-1],
                                      scan_mask[:, lo_:hi_][:, ::-1], 1.0, ALU.mult, ALU.max,
                                      [t2, scan_mask_ready, ends_ready, free]))
                for lo_, hi_, off in ((0, P, 1), (P, 3 * P, 2)):
                    t = q.tt(weight[h % 2][:, lo_:hi_], beta[h % 2][:, lo_:hi_],
                             r[:, lo_ + off:hi_ + off], ALU.mult, [ts_, t1, free], engine="pool")
                return t

            def stick_transpose(h, weight_ready):
                blocks = [weight[h % 2][:, i * P:(i + 1) * P] for i in range(3)]
                for i in range(3):
                    t = q.transpose(bank[T_BANK][:, i * P:(i + 1) * P], blocks[i], ident[:],
                                    [weight_ready, bank_readers[T_BANK]], signal=(i == 2))
                head[h] = t
                t = q.tt(weight_T[h % 2][:], bank[T_BANK][:, 0:3 * P], mask_T[:], ALU.mult,
                         [t, mask_T_ready, head.get(("o", h - 2))])
                bank_readers[T_BANK] = t
                return t

            def stick_output(h, ready):
                base = h % 2 * HD
                o = bank[O_BANK][base:base + HD, :]
                q.matmul(o[:, 0:T], v_nat[:, 0, h * HD:(h + 1) * HD], weight_T[h % 2][:, 0:T], True, False,
                         [ready, v_ready, bank_readers[O_BANK]])
                t = q.matmul(o[:, P:T], v_nat[:, 1, h * HD:(h + 1) * HD], weight_T[h % 2][:, 2 * P:3 * P],
                             False, True, signal=True)
                head[("o", h)] = t
                if h % 2:
                    bank_readers[O_BANK] = split_tiles(heads_o, h // 2, 1, bank[O_BANK][:, 0:T].rearrange(
                        "p (k t) -> p k t", k=1), t)

            def short_conv():
                for j in range(CT):
                    t = q.ts(conv_y[:, j, :], padded[:, j, 0:T], cols("conv_w", j, 1), ALU.mult,
                             waits=[u_ready, pad_ready])
                    for k in (1, 2):
                        t = q.stt(conv_y[:, j, :], padded[:, j, k:k + T], cols("conv_w", k * CT + j, 1),
                                  conv_y[:, j, :], ALU.mult, ALU.add, t)
                    yield
                    t = q.tt(conv_y[:, j, :], conv_y[:, j, :], b_gate[:, j, :], ALU.mult, [t, b_ready])
                    if j % 2:
                        split_tiles(mixed, j - 1, 2, conv_y[:, j - 1:j + 1, :], t)
                        yield

            weights_of, attending, step = {}, False, 0
            conv_steps = short_conv()
            b_ready = c_ready = u_ready = qk_ready = v_ready = None
            stick_T = {}
            for n, (name, i, _) in enumerate(in1_chunks):
                if attending and step < HEADS + 2:
                    if step < HEADS:
                        weights_of[step] = stick_scores(step)
                    if 1 <= step <= HEADS:
                        stick_T[step - 1] = stick_transpose(step - 1, weights_of[step - 1])
                    if step >= 2:
                        stick_output(step - 2, stick_T[step - 2])
                    step += 1
                b = next_bank()
                t = product(b, act, tokens_first=(name == "v"))
                act_free[0] = t
                src = bank[b][:].rearrange("p (k t) -> p k t", k=2)
                s2 = slice(2 * i, 2 * i + 2)
                if name in "qk":
                    t = q.copy(qk_T["qk".index(name)][:, s2, :], src, t)
                    qk_ready = t
                elif name == "v":
                    t = q.copy(v_nat[:, :, i * CHUNK_COLS:(i + 1) * CHUNK_COLS], src, t)
                    v_ready = t
                    attending = i == 1
                elif name == "c":
                    t = c_ready = q.act(c_gate[:, s2, :], src, ACT.Copy, t)
                elif name == "u":
                    t = u_ready = q.tt(padded[:, s2, 2:], src, c_gate[:, s2, :], ALU.mult, [t, c_ready])
                elif name == "b":
                    t = b_ready = q.act(b_gate[:, s2, :], src, ACT.Copy, t)
                else:
                    t = gates_ready = q.act(gates["ga gb".split().index(name)][:, s2, :], src, ACT.Sigmoid,
                                            [t, act.ready[DT - 1]])
                bank_readers[b] = t
                between()
                if name[0] == "g":
                    next(conv_steps, None)
            assert step == HEADS + 2 and next(conv_steps, None) is None
            preload(ACT.Sqrt)
            conv_part = wide[2]
            for i in range(DT // 2):
                b = next_bank()
                t = product(b, mixed)
                s2 = slice(2 * i, 2 * i + 2)
                conv_part_ready = bank_readers[b] = q.tt(
                    conv_part[:, s2, :], bank[b][:].rearrange("p (k t) -> p k t", k=2), gates[0][:, s2, :],
                    ALU.mult, [t, gates_ready])
                between()
            for i in range(DT // 2):
                b = next_bank()
                t = product(b, heads_o, last=True)
                s2 = slice(2 * i, 2 * i + 2)
                t = bank_readers[b] = q.tt(gates[1][:, s2, :], bank[b][:].rearrange("p (k t) -> p k t", k=2),
                                           gates[1][:, s2, :], ALU.mult, [t, gates_ready])
                stream.ahead()
                t = q.tt(gates[1][:, s2, :], gates[1][:, s2, :], conv_part[:, s2, :], ALU.add,
                         [t, conv_part_ready], engine="pool" if i < DT // 2 - 1 else "dve")
                merged_ready = split_tiles(act, 2 * i, 2, gates[1][:, s2, :], t, act_free[0])
                between()
            mod_ready = q.tt(gain1[:], mod[:, GATE1 * DT:(GATE1 + 1) * DT], cols("g_post_mix", 0, DT), ALU.mult,
                             [mod_vector[GATE1], cols_ready])

        ON_POOL = (1, 3, 5)

        def residual_norm(source, rstd_ready, then=None):
            product_ready, ready = {}, [None] * DT

            def add(k):
                ready[k] = q.tt(x_T[:, k, :], x_T[:, k, :], source[:, k, :], ALU.add, product_ready[k],
                                engine="pool" if k in ON_POOL else "dve")

            order = [k for k in range(DT) if k not in ON_POOL]
            for k in ON_POOL:
                product_ready[k] = q.tt(source[:, k, :], source[:, k, :], rstd[:], ALU.mult, rstd_ready, engine="pool")
                add(k)
            added = 0
            for n, k in enumerate(order + [None]):
                if k is not None:
                    product_ready[k] = q.tt(source[:, k, :], source[:, k, :], rstd[:], ALU.mult, rstd_ready)
                if n:
                    add(order[n - 1])
                while added < DT and ready[added] and ready[added + 1]:
                    if then:
                        then(added, ready[added:added + 2])
                    norm_begin(added, 2, x_T[:, added:added + 2, :], ready[added:added + 2], rstd_ready)
                    added += 2
            return ready

        def branch_tiles(branch, i, b, t, gain, gain_ready, free=None):
            src = bank[b][:].rearrange("p (k t) -> p k t", k=2)
            norm_begin(2 * i, 2, src, t, free, pair_add="dve" if i < DT // 2 - 1 else None)
            for j in range(2):
                bank_readers[b] = q.act(branch[:, 2 * i + j, :], src[:, j, :], ACT.Copy, [t, free, gain_ready],
                                        scale=gain[:, 2 * i + j:2 * i + j + 1])
            return bank_readers[b]

        branch = wide[0]
        main_ring[:] = [b for b in range(8) if b != SUMS]
        for i, b, t in each_product(DT // 2, act):
            branch_ready = branch_tiles(branch, i, b, t, gain1, mod_ready, merged_ready)
            between()
        rstd_ready = norm_end(D)
        finish = [modulation_sum(v, later=True) for v in (SHIFT2, SCALE2)]
        x_ready = residual_norm(branch, [rstd_ready, branch_ready])
        mod_ready = [f() for f in finish]
        t = q.ts(scale2[:], mod[:, SCALE2 * DT:(SCALE2 + 1) * DT], 1.0, ALU.add, waits=mod_ready)
        mod_ready.append(q.tt(scale2[:], scale2[:], cols("g_pre_mlp", 0, DT), ALU.mult, [t, cols_ready]))
        rstd_ready = norm_end(D, x_ready)
        shift2 = mod[:, SHIFT2 * DT:(SHIFT2 + 1) * DT]
        for k in range(DT + 2):
            if k < DT:
                scale_tile(k, scale2, [rstd_ready, x_ready[k], mod_ready])
                shift_tile_high(k, shift2, mod_ready)
            if k >= 2:
                shift_tile_low(k - 2, shift2, mod_ready)

        def accumulate_tiles(source, n_tiles, evacuate):
            for i in range(DT // 2):
                b = next_bank()
                for r in range(0, n_tiles, CHUNK_TILES):
                    t = product(b, source, k0=r, start=(r == 0), stop=(r + CHUNK_TILES >= n_tiles),
                                last=(i == DT // 2 - 1 and r + CHUNK_TILES >= n_tiles))
                evacuate(i, b, t)
            return t

        with ExitStack() as phase:
            FT = FF // P
            hidden = Split(alloc(phase, "hidden_hi", [P, FT, T], F32R), alloc(phase, "hidden_lo", [P, FT, T], F32R), FT)
            relu = [wide[0][:, 2 * i:2 * i + 2, :] for i in range(4)]
            relu_free = [x_ready[DT - 1]] * 4
            for i, b, t in each_product(FT // 2, act):
                stream.ahead()
                r = relu[i % 4]
                t = bank_readers[b] = q.act(r, bank[b][:].rearrange("p (k t) -> p k t", k=2), ACT.Relu,
                                            [t, relu_free[i % 4]])
                t = q.tt(r, r, r, ALU.mult, t)
                relu_free[i % 4] = split_tiles(hidden, 2 * i, 2, r, t)
                between()
            mod_ready = q.tt(gain2[:], mod[:, GATE2 * DT:], cols("g_post_mlp", 0, DT), ALU.mult, mod_vector[GATE2])
            branch, branch_ready = wide[1], [None]

            def evacuate(i, b, t):
                branch_ready[0] = branch_tiles(branch, i, b, t, gain2, mod_ready, act_free[0])

            mlp_done = accumulate_tiles(hidden, FT, evacuate)
        rstd_ready = norm_end(D)

        def attn_parts(k, ready):
            scaled_parts(act, k, 2, cols("attn_norm_2", 0, DT), ready, act_free[0])

        x_ready = residual_norm(branch, [rstd_ready, branch_ready[0]], then=attn_parts)

        with ExitStack() as phase:
            CT2 = CH2 // P
            PAD = TAPS2 - 1
            q2 = alloc(phase, "q2", [HD, QH, T])
            keys = {n: alloc(phase, n + "_T", [HD, KV, T]) for n in ("ks", "kw")}
            vals = {n: alloc(phase, n + "_nat", [P, TT, KVW]) for n in ("vs", "vw")}
            gate = alloc(phase, "gate", [P, TT, 3 * QH])
            bias = alloc(phase, "bias", [P, QH, 3 * P])
            dist_i = alloc(phase, "dist_i", [P, 3 * P], I32)
            dist = mod_acc[0][:, 0:3 * P]
            far = mod_acc[0][:, 3 * P:6 * P]
            bias_c = alloc(phase, "bias_c", [P, TT, QH, N_CMP])
            dist_ci = alloc(phase, "dist_ci", [P, TT, N_CMP], I32)
            dist_c = alloc(phase, "dist_c", [P, TT, N_CMP])
            far_c = alloc(phase, "far_c", [P, TT, N_CMP])
            cmp_in = alloc(phase, "cmp_in", [P, CMP_LEN // 4, KV + 1, N_CHUNKS])
            cmp_hid = alloc(phase, "cmp_hid", [P, 2, KV * N_CMP])
            cmp_pe = alloc(phase, "cmp_pe", [P, 2])
            C_HEADS = QH // 2
            C_ROWS = C_HEADS * N_CMP
            repeat = mod_acc[0][0:N_CMP, 6 * P:6 * P + C_ROWS]
            KC_AT = (C_HEADS - 1) * N_CMP
            kc_wide = mod_acc[1][0:HD, 0:KV * (2 * KC_AT + N_CMP)].rearrange("p (g c) -> p g c", g=KV)
            own_rows = alloc(phase, "own_rows", [C_ROWS, C_HEADS])
            vc_own = alloc(phase, "vc_own", [C_ROWS, QH, HD])
            score_c = alloc(phase, "score_c", [P, TT * QH, N_CMP])
            stat_c = alloc(phase, "stat_c", [P, TT * QH])
            free = mlp_done

            conv_u = wide[0][:, 0:CT2, :]
            conv_s = wide[0][:, CT2:2 * CT2, :]
            conv_acc = wide[0][:, 4:4 + CT2, :]
            conv_tmp = wide[0][:, 6:6 + CT2, :]
            conv_pad = wide[1][:].rearrange("p k t -> p (k t)")[:, 0:CT2 * (T + PAD)].rearrange(
                "p (k t) -> p k t", k=CT2)
            cmp_raw = wide[2][:, 0:2, :]
            heads_o2 = [wide[0][:, i, :] for i in range(4)] + [wide[1][:, 3 + i, :] for i in range(QH // 2 - 4)]
            pc_T = wide[1][0:C_ROWS, 5:7, :]
            N_WINDOWS = (KV + 1) * N_CHUNKS - 1
            cmp_out = wide[1][0:N_WINDOWS, 7, :]
            vc_nat = wide[1][0:N_CMP, 7, :]
            mean = conv_tmp[:, 0, :]
            t = q.put("pool", lambda e: e.iota(dist_i[:, 0:P], pattern=[[-1, P]], base=0,
                                               channel_multiplier=1), free)
            t = q.put("pool", lambda e: e.iota(dist_i[:, P:], pattern=[[-1, 2 * P]], base=P,
                                               channel_multiplier=1), free)
            dist_ready = q.copy(dist[:], dist_i[:], [t, free])
            t = q.memset(far[:], 0.0, free, engine="pool")
            q.put("pool", lambda e: e.affine_select(
                out=far[:, 0:P], in_=far[:, 0:P], compare_op=ALU.is_ge, fill=MASKED, base=0,
                pattern=[[-1, P]], channel_multiplier=1), t)
            far_ready = q.put("pool", lambda e: e.affine_select(
                out=far[:, P:], in_=far[:, P:], compare_op=ALU.is_ge, fill=MASKED, base=P,
                pattern=[[-1, 2 * P]], channel_multiplier=1), t)
            t = q.put("pool", lambda e: e.iota(dist_ci[:], pattern=[[P, TT], [-STRIDE, N_CMP]], base=0,
                                               channel_multiplier=1), free)
            dist_c_ready = q.ts(dist_c[:], dist_ci[:], -0.5 * (CMP_LEN - 1), ALU.add, waits=[t, free])
            t = q.memset(far_c[:], 0.0, free, engine="pool")
            far_c_ready = q.put("pool", lambda e: e.affine_select(
                out=far_c[:], in_=far_c[:], compare_op=ALU.is_ge, fill=MASKED, base=-(CMP_LEN - 1),
                pattern=[[P, TT], [-STRIDE, N_CMP]], channel_multiplier=1), t)
            t = q.memset(own_rows[:], 1.0, free, engine="pool")
            t = q.put("pool", lambda e: e.affine_select(
                out=own_rows[:], in_=own_rows[:], compare_op=ALU.is_ge, fill=0.0, base=0,
                pattern=[[-N_CMP, C_HEADS]], channel_multiplier=1), t)
            own_ready = q.put("pool", lambda e: e.affine_select(
                out=own_rows[:], in_=own_rows[:], compare_op=ALU.is_ge, fill=0.0, base=N_CMP - 1,
                pattern=[[N_CMP, C_HEADS]], channel_multiplier=-1), t)
            t = q.memset(repeat, 0.0, free, engine="pool")
            repeat_ready = q.put("pool", lambda e: e.affine_select(
                out=repeat, in_=repeat, compare_op=ALU.not_equal, fill=1.0, base=0,
                pattern=[[0, C_HEADS], [-1, N_CMP]], channel_multiplier=1), t)
            kc_zeros = q.memset(kc_wide, 0.0, free, engine="pool")
            cmp_zeros = q.memset(cmp_in[:, :, KV, :], 0.0, free, engine="pool")
            pad2_ready = q.memset(conv_pad[:, :, 0:PAD], 0.0, act.ready[DT - 1], engine="pool")

            ready = {}
            conv_done = [None] * CT2

            def mixer_conv(j):
                eng = "pool" if j == 0 else "dve"
                t = q.ts(conv_acc[:, j, :], conv_pad[:, j, 0:T], cols("conv_w_2", j, 1), ALU.mult,
                         cols("conv_b_2", j, 1), ALU.add, waits=[ready["pad"], pad2_ready, cols1_ready], engine=eng)
                for k in range(1, TAPS2):
                    yield
                    tap = cols("conv_w_2", k * CT2 + j, 1)
                    if eng == "dve":
                        t = q.stt(conv_acc[:, j, :], conv_pad[:, j, k:k + T], tap, conv_acc[:, j, :],
                                  ALU.mult, ALU.add, t)
                    else:
                        tmp = conv_tmp[:, k % 2, :]
                        tm = q.ts(tmp, conv_pad[:, j, k:k + T], tap, ALU.mult, waits=t if k > 2 else None, engine=eng)
                        t = q.tt(conv_acc[:, j, :], conv_acc[:, j, :], tmp, ALU.add, [t, tm], engine=eng)
                conv_done[j] = t

            def bias_tables():
                for h in range(QH):
                    ready["bias", h] = q.stt(bias[:, h, :], dist[:], -slopes[h], far[:], ALU.mult, ALU.add,
                                          [dist_ready, far_ready])
                    ready["bias_c"] = q.stt(bias_c[:, :, h, :], dist_c[:], -slopes[h], far_c[:], ALU.mult, ALU.add,
                                            [dist_c_ready, far_c_ready])
                    yield

            def pair_tokens(name):
                waits = [ready[name], cmp_zeros, ready.get("cmp_in_free")]
                out_ = []
                for g in range(KV):
                    src = cmp_raw[g % 2 * HD:(g % 2 + 1) * HD, g // 2, :].rearrange(
                        "p (c l two) -> p two l c", two=2, l=STRIDE // 2)
                    for par in range(2):
                        o = cmp_in[par * HD:(par + 1) * HD, :, g, :]
                        if par:
                            out_.append(q.act(o, src[:, par], ACT.Copy, waits))
                        else:
                            out_.append(q.copy(o, src[:, par], waits))
                ready["cmp_raw_free"] = list(out_)
                out_.append(q.copy(cmp_in[:, :, KV, 0:2], cols(f"cmp_{name[0]}_pe_2", 0, CMP_LEN // 2).rearrange(
                    "p (s l) -> p l s", s=2), [cols1_ready, waits]))
                ready["cmp_in"] = out_

            def compress(half):
                c = stream.next()
                src = stream.raw_view(c)
                dst = bank[SUMS][0:N_WINDOWS, 0:CMP_HID]
                for j in range(CHUNK_TILES):
                    first = half == 0 and j == 0
                    flat_in = cmp_in[:, j].rearrange("p g c -> p (g c)")
                    t = q.matmul(dst, flat_in[:, half:half + N_WINDOWS], src[:, j, :], first,
                                 half == 1 and j == CHUNK_TILES - 1,
                                 [stream.landed[c], ready["cmp_in"], bank_readers[SUMS] if first else None],
                                 signal=(j == CHUNK_TILES - 1))
                stream.done(c, t)
                if half == 1:
                    ready["cmp_in_free"] = t
                    ready["cmp_out"] = bank_readers[SUMS] = q.act(cmp_out, dst, ACT.Copy,
                                                                  [t, ready.get("cmp_out_free"), act.ready[DT - 1]])

            def cmp_hidden():
                b, rows_ = next_bank(), N_WINDOWS
                for m in range(2):
                    t = q.transpose(bank[b][:, m * P:m * P + rows_], cmp_out[:, m * P:(m + 1) * P],
                                    ident[0:rows_, 0:rows_], [ready["cmp_out"], bank_readers[b]], signal=(m == 1))
                ready["cmp_out_free"] = t
                src = bank[b][:, 0:2 * P].rearrange("p (m g c) -> p m g c", m=2, c=N_CHUNKS)
                tp = q.copy(cmp_pe[:], src[:, :, KV, 0], [t, ready.get("cmp_hid_free"), free])
                for m in range(2):
                    t = q.act(cmp_hid[:, m, :].rearrange("p (g n) -> p g n", g=KV), src[:, m, 0:KV, 0:N_CMP], ACT.Silu, tp, bias=cmp_pe[:, m:m + 1])
                ready["cmp_hid"] = bank_readers[b] = t
                preload(ACT.Exp)

            def cmp_keys():
                b = next_bank()
                for m in range(2):
                    t = q.matmul(bank[b][0:HD, 0:KV * N_CMP], w2k[:, m, :], cmp_hid[:, m, :], m == 0, m == 1,
                                 [ready["cmp_hid"], w2_landed, bank_readers[b]], signal=True)
                ready["cmp_hid_free"] = t
                ready["kc"] = bank_readers[b] = q.copy(
                    kc_wide[:, :, KC_AT:KC_AT + N_CMP], bank[b][0:HD, 0:KV * N_CMP].rearrange("p (g n) -> p g n", g=KV),
                    [t, kc_zeros])

            def cmp_values():
                b = next_bank()
                for g in range(KV):
                    for m in range(2):
                        t = q.matmul(bank[b][0:N_CMP, g * HD:(g + 1) * HD], cmp_hid[:, m, g * N_CMP:(g + 1) * N_CMP],
                                     w2v[:, m, :], m == 0, m == 1,
                                     [ready["cmp_hid"], w2_landed, bank_readers[b]], signal=True)
                t = bank_readers[b] = q.copy(vc_nat, bank[b][0:N_CMP, 0:KVW], [t, ready["cmp_out_free"]])
                b = next_bank()
                t = q.matmul(bank[b][0:C_ROWS, 0:KVW], repeat, vc_nat, True, True,
                                                    [t, repeat_ready, bank_readers[b]], signal=True)
                G = C_HEADS // PER_KV
                for part in range(2):
                    src = bank[b][0:C_ROWS, part * G * HD:(part + 1) * G * HD].rearrange("p (g o d) -> p g o d", g=G, o=1)
                    own = own_rows[:].rearrange("p (g h o) -> p g h o", g=G, o=1)
                    t2 = q.tt(vc_own[:, part * C_HEADS:(part + 1) * C_HEADS, :].rearrange("p (g h) d -> p g h d", g=G),
                              src.to_broadcast([C_ROWS, G, PER_KV, HD]), own.to_broadcast([C_ROWS, G, PER_KV, HD]),
                              ALU.mult, [t, own_ready])
                ready["vc"] = bank_readers[b] = t2

            def cmp_scores():
                b = next_bank()
                for h in range(QH):
                    at = KC_AT - h % C_HEADS * N_CMP
                    dst = bank[b][0:C_ROWS, h // C_HEADS * T:(h // C_HEADS + 1) * T]
                    t = q.matmul(dst, kc_wide[:, h // PER_KV, at:at + C_ROWS], q2[:, h, :], h == 0,
                                 h % C_HEADS == C_HEADS - 1, [ready["q2"], ready["kc"], bank_readers[b]],
                                 signal=(h == QH - 1))
                ready["c_products"] = bank_readers[b] = q.act(
                    pc_T, bank[b][0:C_ROWS, :].rearrange("p (k t) -> p k t", k=2), ACT.Copy, [t, act.ready[DT - 1]])

            def spread(v):
                return v.rearrange("p (h o) -> p h o", o=1).to_broadcast([P, QH * TT, N_CMP])

            def cmp_softmax():
                b = next_bank()
                for tt_ in range(TT):
                    for part in range(2):
                        c0 = (tt_ * 2 + part) * C_ROWS
                        t = q.transpose(bank[b][:, c0:c0 + C_ROWS], pc_T[:, part, tt_ * P:(tt_ + 1) * P],
                                        ident[0:C_ROWS, 0:C_ROWS], [ready["c_products"], bank_readers[b]],
                                        signal=(part + tt_ == 2))
                ready["pc_T_free"] = t
                n_c = QH * TT * N_CMP
                for tt_ in range(TT):
                    own = slice(tt_ * QH, (tt_ + 1) * QH)
                    t2 = q.stt(score_c[:, own, :], bank[b][:, 0:n_c].rearrange("p (h n) -> p h n", n=N_CMP)[:, own, :],
                               q_scale[:, tt_:tt_ + 1], bias_c[:, tt_], ALU.mult, ALU.add,
                               [t, ready["bias_c"], q_scale_ready, free])
                t = t2
                bank_readers[b] = t
                t = q.reduce(stat_c[:], score_c[:], ALU.max, t)
                t = q.ts(stat_c[:], stat_c[:], MASK_LIMIT, ALU.max, waits=t)
                t = q.tt(score_c[:], score_c[:], spread(stat_c[:]), ALU.subtract, t)
                t = q.act(score_c[:], score_c[:], ACT.Exp, t)
                ready["c_exps"] = t

            def cmp_normalise():
                t = q.reduce(stat_c[:], score_c[:], ALU.add, ready["c_exps"])
                t = q.ts(stat_c[:], stat_c[:], 1e-30, ALU.max, waits=t)
                t = q.recip(stat_c[:], stat_c[:], t)
                t = q.tt(stat_c[:].rearrange("p (t h) -> p t h", t=TT), stat_c[:].rearrange("p (t h) -> p t h", t=TT),
                         gate[:].rearrange("p t (h b) -> p t h b", b=3)[:, :, :, 0], ALU.mult, [t, ready["g"]])
                ready["p_c"] = q.tt(score_c[:], score_c[:], spread(stat_c[:]), ALU.mult, t)

            def cmp_turn():
                b = next_bank()
                for part in range(2):
                    for tt_ in range(TT):
                        h0 = tt_ * QH + part * C_HEADS
                        t = q.transpose(bank[b][0:C_ROWS, (part * TT + tt_) * P:(part * TT + tt_ + 1) * P],
                                        score_c[:, h0:h0 + C_HEADS, :].rearrange("p h n -> p (h n)"), ident[:],
                                        [ready["p_c"], bank_readers[b]], signal=(part + tt_ == 2))
                ready["pc_T"] = bank_readers[b] = q.act(
                    pc_T, bank[b][0:C_ROWS, :].rearrange("p (k t) -> p k t", k=2), ACT.Copy, [t, ready["pc_T_free"]])

            def conv_norm_begin():
                for j in range(CT2):
                    t = q.matmul(bank[SUMS][:, 0:T], ones[:], conv_acc[:, j, :], j == 0, j == CT2 - 1,
                                 [conv_done[j], bank_readers[SUMS]], signal=True)
                t = bank_readers[SUMS] = q.ts(mean, bank[SUMS][:, 0:T], 1.0 / CH2, ALU.mult,
                                              waits=[t, conv_done])
                for j in range(CT2):
                    t2 = q.tt(conv_acc[:, j, :], conv_acc[:, j, :], mean, ALU.subtract, [t, conv_done[j]])
                    norm_begin(j, 1, conv_acc[:, j:j + 1, :], t2, ready["cmp_raw_free"], last=CT2 - 1)
                ready["centred"] = t2

            def conv_norm_end():
                conv_rstd = conv_tmp[:, 1, :]
                t_rstd = norm_end(CH2, conv_done, conv_rstd)
                ready["conv_squares_free"] = sums_done[0]
                preload(ACT.Silu)
                for j in range(CT2):
                    z = conv_acc[:, j, :]
                    t = q.tt(z, z, conv_rstd, ALU.mult, [t_rstd, ready["centred"]])
                    t = q.ts(z, z, cols("conv_ln_g_2", j, 1), ALU.mult, cols("conv_ln_b_2", j, 1), ALU.add, waits=t)
                    ready["conv", j] = q.act(z, z, ACT.Silu, t)
                preload(ACT.Exp)

            def conv_parts():
                split_tiles(act, 0, CT2, conv_acc, [ready["conv", j] for j in range(CT2)], act_free[0])


            N_HEADS_IN_FLIGHT = 3
            exps = {}
            score = [alloc(phase, f"score{i}", [P, 3 * P]) for i in range(2 * N_HEADS_IN_FLIGHT)]
            prob_T = [wide[2][:].rearrange("p k t -> p (k t)")[:, 2 * T + i * 3 * P:2 * T + (i + 1) * 3 * P]
                      for i in range(4)]
            neg_max = [alloc(phase, f"neg_max{i}", [P, 4]) for i in range(N_HEADS_IN_FLIGHT)]
            total = [alloc(phase, f"total{i}", [P, 4]) for i in range(N_HEADS_IN_FLIGHT)]
            S2_BANKS, T2_BANKS, O2_BANK = (2, 4), (5, 6), 7
            BR = (("ks", "vs"), ("kw", "vw"))
            free_score, free_probs = {}, {}

            def softmax(h):
                g, par = h // PER_KV, h % N_HEADS_IN_FLIGHT
                ts_ = []
                for br, (kn, _) in enumerate(BR):
                    b, sc = S2_BANKS[br], score[2 * par + br]
                    q.matmul(bank[b][:, 0:P], q2[:, h, 0:P], keys[kn][:, g, 0:P], True, True,
                             [ready[f"q{h // 4}"], ready[kn], bank_readers[b]])
                    t = q.matmul(bank[b][:, P:3 * P], q2[:, h, P:T], keys[kn][:, g, :], True, True, signal=True)
                    for tt_, (lo_, hi_) in enumerate(((0, P), (P, 3 * P))):
                        t2 = q.stt(sc[:, lo_:hi_], bank[b][:, lo_:hi_], q_scale[:, tt_:tt_ + 1], bias[:, h, lo_:hi_],
                                   ALU.mult, ALU.add, [t, ready["bias", h], q_scale_ready,
                                                       free_score.get(h - N_HEADS_IN_FLIGHT)])
                    t = bank_readers[b] = t2
                    for i, (lo_, hi_) in enumerate(((0, P), (P, 3 * P))):
                        c = 2 * br + i
                        t2 = q.reduce(neg_max[par][:, c:c + 1], sc[:, lo_:hi_], ALU.max,
                                      [t, free_score.get(h - N_HEADS_IN_FLIGHT)], negate=True)
                        ts_.append(q.act(sc[:, lo_:hi_], sc[:, lo_:hi_], ACT.Exp, [t2, free_score.get(h - N_HEADS_IN_FLIGHT)],
                                         bias=neg_max[par][:, c:c + 1], accum=total[par][:, c:c + 1]))
                exps[h] = ts_

            def normalise(h):
                par = h % N_HEADS_IN_FLIGHT
                tot = total[par]
                t = q.ts(tot[:], tot[:], 1e-30, ALU.max, waits=exps[h])
                t = q.recip(tot[:], tot[:], t)
                t = q.tt(tot[:].rearrange("p (b t) -> p b t", t=TT), tot[:].rearrange("p (b t) -> p b t", t=TT),
                         gate[:, :, 3 * h + 1:3 * h + 3].rearrange("p t b -> p b t"), ALU.mult, [t, ready["g"]])
                out_ = []
                for br in range(2):
                    for i, (lo_, hi_) in enumerate(((0, P), (P, 3 * P))):
                        c = 2 * br + i
                        sc = score[2 * par + br]
                        if br and i:
                            out_.append(q.act(sc[:, lo_:hi_], sc[:, lo_:hi_], ACT.Copy, t, scale=tot[:, c:c + 1]))
                        else:
                            out_.append(q.ts(sc[:, lo_:hi_], sc[:, lo_:hi_], tot[:, c:c + 1], ALU.mult, waits=t))
                return out_

            def turn(h, probs_ready):
                par, two = h % N_HEADS_IN_FLIGHT, h % 2
                out_ = []
                for br in range(2):
                    b = T2_BANKS[br]
                    for i in range(3):
                        t = q.transpose(bank[b][:, i * P:(i + 1) * P], score[2 * par + br][:, i * P:(i + 1) * P],
                                        ident[:], [probs_ready, bank_readers[b]], signal=(i == 2))
                    bank_readers[b] = q.act(prob_T[2 * two + br][:], bank[b][:, 0:3 * P], ACT.Copy,
                                            [t, free_probs.get(h - 2)])
                    out_.append(bank_readers[b])
                free_score[h] = t
                return out_

            def attend(h, probs_T_ready):
                g, par, base = h // PER_KV, h % 2, h % 2 * HD
                o = bank[O2_BANK][base:base + HD, :]
                for br, (_, vn) in enumerate(BR):
                    p_T, v = prob_T[2 * par + br], vals[vn]
                    q.matmul(o[:, 0:T], v[:, 0, g * HD:(g + 1) * HD], p_T[:, 0:T], br == 0, False,
                             [ready[vn], probs_T_ready, bank_readers[O2_BANK]])
                    t = q.matmul(o[:, P:T], v[:, 1, g * HD:(g + 1) * HD], p_T[:, 2 * P:3 * P], False, br == 1,
                                 signal=True)
                free_probs[h] = t
                if par:
                    ready["o", h // 2] = bank_readers[O2_BANK] = q.act(
                        heads_o2[h // 2], bank[O2_BANK][:, 0:T], ACT.Copy, [t, ready["pad"], act.ready[DT - 1]])

            probs, probs_T = {}, {}

            def head_step(h):
                if 2 <= h <= QH + 1:
                    probs_T[h - 2] = turn(h - 2, probs[h - 2])
                if h < QH:
                    softmax(h)
                if 1 <= h <= QH:
                    probs[h - 1] = normalise(h - 1)
                if 3 <= h:
                    attend(h - 3, probs_T[h - 3])

            def chunk(name, b=None, t=None):
                if name.startswith("w1"):
                    compress(int(name[3]))
                    return
                if b is None:
                    b = next_bank()
                    t = act_free[0] = product(b, act, tokens_first=(name in ("vs", "vw", "g")))
                src = bank[b][:].rearrange("p (k t) -> p k t", k=2)
                t = [t, rstd_ready]
                if name == "cu":
                    t = ready["cu"] = q.tt(conv_u, src, rstd_2, ALU.mult, [t, x_ready])
                elif name == "cv":
                    t = q.tt(conv_s, src, rstd_2, ALU.mult, [t, x_ready])
                    bank_readers[b] = t
                    t = q.act(conv_s, conv_s, ACT.Sigmoid, t)
                    ready["pad"] = q.tt(conv_pad[:, :, PAD:], conv_u, conv_s, ALU.mult, [t, ready["cu"]])
                    work["dve"].append(mixer_conv(1))
                    work["pool"].append(mixer_conv(0))
                    return
                elif name in ("kc", "vc"):
                    t = ready[name] = q.tt(cmp_raw, src, rstd_2, ALU.mult,
                                      [t, ready.get("cmp_raw_free"), ready.get("conv_squares_free")])
                    pair_tokens(name)
                elif name[0] == "q":
                    for j in range(4):
                        s_ = bank[b][j % 2 * HD:(j % 2 + 1) * HD, j // 2 * T:(j // 2 + 1) * T]
                        t2 = q.act(q2[:, 4 * int(name[1]) + j, :], s_, ACT.Copy, [t[0], free])
                    t = ready[name] = t2
                elif name in ("ks", "kw"):
                    for g in range(KV):
                        s_ = bank[b][g % 2 * HD:(g % 2 + 1) * HD, g // 2 * T:(g // 2 + 1) * T]
                        t2 = q.tt(keys[name][:, g, :], s_, rstd[g % 2 * HD:(g % 2 + 1) * HD, :], ALU.mult, [t, free])
                    t = ready[name] = t2
                elif name in ("vs", "vw"):
                    for tt_ in range(TT):
                        t2 = q.act(vals[name][:, tt_, :], src[:, tt_, :], ACT.Copy, [t, rstd_col_ready, free],
                                   scale=rstd_col[:, tt_:tt_ + 1])
                    t = ready[name] = t2
                else:
                    for tt_ in range(TT):
                        t2 = q.act(gate[:, tt_, :], bank[b][:, tt_ * 3 * QH:(tt_ + 1) * 3 * QH], ACT.Sigmoid,
                                   [t, rstd_col_ready, free], scale=rstd_col[:, tt_:tt_ + 1])
                    t = ready["g"] = t2
                    preload(ACT.Exp)
                bank_readers[b] = t

            def cmp_output(i):
                b = next_bank()
                for h in (2 * i, 2 * i + 1):
                    base = h % 2 * HD
                    t = q.matmul(bank[b][base:base + HD, 0:T], vc_own[:, h, :], pc_T[:, h // C_HEADS, :], True, True,
                                 [ready["vc"], ready["pc_T"], bank_readers[b]], signal=True)
                t = bank_readers[b] = q.tt(heads_o2[i], heads_o2[i], bank[b][:, 0:T], ALU.add, [t, ready["o", i]])
                split_tiles(act, CT2 + i, 1, heads_o2[i].rearrange("p (k t) -> p k t", k=1), t, act_free[0])

            work = {"bias": [bias_tables()], "dve": [], "pool": []}

            def background(engine, n):
                while n and work[engine]:
                    try:
                        next(work[engine][0])
                        n -= 1
                    except StopIteration:
                        work[engine].pop(0)

            rstd_col = alloc(phase, "rstd_col", [P, TT])
            q_scale = alloc(phase, "q_scale", [P, TT])
            chunks = list(in2_order[FIRST_HEAD_AFTER + 1:])
            after_k, after_v = chunks.index("w1k1") + 1, chunks.index("w1v1") + 1
            stages = {after_k: [cmp_hidden, conv_norm_begin], after_k + 1: [cmp_keys, conv_norm_end],
                      after_k + 2: [cmp_scores, conv_parts], after_k + 3: [cmp_softmax], after_v: [cmp_normalise, cmp_hidden],
                      after_v + 1: [cmp_turn, cmp_values]}
            assert chunks.index("vc") < after_k + 3 and chunks.index("q2") < after_k + 2 and after_k + 3 < after_v
            for i in range(QH // 2 - 1):
                stages.setdefault(QH + i // 2, []).append(partial(cmp_output, i))
            b0, b1 = next_bank(), next_bank()
            t0, t1 = act_free[0] = two_products(b0, b1, act)
            rstd_ready = norm_end(D, x_ready)
            stream.ahead()
            background("bias", 1)
            preload(ACT.Sigmoid)
            chunk("cu", b0, t0)
            chunk("cv", b1, t1)
            assert in2_order[0:2] == ("cu", "cv")
            for name in in2_order[2:FIRST_HEAD_AFTER + 1]:
                background("bias", 1)
                background("dve", 2)
                background("pool", 2)
                chunk(name)
                if name == in2_order[2]:
                    b = next_bank()
                    for tt_ in range(TT):
                        t = q.transpose(bank[b][:, tt_ * P:(tt_ + 1) * P], rstd[:, tt_ * P:(tt_ + 1) * P], ident[:],
                                        [rstd_ready, bank_readers[b]], signal=(tt_ == TT - 1))
                    rstd_col_ready = bank_readers[b] = q.copy(
                        rstd_col[:], bank[b][:, 0:TT * P].rearrange("p (k t) -> p k t", k=TT)[:, :, 0], [t, free])
                    q_scale_ready = q.ts(q_scale[:], rstd_col[:], INV_SQRT, ALU.mult, waits=[rstd_col_ready, free])
            POOL_SPLITS_FROM = 8
            main_ring[:] = [0, 1]
            for h in range(QH + 3):
                head_step(h)
                if h == POOL_SPLITS_FROM:
                    stream.low_engine = "pool"
                background("bias", 1)
                background("dve", 4)
                background("pool", 3)
                if h == after_k:
                    background("dve", 1000)
                    background("pool", 1000)
                for stage in stages.get(h, ()):
                    stage()
                if h < len(chunks):
                    chunk(chunks[h])

            stream.low_engine = "dve"
            cmp_output(QH // 2 - 1)
            main_ring[:] = [b for b in range(8) if b != SUMS]
            preload(ACT.Sqrt)
            mixer2_done = list(act.ready)

        ffn = fixed.enter_context(ExitStack())
        act_ffn = Split(alloc(ffn, "ffn_hi", [P, DT, T], F32R), alloc(ffn, "ffn_lo", [P, DT, T], F32R), DT)
        for i in range(DT // 2):
            b = next_bank()
            t = act_free[0] = product(b, act, last=(i == DT // 2 - 1))
            s2 = slice(2 * i, 2 * i + 2)
            t = bank_readers[b] = q.tt(x_T[:, s2, :], x_T[:, s2, :], bank[b][:].rearrange("p (k t) -> p k t", k=2),
                                       ALU.add, t)
            x_ready[2 * i] = x_ready[2 * i + 1] = t
            scaled_parts(act_ffn, 2 * i, 2, cols("ffn_norm_2", 0, DT), t, mixer2_done)
            norm_begin(2 * i, 2, x_T[:, s2, :], t, pair_add="dve")
        with ExitStack() as phase:
            FT = FF2 // P
            hidden = Split(alloc(phase, "hidden2_hi", [P, FT, T], F32R), alloc(phase, "hidden2_lo", [P, FT, T], F32R), FT)
            silu = [wide[0][:, 2 * i:2 * i + 2, :] for i in range(4)]
            silu_free = [mixer2_done] * 4
            for i in range(FT // 2):
                b, b_up = next_bank(), next_bank()
                if i == 0:
                    t, t_up = act_free[0] = two_products(b, b_up, act_ffn)
                    rstd_ready = norm_end(D)
                    preload(ACT.Silu)
                    stream.ahead()
                else:
                    t = product(b, act_ffn)
                s_ = silu[i % 4]
                t = bank_readers[b] = q.tt(s_, bank[b][:].rearrange("p (k t) -> p k t", k=2), rstd_2, ALU.mult,
                                           [t, rstd_ready, silu_free[i % 4]])
                t = q.act(s_, s_, ACT.Silu, t)
                t = q.tt(s_, s_, rstd_2, ALU.mult, [t, rstd_ready], engine="pool")
                if i:
                    t_up = act_free[0] = product(b_up, act_ffn)
                t = bank_readers[b_up] = q.tt(s_, bank[b_up][:].rearrange("p (k t) -> p k t", k=2), s_, ALU.mult,
                                              [t, t_up])
                silu_free[i % 4] = split_tiles(hidden, 2 * i, 2, s_, t)
            preload(ACT.Sqrt)

            normed = wide[1]
            closed, turned = [None], {}
            OUT_BANKS = {(0, 0): 4, (1, 0): 5, (0, 1): 6, (1, 1): 7}
            main_ring[:] = [0, 1, 2]

            def closing(k, ready):
                x_tiles = x_T[:, k:k + 2, :]
                ready_sq = q.act(squares[:, k:k + 2, :], x_tiles, ACT.Square, ready)
                ready_g = [q.act(normed[:, i, :], x_T[:, i, :], ACT.Copy, [ready, cols_ready],
                                 scale=cols("final_norm", i, 1)) for i in (k, k + 1)]

                def turn_and_sum():
                    for tt_ in range(TT):
                        for i in (k, k + 1):
                            closed[0] = q.matmul(bank[SUMS][:, tt_:tt_ + 1], squares[:, i, tt_ * P:(tt_ + 1) * P],
                                                 ones[:, 0:1], i == 0 and tt_ == 0, i == DT - 1,
                                                 [ready_sq, bank_readers[SUMS] if i == 0 else None], signal=True)
                    for tt_ in range(TT):
                        b = OUT_BANKS[tt_, k // 4]
                        for i in (k, k + 1):
                            turned[b] = q.transpose(bank[b][:, i % 4 * P:(i % 4 + 1) * P],
                                                    normed[:, i, tt_ * P:(tt_ + 1) * P], ident[:],
                                                    [ready_g, bank_readers[b]], signal=True)

                pending_sums.append(turn_and_sum)

            def evacuate2(i, b, t):
                x_tiles = x_T[:, 2 * i:2 * i + 2, :]
                t = bank_readers[b] = q.tt(x_tiles, x_tiles, bank[b][:].rearrange("p (k t) -> p k t", k=2), ALU.add, t)
                closing(2 * i, t)

            accumulate_tiles(hidden, FT, evacuate2)

        flush_sums()
        rstd_out = alloc(fixed, "rstd_out", [P, TT])
        t = q.act(rstd_out[:], bank[SUMS][:, 0:TT], ACT.Sqrt, [closed[0], eps_ready], scale=1.0 / D, bias=eps[:, 0:1])
        rstd_out_ready = q.recip(rstd_out[:], rstd_out[:], t)
        out_v = wide[0][:].rearrange("p k t -> p (k t)").rearrange("p (t d) -> p t d", t=TT)
        n_stores = 0
        for (tt_, part), b in OUT_BANKS.items():
            dst = out_v[:, tt_, part * 4 * P:(part + 1) * 4 * P]
            if tt_:
                t = q.act(dst, bank[b][:], ACT.Copy, [turned[b], rstd_out_ready, silu_free],
                          scale=rstd_out[:, tt_:tt_ + 1])
            else:
                t = q.ts(dst, bank[b][:], rstd_out[:, tt_:tt_ + 1], ALU.mult, waits=[turned[b], rstd_out_ready, silu_free])
            n_stores += 1
            q.load("act" if tt_ else "sp", out[0, tt_ * P:(tt_ + 1) * P, part * 4 * P:(part + 1) * 4 * P], dst,
                   out_sem, 16 * n_stores, t)
        q.put("sp", lambda e: e.wait_ge(out_sem, 16 * n_stores), signal=False)
        assert stream.used == len(stream.plan)

        block = fixed.enter_context(nc.Block())

        @block.sync
        def _(e):
            for issue in q.items["sp"]:
                issue(e)

        @block.tensor
        def _(e):
            for issue in q.items["pe"]:
                issue(e)

        @block.scalar
        def _(e):
            for issue in q.items["act"]:
                issue(e)

        @block.vector
        def _(e):
            for issue in q.items["dve"]:
                issue(e)

        @block.gpsimd
        def _(e):
            for issue in q.items["pool"]:
                issue(e)


INPUTS = ["x", "c", "w_ada", "b_ada", "g_pre_mix", "g_post_mix", "g_pre_mlp", "g_post_mlp", "w_in", "conv_w",
          "w_proj_conv", "w_proj_attn", "w_out", "w_mlp_in", "w_mlp_out", "attn_norm_2", "w_in_2", "conv_w_2",
          "conv_b_2", "conv_ln_g_2", "conv_ln_b_2", "cmp_k_pe_2", "cmp_k_w1_2", "cmp_k_w2_2", "cmp_v_pe_2",
          "cmp_v_w1_2", "cmp_v_w2_2", "w_out_2", "ffn_norm_2", "w_gate_up_2", "w_down_2", "final_norm_2"]


def kernel(**inputs):
    import numpy as _np
    import concourse.bacc as _bacc
    from concourse import mybir as _mybir
    from concourse.bass_utils import run_bass_kernel_spmd as _run

    nc = _bacc.Bacc("TRN2", target_bir_lowering=False, num_devices=1)
    arrays, aps = {}, {}
    for name in INPUTS:
        v = _np.ascontiguousarray(inputs[name])
        arrays[f"in_{name}"] = v
        aps[name] = nc.dram_tensor(f"in_{name}", v.shape, _mybir.dt.from_np(v.dtype), kind="ExternalInput").ap()
    y = nc.dram_tensor("out_y", arrays["in_x"].shape, _mybir.dt.float32, kind="ExternalOutput").ap()
    build(nc, aps, y)
    r = _run(nc, [arrays], core_ids=[0])
    return r.results[0]["out_y"]
```
